# Optimizing a Trainium2 kernel written in Bass

```python
import jax, jax.numpy as jnp
from jax import lax
import numpy as np
import math

D_MODEL = 1024
BATCH = 1
SEQ = 256
DEPTH = 1

N_MIXERS = 3
CONF_CONV_WIDTH = 31
POOL_WINDOWS = (2, 4, 8, 16)
POOL_GROUPS = len(POOL_WINDOWS)
POOL_GROUP_DIM = D_MODEL // POOL_GROUPS
SHORT_CONV_WIDTH = 3
FFN_CONV_WIDTH = 3
D_FF = 2816
RMS_EPS = 1e-6
LN_EPS = 1e-5
N_A = (DEPTH + N_MIXERS - 1) // N_MIXERS
N_B = (DEPTH + N_MIXERS - 2) // N_MIXERS
N_C = (DEPTH + N_MIXERS - 3) // N_MIXERS


def rmsnorm(x, g):
    x32 = x.astype(jnp.float32)
    y = x32 * lax.rsqrt(jnp.mean(x32 * x32, axis=-1, keepdims=True) + RMS_EPS)
    return y.astype(x.dtype) * g

def layernorm(x, g, b):
    x32 = x.astype(jnp.float32)
    mu = jnp.mean(x32, axis=-1, keepdims=True)
    var = jnp.mean(jnp.square(x32 - mu), axis=-1, keepdims=True)
    y = (x32 - mu) * lax.rsqrt(var + LN_EPS)
    return y.astype(x.dtype) * g + b

def causal_dwconv(x, w):
    k, ch = w.shape
    return lax.conv_general_dilated(
        x, w[:, None, :].astype(x.dtype), window_strides=(1,), padding=[(k - 1, 0)],
        dimension_numbers=("NWC", "WIO", "NWC"), feature_group_count=ch)

def conformer_conv_module(h, w1, b1, dw_w, dw_b, ln_g, ln_b, w2, b2):
    u = h @ w1 + b1
    a, gt = jnp.split(u, 2, axis=-1)
    u = a * jax.nn.sigmoid(gt)
    u = causal_dwconv(u, dw_w) + dw_b
    u = jax.nn.silu(layernorm(u, ln_g, ln_b))
    return u @ w2 + b2

def pooling_mixer(h, group_w, group_b, ch_scale):
    bsz, t_len, d = h.shape
    h32 = h.astype(jnp.float32)
    cs = jnp.cumsum(h32, axis=1)
    pos = jnp.arange(1, t_len + 1, dtype=jnp.float32)[None, :, None]
    means = []
    for g, w in enumerate(POOL_WINDOWS):
        csg = cs[..., g * POOL_GROUP_DIM:(g + 1) * POOL_GROUP_DIM]
        prev = jnp.pad(csg, ((0, 0), (w, 0), (0, 0)))[:, :t_len]
        means.append((csg - prev) / jnp.minimum(pos, float(w)))
    pooled = (jnp.concatenate(means, axis=-1) - h32).astype(h.dtype)
    pooled = pooled.reshape(bsz, t_len, POOL_GROUPS, POOL_GROUP_DIM)
    mixed = jnp.einsum("btgc,gcd->btgd", pooled, group_w).reshape(bsz, t_len, d)
    return (mixed + group_b) * ch_scale

def short_conv_mixer(h, w_in, w_conv, w_out):
    bcx = h @ w_in
    gb, gc, v = jnp.split(bcx, 3, axis=-1)
    return (gb * causal_dwconv(gc * v, w_conv)) @ w_out

def conv_ffn(h, w_up, dw_w, dw_b, w_down):
    u = causal_dwconv(h @ w_up, dw_w) + dw_b
    gt, v = jnp.split(u, 2, axis=-1)
    return (jax.nn.silu(gt) * v) @ w_down

def first_inputs(seed: int = 0) -> dict:
    key = jax.random.key(seed)
    ks = iter(jax.random.split(key, 40))
    d, f = D_MODEL, D_FF

    def nrm(shape, scale):
        return scale * jax.random.normal(next(ks), shape, jnp.float32)

    def gain(shape):
        return 1.0 + nrm(shape, 0.05)

    return {
        "x": nrm((BATCH, SEQ, d), 1.0),
        "c": nrm((BATCH, d), 1.0),
        "mod_w": nrm((DEPTH, d, 6 * d), 0.5 * d ** -0.5),
        "mod_b": nrm((DEPTH, 6 * d), 0.02),
        "norm_pre_mix": gain((DEPTH, d)),
        "norm_post_mix": gain((DEPTH, d)),
        "norm_pre_ffn": gain((DEPTH, d)),
        "norm_post_ffn": gain((DEPTH, d)),
        "a_pw1_w": nrm((N_A, d, 2 * d), d ** -0.5),
        "a_pw1_b": nrm((N_A, 2 * d), 0.02),
        "a_dw_w": nrm((N_A, CONF_CONV_WIDTH, d), CONF_CONV_WIDTH ** -0.5),
        "a_dw_b": nrm((N_A, d), 0.02),
        "a_ln_g": gain((N_A, d)),
        "a_ln_b": nrm((N_A, d), 0.02),
        "a_pw2_w": nrm((N_A, d, d), d ** -0.5),
        "a_pw2_b": nrm((N_A, d), 0.02),
        "b_group_w": nrm((N_B, POOL_GROUPS, POOL_GROUP_DIM, POOL_GROUP_DIM), POOL_GROUP_DIM ** -0.5),
        "b_group_b": nrm((N_B, d), 0.02),
        "b_scale": gain((N_B, d)),
        "c_in_w": nrm((N_C, d, 3 * d), d ** -0.5),
        "c_conv_w": nrm((N_C, SHORT_CONV_WIDTH, d), SHORT_CONV_WIDTH ** -0.5),
        "c_out_w": nrm((N_C, d, d), d ** -0.5),
        "f_up_w": nrm((DEPTH, d, 2 * f), d ** -0.5),
        "f_dw_w": nrm((DEPTH, FFN_CONV_WIDTH, 2 * f), FFN_CONV_WIDTH ** -0.5),
        "f_dw_b": nrm((DEPTH, 2 * f), 0.02),
        "f_down_w": nrm((DEPTH, f, d), f ** -0.5),
    }

def first_block(x, c, mod_w, mod_b, norm_pre_mix, norm_post_mix, norm_pre_ffn, norm_post_ffn,
              a_pw1_w, a_pw1_b, a_dw_w, a_dw_b, a_ln_g, a_ln_b, a_pw2_w, a_pw2_b,
              b_group_w, b_group_b, b_scale,
              c_in_w, c_conv_w, c_out_w,
              f_up_w, f_dw_w, f_dw_b, f_down_w):
    c_act = jax.nn.silu(c)
    for i in range(DEPTH):
        mod = c_act @ mod_w[i] + mod_b[i]
        sh_m, sc_m, gt_m, sh_f, sc_f, gt_f = [m[:, None, :] for m in jnp.split(mod, 6, axis=-1)]

        h = rmsnorm(x, norm_pre_mix[i]) * (1.0 + sc_m) + sh_m
        kind, slot = i % N_MIXERS, i // N_MIXERS
        if kind == 0:
            y = conformer_conv_module(h, a_pw1_w[slot], a_pw1_b[slot], a_dw_w[slot], a_dw_b[slot],
                                      a_ln_g[slot], a_ln_b[slot], a_pw2_w[slot], a_pw2_b[slot])
        elif kind == 1:
            y = pooling_mixer(h, b_group_w[slot], b_group_b[slot], b_scale[slot])
        else:
            y = short_conv_mixer(h, c_in_w[slot], c_conv_w[slot], c_out_w[slot])
        x = x + gt_m * rmsnorm(y, norm_post_mix[i])

        h = rmsnorm(x, norm_pre_ffn[i]) * (1.0 + sc_f) + sh_f
        y = conv_ffn(h, f_up_w[i], f_dw_w[i], f_dw_b[i], f_down_w[i])
        x = x + gt_f * rmsnorm(y, norm_post_ffn[i])
    return x


DEPTH_2 = 2

CHUNK = 64
N_MEM = 256
HEAD_DIM = 64
MIX_WIDTH = (D_MODEL * 3) // 4
N_MIX_HEADS = MIX_WIDTH // HEAD_DIM
MEM_WIDTH = D_MODEL - MIX_WIDTH
N_MEM_HEADS = MEM_WIDTH // HEAD_DIM
DECAY_LORA = 64
AAA_LORA = 64
GATE_LORA = 128
Q_BLOCK = 128
N_MIXERS_2 = 2
N_RWKV = (DEPTH_2 + 1) // 2
N_SB = DEPTH_2 // 2
ALPHA = (2 * DEPTH_2) ** 0.25
BETA = (8 * DEPTH_2) ** -0.25
LNX_EPS = 64e-5
RWKV_SHIFT = 3 * MIX_WIDTH + DECAY_LORA + AAA_LORA + GATE_LORA
RWKV_IN = RWKV_SHIFT + MEM_WIDTH
SB_IN = 3 * MIX_WIDTH + MEM_WIDTH


def layer_norm(x, g, b):
    xf = x.astype(jnp.float32)
    mu = jnp.mean(xf, axis=-1, keepdims=True)
    var = jnp.mean(jnp.square(xf - mu), axis=-1, keepdims=True)
    return ((xf - mu) * lax.rsqrt(var + LN_EPS) * g + b).astype(x.dtype)

def swiglu(x, w_gate, w_up, w_down):
    return (jax.nn.silu(x @ w_gate) * (x @ w_up)) @ w_down

def split_heads(t):
    b, s, _ = t.shape
    return t.reshape(b, s, -1, HEAD_DIM).transpose(0, 2, 1, 3)

def merge_heads(t):
    b, h, s, d = t.shape
    return t.transpose(0, 2, 1, 3).reshape(b, s, h * d)

def token_shift(p, mu):
    prev = jnp.pad(p, ((0, 0), (1, 0), (0, 0)))[:, :-1]
    return p + (prev - p) * mu

def memory_attention(mq, mem_k, mem_v):
    q = split_heads(mq)
    scores = jnp.einsum('bhsd,bhmd->bhsm', q, mem_k).astype(jnp.float32) / math.sqrt(HEAD_DIM)
    p = jax.nn.softmax(scores, axis=-1).astype(mq.dtype)
    return merge_heads(jnp.einsum('bhsm,bhmd->bhsd', p, mem_v))

def rwkv7_mix(z_in, mu, w0, w_up, a0, a_up, g_up, k_k, k_a, r_k, lnx_g, lnx_b):
    bsz, seq, _ = z_in.shape
    dt = z_in.dtype
    z = token_shift(z_in, mu)
    c = MIX_WIDTH
    r = z[..., :c]
    k = z[..., c:2 * c]
    v = z[..., 2 * c:3 * c]
    o = 3 * c
    dw = z[..., o:o + DECAY_LORA]
    o += DECAY_LORA
    da = z[..., o:o + AAA_LORA]
    o += AAA_LORA
    dg = z[..., o:o + GATE_LORA]
    w = -jax.nn.softplus(-(w0 + jnp.tanh(dw) @ w_up)) - 0.5
    a = jax.nn.sigmoid(a0 + da @ a_up)
    g = jax.nn.sigmoid(dg) @ g_up

    def hs(t):
        return t.astype(jnp.float32).reshape(bsz, seq, N_MIX_HEADS, HEAD_DIM)

    kk = hs(k * k_k)
    kk = kk * lax.rsqrt(jnp.maximum(jnp.sum(kk * kk, axis=-1, keepdims=True), 1e-24))
    k = hs(k * (1.0 + (a - 1.0) * k_a))
    r, v, a = hs(r), hs(v), hs(a)
    decay = jnp.exp(-jnp.exp(hs(w)))

    n_chunks = seq // CHUNK

    def to_chunks(t):
        return t.transpose(1, 0, 2, 3).reshape(n_chunks, CHUNK, bsz, N_MIX_HEADS, HEAD_DIM)

    xs = (to_chunks(r), to_chunks(decay), to_chunks(k), to_chunks(v), to_chunks(kk), to_chunks(kk * a))

    def step(state, inp):
        r_t, w_t, k_t, v_t, kk_t, b_t = inp
        sa = jnp.einsum('bhij,bhj->bhi', state, kk_t)
        state = (state * w_t[:, :, None, :] - sa[..., :, None] * b_t[..., None, :]
                 + v_t[..., :, None] * k_t[..., None, :])
        return state, jnp.einsum('bhij,bhj->bhi', state, r_t)

    def chunk_step(state, chunk_inp):
        return lax.scan(step, state, chunk_inp)

    state0 = jnp.zeros((bsz, N_MIX_HEADS, HEAD_DIM, HEAD_DIM), jnp.float32)
    _, out = lax.scan(chunk_step, state0, xs)
    out = out.reshape(seq, bsz, N_MIX_HEADS, HEAD_DIM).transpose(1, 0, 2, 3)
    m = jnp.mean(out, axis=-1, keepdims=True)
    var = jnp.mean(jnp.square(out - m), axis=-1, keepdims=True)
    out = ((out - m) * lax.rsqrt(var + LNX_EPS)).reshape(bsz, seq, c) * lnx_g + lnx_b
    bonus = jnp.sum(r * k * r_k, axis=-1, keepdims=True) * v
    y = (out + bonus.reshape(bsz, seq, c)) * g
    return y.astype(dt)

def stick_breaking_mix(q, k, v):
    q, k, v = split_heads(q), split_heads(k), split_heads(v)
    seq = q.shape[2]
    scale = 1.0 / math.sqrt(HEAD_DIM)
    outs = []
    for blk in range(seq // Q_BLOCK):
        start = blk * Q_BLOCK
        end = start + Q_BLOCK
        kb = k[:, :, :end]
        vb = v[:, :, :end]
        z = jnp.einsum('bhtd,bhsd->bhts', q[:, :, start:end], kb).astype(jnp.float32) * scale
        t_pos = start + jnp.arange(Q_BLOCK)[:, None]
        s_pos = jnp.arange(end)[None, :]
        before = s_pos < t_pos
        log_keep = jnp.where(before, -jax.nn.softplus(z), 0.0)
        later = lax.cumsum(log_keep, axis=3, reverse=True) - log_keep
        att = jnp.where(before, jnp.exp(jax.nn.log_sigmoid(z) + later), 0.0)
        outs.append(jnp.einsum('bhts,bhsd->bhtd', att.astype(v.dtype), vb))
    return merge_heads(jnp.concatenate(outs, axis=2))

def second_inputs(seed: int = 0) -> dict:
    key = jax.random.key(seed)
    ks = jax.random.split(key, 32)
    f32 = jnp.float32
    d, f, c = D_MODEL, D_FF, MIX_WIDTH

    def nrm(k, shape, scale):
        return jax.random.normal(k, shape, f32) * scale

    return {
        "x": nrm(ks[0], (BATCH, SEQ, d), 1.0),
        "mem": nrm(ks[1], (BATCH, N_MEM, d), 1.0),
        "ffn1_w_gate": nrm(ks[2], (DEPTH_2, d, f), d ** -0.5),
        "ffn1_w_up": nrm(ks[3], (DEPTH_2, d, f), d ** -0.5),
        "ffn1_w_down": nrm(ks[4], (DEPTH_2, f, d), BETA * f ** -0.5),
        "ffn2_w_gate": nrm(ks[5], (DEPTH_2, d, f), d ** -0.5),
        "ffn2_w_up": nrm(ks[6], (DEPTH_2, d, f), d ** -0.5),
        "ffn2_w_down": nrm(ks[7], (DEPTH_2, f, d), BETA * f ** -0.5),
        "ln_g": 1.0 + nrm(ks[8], (DEPTH_2, 3, d), 0.02),
        "ln_b": nrm(ks[9], (DEPTH_2, 3, d), 0.02),
        "w_out": nrm(ks[10], (DEPTH_2, d, d), BETA * d ** -0.5),
        "w_mem_kv": nrm(ks[11], (d, 2 * MEM_WIDTH), d ** -0.5),
        "rwkv_w_in": nrm(ks[12], (N_RWKV, d, RWKV_IN), d ** -0.5),
        "rwkv_mu": jax.random.uniform(ks[13], (N_RWKV, RWKV_SHIFT), f32),
        "rwkv_w0": jax.random.uniform(ks[14], (N_RWKV, c), f32, -6.0, -1.0),
        "rwkv_w_up": nrm(ks[15], (N_RWKV, DECAY_LORA, c), 0.1 * DECAY_LORA ** -0.5),
        "rwkv_a0": nrm(ks[16], (N_RWKV, c), 0.5),
        "rwkv_a_up": nrm(ks[17], (N_RWKV, AAA_LORA, c), 0.5 * AAA_LORA ** -0.5),
        "rwkv_g_up": nrm(ks[18], (N_RWKV, GATE_LORA, c), GATE_LORA ** -0.5),
        "rwkv_k_k": 1.0 + nrm(ks[19], (N_RWKV, c), 0.1),
        "rwkv_k_a": 1.0 + nrm(ks[20], (N_RWKV, c), 0.1),
        "rwkv_r_k": nrm(ks[21], (N_RWKV, N_MIX_HEADS, HEAD_DIM), 0.1),
        "rwkv_lnx_g": 1.0 + nrm(ks[22], (N_RWKV, c), 0.02),
        "rwkv_lnx_b": nrm(ks[23], (N_RWKV, c), 0.02),
        "sb_w_in": nrm(ks[24], (N_SB, d, SB_IN), d ** -0.5),
    }

def second_block(x, mem, ffn1_w_gate, ffn1_w_up, ffn1_w_down, ffn2_w_gate, ffn2_w_up, ffn2_w_down,
              ln_g, ln_b, w_out, w_mem_kv, rwkv_w_in, rwkv_mu, rwkv_w0, rwkv_w_up, rwkv_a0,
              rwkv_a_up, rwkv_g_up, rwkv_k_k, rwkv_k_a, rwkv_r_k, rwkv_lnx_g, rwkv_lnx_b, sb_w_in):
    mem_kv = mem @ w_mem_kv
    mem_k = split_heads(mem_kv[..., :MEM_WIDTH])
    mem_v = split_heads(mem_kv[..., MEM_WIDTH:])
    c = MIX_WIDTH
    for i in range(DEPTH_2):
        x = layer_norm(ALPHA * x + 0.5 * swiglu(x, ffn1_w_gate[i], ffn1_w_up[i], ffn1_w_down[i]),
                       ln_g[i, 0], ln_b[i, 0])
        j = i // N_MIXERS_2
        if i % N_MIXERS_2 == 0:
            proj = x @ rwkv_w_in[j]
            mix = rwkv7_mix(proj[..., :RWKV_SHIFT], rwkv_mu[j], rwkv_w0[j], rwkv_w_up[j],
                            rwkv_a0[j], rwkv_a_up[j], rwkv_g_up[j], rwkv_k_k[j], rwkv_k_a[j],
                            rwkv_r_k[j], rwkv_lnx_g[j], rwkv_lnx_b[j])
            mq = proj[..., RWKV_SHIFT:]
        else:
            proj = x @ sb_w_in[j]
            mix = stick_breaking_mix(proj[..., :c], proj[..., c:2 * c], proj[..., 2 * c:3 * c])
            mq = proj[..., 3 * c:]
        heads = jnp.concatenate([mix, memory_attention(mq, mem_k, mem_v)], axis=-1)
        x = layer_norm(ALPHA * x + heads @ w_out[i], ln_g[i, 1], ln_b[i, 1])
        x = layer_norm(ALPHA * x + 0.5 * swiglu(x, ffn2_w_gate[i], ffn2_w_up[i], ffn2_w_down[i]),
                       ln_g[i, 2], ln_b[i, 2])
    return x


def setup_inputs(seed=0):
    out = dict(first_inputs(seed))
    for name, value in second_inputs(seed + 1).items():
        if name != "x":
            out[name + "_2"] = value
    return out


def reference(
    x, c, mod_w, mod_b, norm_pre_mix, norm_post_mix, norm_pre_ffn, norm_post_ffn, a_pw1_w,
    a_pw1_b, a_dw_w, a_dw_b, a_ln_g, a_ln_b, a_pw2_w, a_pw2_b, b_group_w, b_group_b, b_scale,
    c_in_w, c_conv_w, c_out_w, f_up_w, f_dw_w, f_dw_b, f_down_w, mem_2, ffn1_w_gate_2,
    ffn1_w_up_2, ffn1_w_down_2, ffn2_w_gate_2, ffn2_w_up_2, ffn2_w_down_2, ln_g_2, ln_b_2,
    w_out_2, w_mem_kv_2, rwkv_w_in_2, rwkv_mu_2, rwkv_w0_2, rwkv_w_up_2, rwkv_a0_2, rwkv_a_up_2,
    rwkv_g_up_2, rwkv_k_k_2, rwkv_k_a_2, rwkv_r_k_2, rwkv_lnx_g_2, rwkv_lnx_b_2, sb_w_in_2,
):
    x = first_block(
        x, c, mod_w, mod_b, norm_pre_mix, norm_post_mix, norm_pre_ffn, norm_post_ffn, a_pw1_w,
        a_pw1_b, a_dw_w, a_dw_b, a_ln_g, a_ln_b, a_pw2_w, a_pw2_b, b_group_w, b_group_b,
        b_scale, c_in_w, c_conv_w, c_out_w, f_up_w, f_dw_w, f_dw_b, f_down_w,
    )
    return second_block(
        x, mem_2, ffn1_w_gate_2, ffn1_w_up_2, ffn1_w_down_2, ffn2_w_gate_2, ffn2_w_up_2,
        ffn2_w_down_2, ln_g_2, ln_b_2, w_out_2, w_mem_kv_2, rwkv_w_in_2, rwkv_mu_2, rwkv_w0_2,
        rwkv_w_up_2, rwkv_a0_2, rwkv_a_up_2, rwkv_g_up_2, rwkv_k_k_2, rwkv_k_a_2, rwkv_r_k_2,
        rwkv_lnx_g_2, rwkv_lnx_b_2, sb_w_in_2,
    )


_drawn_inputs = setup_inputs


def setup_inputs(seed=0):
    import zlib

    import numpy as np

    out = dict(_drawn_inputs(seed))
    spreads = {}
    factors = {'norm_pre_mix': 3.3,
     'norm_post_mix': 3.123,
     'norm_post_ffn': 3.879,
     'a_pw1_b': 7.69,
     'a_dw_b': 4.049,
     'a_ln_g': 2.985,
     'a_ln_b': 8.0,
     'a_pw2_b': 5.195,
     'f_dw_b': 6.976,
     'rwkv_w_up_2': 8.0,
     'rwkv_k_k_2': 4.919,
     'rwkv_k_a_2': 2.982,
     'rwkv_lnx_g_2': 8.0,
     'rwkv_lnx_b_2': 8.0}
    for name, (base, spread) in spreads.items():
        noise = np.random.default_rng([zlib.crc32(name.encode()), seed]).standard_normal(out[name].shape)
        drawn = base * np.exp(spread * noise) if base else spread * noise
        out[name] = __import__('jax').numpy.asarray(drawn.astype(out[name].dtype))
    for name, factor in factors.items():
        out[name] = (out[name] * factor).astype(out[name].dtype)
    return out
```

```python
import math
from contextlib import ExitStack

import concourse.bass as bass
from concourse import mybir

F32 = mybir.dt.float32
F32R = mybir.dt.float32r
ALU = mybir.AluOpType
ACT = mybir.ActivationFunctionType
AX_X = mybir.AxisListType.X

P = 128
SEQ, D, DFF = 256, 1024, 2816
NT = SEQ // P
KD = D // P
NF = DFF // P
CONVW, FCONVW = 31, 3
PAD = CONVW - 1
C = 768
MT6 = C // P
HD = 64
NH, NMH = C // HD, 4
NMEM = 256
CHUNK = 64
ALPHA = 4.0 ** 0.25
DECAY = math.exp(-0.5)
RMS_EPS, LN_EPS, LNX_EPS = 1e-6, 1e-5, 64e-5
MOD_EARLY = 6
ACH, BCH = 2048, 1024


class Signal:

    def __init__(self, sem):
        self.sem, self.total, self.count, self.todo = sem, 0, {}, []

    def events(self, names):
        assert not self.todo, self.todo
        self.todo = list(names)
        self.count = {n: self.total + i + 1 for i, n in enumerate(self.todo)}
        self.total += len(self.todo)
        assert len(self.count) == len(self.todo)

    def raised(self, ins, name):
        assert self.todo and self.todo[0] == name, (self.todo[:1], name)
        self.todo.pop(0)
        ins.then_inc(self.sem, 1)

    def wait(self, eng, name):
        eng.wait_ge(self.sem, self.count[name])


class Steps:

    def __init__(self, sem):
        self.sem, self.n = sem, 0

    def mark(self, ins):
        self.n += 1
        ins.then_inc(self.sem, 1)
        return self.n

    def step(self, eng, ins):
        self.mark(ins)
        eng.wait_ge(self.sem, self.n)

    def upto(self, eng, n):
        eng.wait_ge(self.sem, n)


class Ring:

    def __init__(self, raw, parts, sems, chunks):
        self.raw, self.parts, self.chunks = raw, parts, chunks
        self.loaded, self.hi_done, self.lo_done, self.used, self.raw_used = sems
        self.split_no, self.raw_no, self.load_no = [], [], []
        split = direct = 0
        loads = [0, 0]
        for g, (dmas, is_split) in enumerate(chunks):
            loads[g % 2] += 16 * len(dmas)
            self.load_no.append(loads[g % 2])
            self.split_no.append(split)
            self.raw_no.append(direct)
            split, direct = split + is_split, direct + (not is_split)

    def wait_raw_free(self, sp, g):
        if g >= 2:
            if self.chunks[g - 2][1]:
                sp.wait_ge(self.lo_done, self.split_no[g - 2] + 1)
            else:
                sp.wait_ge(self.raw_used, self.raw_no[g - 2] + 1)

    def load(self, sp, g):
        if g >= len(self.chunks):
            return
        self.wait_raw_free(sp, g)
        for cols, view, src in self.chunks[g][0]:
            dst = self.raw[:, g % 2, cols[0]:cols[1]]
            sp.dma_start(dst.rearrange(view[0], **view[1]) if view else dst, src).then_inc(self.loaded[g % 2], 16)

    def split_hi(self, act, g):
        s = self.split_no[g]
        act.wait_ge(self.loaded[g % 2], self.load_no[g])
        if s >= 2:
            act.wait_ge(self.used, s - 1)
        act.activation(self.parts[:, s % 2, 0], self.raw[:, g % 2], ACT.Copy).then_inc(self.hi_done, 1)

    def split_lo(self, dve, g):
        s = self.split_no[g]
        dve.wait_ge(self.hi_done, s + 1)
        dve.tensor_tensor(self.parts[:, s % 2, 1], self.raw[:, g % 2], self.parts[:, s % 2, 0].bitcast(F32),
                          ALU.subtract).then_inc(self.lo_done, 1)

    def wait_split(self, pe, g):
        pe.wait_ge(self.lo_done, self.split_no[g] + 1)

    def wait_raw(self, pe, g):
        pe.wait_ge(self.loaded[g % 2], self.load_no[g])

    def wait_used(self, eng, g):
        eng.wait_ge(self.used, self.split_no[g] + 1)

    def part(self, g, which, lo, hi):
        return self.parts[:, self.split_no[g] % 2, which, lo:hi]


def mm3(pe, out, lhs, rhs, start, stop):
    pe.matmul(out, lhs[0], rhs[0], start=start, stop=False)
    pe.matmul(out, lhs[0], rhs[1], start=False, stop=False)
    return pe.matmul(out, lhs[1], rhs[0], start=False, stop=stop)


def param_columns(A):
    def rows(ap):
        return ap.rearrange("(r p) -> r p", p=P)

    parts = [("c", rows(A["c"][0])), ("norm_pre_mix", rows(A["norm_pre_mix"][0])),
             ("norm_pre_ffn", rows(A["norm_pre_ffn"][0])), ("a_pw1_b", rows(A["a_pw1_b"][0])),
             ("a_dw_b", rows(A["a_dw_b"][0])), ("a_ln_g", rows(A["a_ln_g"][0])), ("a_ln_b", rows(A["a_ln_b"][0])),
             ("mod_sh_m", rows(A["mod_b"][0, 0:D])), ("mod_sc_m", rows(A["mod_b"][0, D:2 * D])),
             ("mod_sh_f", rows(A["mod_b"][0, 3 * D:4 * D])), ("mod_sc_f", rows(A["mod_b"][0, 4 * D:5 * D]))]
    parts += [("a_dw_w", A["a_dw_w"][0].rearrange("k (r p) -> (k r) p", p=P))]
    parts += [("f_dw_w", A["f_dw_w"][0].rearrange("k (r p) -> (k r) p", p=P)), ("f_dw_b", rows(A["f_dw_b"][0])),
              ("mu", rows(A["rwkv_mu_2"][0]))]
    for n in ("w0", "a0", "k_k", "k_a"):
        parts.append((n, rows(A[f"rwkv_{n}_2"][0])))
    parts.append(("r_k", A["rwkv_r_k_2"][0].rearrange("(a b) d -> a (b d)", b=2)))
    parts += [("lnx_g", rows(A["rwkv_lnx_g_2"][0])), ("lnx_b", rows(A["rwkv_lnx_b_2"][0]))]
    at, first, loads = 0, {}, []
    for name, view in parts:
        first[name] = at
        n, done = view.shape[0], 0
        while done < n:
            m = min(n - done, P - at % P)
            loads.append((at // P, at % P, m, view[done:done + m, :]))
            done, at = done + m, at + m
    return first, loads, at


def weight_chunks(A):
    ring_a, ring_b, first = [], [], {}

    def up(name, w, cols):
        first[name] = len(ring_a)
        v = w.rearrange("(k p) n -> p k n", p=P)
        for ranges in cols:
            at, dmas = 0, []
            for a, b in ranges:
                dmas.append(((at, at + KD * (b - a)), ("p (k n) -> p k n", {"k": KD}), v[:, :, a:b]))
                at += KD * (b - a)
            ring_a.append((dmas, True))

    def raw_up(name, w, start, n):
        first[name] = len(ring_a)
        v = w.rearrange("(k p) n -> p k n", p=P)
        for a in range(start, start + n, 256):
            ring_a.append(([((0, ACH), ("p (k n) -> p k n", {"k": KD}), v[:, :, a:a + 256])], False))

    def rows2(name, w):
        first[name] = len(ring_a)
        for c in range(KD // 2):
            src = w[2 * c * P:(2 * c + 2) * P, :].rearrange("(k p) n -> p k n", p=P)
            ring_a.append(([((0, ACH), ("p (k n) -> p k n", {"k": 2}), src)], True))

    def ffn(name, gate, up_w, down):
        first[name] = len(ring_a)
        first[name, "B"] = len(ring_b)
        g, u = (w.rearrange("(k p) n -> p k n", p=P) for w in (gate, up_w))
        for i in range(NF):
            ring_a.append(([((0, BCH), ("p (k n) -> p k n", {"k": KD}), g[:, :, i * P:(i + 1) * P]),
                            ((BCH, ACH), ("p (k n) -> p k n", {"k": KD}), u[:, :, i * P:(i + 1) * P])], True))
            ring_b.append(([((0, BCH), None, down[i * P:(i + 1) * P, :])], True))

    wide = lambda n: [[(256 * c, 256 * c + 256)] for c in range(n)]
    up("mem_kv", A["w_mem_kv_2"], wide(2))
    raw_up("mod_mix", A["mod_w"][0], MOD_EARLY * 256, 2 * D - MOD_EARLY * 256)
    up("pw1", A["a_pw1_w"][0], [[(j * P, j * P + P), (D + j * P, D + j * P + P)] for j in range(KD)])
    raw_up("mod_gate_m", A["mod_w"][0], 2 * D, D)
    raw_up("mod_ffn", A["mod_w"][0], 3 * D, 2 * D)
    raw_up("mod_gate_f", A["mod_w"][0], 5 * D, D)
    rows2("pw2", A["a_pw2_w"][0])
    ffn("ffn", A["f_up_w"][0][:, 0:DFF], A["f_up_w"][0][:, DFF:2 * DFF], A["f_down_w"][0])
    for i in range(2):
        ffn(("ffn1", i), A["ffn1_w_gate_2"][i], A["ffn1_w_up_2"][i], A["ffn1_w_down_2"][i])
        if i == 0:
            w = A["rwkv_w_in_2"][0]
            up("rwkv_in", w, wide(10) + [[(2560, 2688)], [(2688, 2816)]])
        else:
            up("sb_in", A["sb_w_in_2"][0], wide(10))
        rows2(("w_out", i), A["w_out_2"][i])
        ffn(("ffn2", i), A["ffn2_w_gate_2"][i], A["ffn2_w_up_2"][i], A["ffn2_w_down_2"][i])
    return ring_a, ring_b, first


def build_program(nc, A, out):
    with ExitStack() as ctx:
        def sb(name, shape, dt=F32):
            return ctx.enter_context(nc.sbuf_tensor(name, shape, dt))

        def sem(name):
            return ctx.enter_context(nc.semaphore(name))

        def signal(name):
            return Signal(sem(name))

        a_raw, a_parts = sb("a_raw", [P, 2, ACH]), sb("a_parts", [P, 2, 2, ACH], F32R)
        b_raw, b_parts = sb("b_raw", [P, 2, BCH]), sb("b_parts", [P, 2, 2, BCH], F32R)
        x_tok = sb("x_tok", [P, NT, D])
        actT = sb("actT", [P, 2, KD, SEQ], F32R)
        hid = sb("hid", [P, 2, 2, SEQ], F32R)
        gate_m, gate_f = sb("gate_m", [P, D]), sb("gate_f", [P, D])
        rows = sb("rows", [P, 2, D])
        memkT = sb("memkT", [P, 2, NMEM])
        memv = sb("memv", [P, 2, 256])
        ident = sb("ident", [P, P])
        ones_mean = sb("ones_mean", [P, P])
        head_ones = sb("head_ones", [P, P])
        mod_cols = sb("mod_cols", [P, 4, KD])
        eps = sb("eps", [P, 3])
        stats = sb("stats", [P, NT, 16])
        small = sb("small", [P, 112])
        first_col, param_loads, n_params = param_columns(A)
        par = sb("par", [P, n_params])
        arena_words = nc.sbuf_bytes_remaining // 4 - 16
        arena = sb("arena", [P, arena_words])
        ps = ctx.enter_context(nc.psum_tensor("ps", [P, 8, 512], F32))

        def carve(*shapes):
            at, got = 0, []
            for shape in shapes:
                n = math.prod(shape)
                ap = arena[:, at:at + n]
                if len(shape) == 2:
                    ap = ap.rearrange("p (a b) -> p a b", a=shape[0])
                elif len(shape) == 3:
                    ap = ap.rearrange("p (a b c) -> p a b c", a=shape[0], b=shape[1])
                got.append(ap)
                at += n
            assert at <= arena_words, (at, arena_words)
            return got

        def col(name, i=0):
            return par[:, first_col[name] + i:first_col[name] + i + 1]

        def cols(name, n):
            return par[:, first_col[name]:first_col[name] + n]

        turned = ps[:, 4:8, :].rearrange("p b (k t) -> p (b k) t", k=2)
        acc = [ps[:, 2 * t:2 * t + 2, :].rearrange("p b n -> p (b n)") for t in range(NT)]

        chunks_a, chunks_b, sec = weight_chunks(A)
        ring_a = Ring(a_raw, a_parts, ([sem("a_loaded0"), sem("a_loaded1")], sem("a_hi_done"), sem("a_lo_done"),
                                       sem("a_used"), sem("a_raw_used")), chunks_a)
        ring_b = Ring(b_raw, b_parts, ([sem("b_loaded0"), sem("b_loaded1")], sem("b_hi_done"), sem("b_lo_done"),
                                       sem("b_used"), sem("b_raw_used")), chunks_b)
        dve_steps, act_steps, pool_steps = Steps(sem("dve_steps")), Steps(sem("act_steps")), Steps(sem("pool_steps"))
        params_loaded = sem("params_loaded")
        rows_loaded = sem("rows_loaded")
        rows_count = [0]
        turned_done = signal("turned_done")
        turned_read = signal("turned_read")
        stat_ready, stat_root = signal("stat_ready"), signal("stat_root")
        pe_out, pe_in = signal("pe_out"), signal("pe_in")
        act_out, dve_out = signal("act_out"), signal("dve_out")
        pool_out = signal("pool_out")

        def load_row(eng, slot, vec):
            eng.dma_start(rows[:, slot], vec.partition_broadcast(P)).then_inc(rows_loaded, 16)


        def loads(sp, name, n_a, n_b=0):
            for g in range(sec[name] + 2, sec[name] + 2 + n_a):
                ring_a.load(sp, g)

        def rms_scale(act, dve, t, scratch):
            if act is not None:
                act_steps.step(act, act.activation(scratch[:, t], x_tok[:, t], ACT.Square,
                                                   accum_out=stats[:, t, 0:1]))
                act_out.raised(act.activation(stats[:, t, 1:2], stats[:, t, 0:1], ACT.Sqrt, bias=eps[:, 0:1],
                                              scale=1.0 / D), ("root", t))
            if dve is not None:
                act_out.wait(dve, ("root", t))
                dve_steps.step(dve, dve.reciprocal(stats[:, t, 2:3], stats[:, t, 1:2]))
                dve_out.raised(dve.tensor_scalar(scratch[:, t], x_tok[:, t], stats[:, t, 2:3], None, ALU.mult),
                               ("xn", t))

        def turn(pe, src, t, k0=0, k1=KD):
            for k in range(k0, k1):
                ins = pe.transpose(turned[:, k, t * P:(t + 1) * P], src[:, t, k * P:(k + 1) * P], ident[:])
            turned_done.raised(ins, t)

        def affine(act, hT, shift):
            for h in range(2):
                for k in range(4 * h, 4 * h + 4):
                    ins = act.activation(hT[:, k], turned[:, k], ACT.Identity, bias=mod_cols[:, shift, k:k + 1],
                                         scale=mod_cols[:, shift + 1, k:k + 1])
                act_out.raised(ins, ("affine", h))

        def split_affine(dve, hT):
            for h in range(2):
                act_out.wait(dve, ("affine", h))
                half = slice(4 * h, 4 * h + 4)
                dve_steps.step(dve, dve.tensor_copy(actT[:, 0, half], hT[:, half]))
                dve_steps.step(dve, dve.tensor_tensor(actT[:, 1, half], hT[:, half], actT[:, 0, half].bitcast(F32),
                                                      ALU.subtract))

        def split_turned_act(act):
            for h in range(2):
                act_out.raised(act.activation(actT[:, 0, 4 * h:4 * h + 4], turned[:, 4 * h:4 * h + 4], ACT.Copy),
                               ("hi", h))

        def split_turned_dve(dve):
            for h in range(2):
                half = slice(4 * h, 4 * h + 4)
                act_out.wait(dve, ("hi", h))
                dve_steps.step(dve, dve.tensor_tensor(actT[:, 1, half], turned[:, half],
                                                      actT[:, 0, half].bitcast(F32), ALU.subtract))

        def mod_chunk(pe, weights, lhs, out_):
            for k in range(KD):
                ins = pe.matmul(out_, lhs(k), weights[:, k * 256:(k + 1) * 256], start=k == 0, stop=k == KD - 1)
            return ins

        def one_row(k):
            return csilu[:, k:k + 1]

        def to_columns(pe, mod_row):
            for j in range(2 * KD):
                ins = pe.matmul(ps[:, 0, j:j + 1], mod_row[0:1, j * P:(j + 1) * P], ones_row[0:1, 0:1],
                                start=True, stop=True)
            return ins

        def mod_finish(dve, shift, names, norm):
            sh, scl = names
            dve_steps.mark(dve.tensor_tensor(mod_cols[:, shift], ps[:, 0, 0:KD], cols(sh, KD), ALU.add))
            dve_steps.step(dve, dve.tensor_tensor(mod_cols[:, shift + 1], ps[:, 0, KD:2 * KD], cols(scl, KD),
                                                  ALU.add))
            dve_out.raised(dve.scalar_tensor_tensor(mod_cols[:, shift + 1], mod_cols[:, shift + 1], 1.0,
                                                    cols(norm, KD), ALU.add, ALU.mult), "mod")

        cb, prow, tokmem, scratch, early = carve((KD, P), (5, P), (NT, D), (NT, D), (MOD_EARLY, ACH))
        hT = tokmem.rearrange("p t d -> p (t d)").rearrange("p (k t) -> p k t", k=KD)
        csilu, csig = small[:, 0:KD], small[:, KD:2 * KD]
        ones_row = small[:, 50:51]
        mod_row = scratch.rearrange("p t d -> p (t d)")
        n_rows = (n_params + P - 1) // P
        g0, gmod = sec["mem_kv"], sec["mod_mix"]
        early_loaded = [sem(f"early_loaded{i}") for i in range(MOD_EARLY)]
        x_loaded, mem_loaded = sem("x_loaded"), sem("mem_loaded")
        turned_done.events(["mem", 0, 1])
        pe_out.events(["params", "row0", "columns"])
        act_out.events([("root", 0), ("root", 1), "memT0", "memT1", "csig", "memkT", "memv", "row0", "row1",
                        ("affine", 0), ("affine", 1)])
        dve_out.events([("xn", 0), ("xn", 1), "memT", "params", "csilu", "mod"])
        mod_v = A["mod_w"][0].rearrange("(k p) n -> p k n", p=P)

        with nc.Block() as block:
            @block.sync
            def _(sp):
                sp.dma_start(x_tok[:], A["x"][0].rearrange("(t p) d -> p t d", p=P)).then_inc(x_loaded, 16)
                sp.dma_start(tokmem, A["mem_2"][0].rearrange("(t p) d -> p t d", p=P)).then_inc(mem_loaded, 16)
                ring_a.load(sp, g0)
                ring_a.load(sp, g0 + 1)
                for c in range(MOD_EARLY):
                    sp.dma_start(early[:, c].rearrange("p (k n) -> p k n", k=KD),
                                 mod_v[:, :, c * 256:(c + 1) * 256]).then_inc(early_loaded[c], 16)
                for g in range(gmod, gmod + 8 - MOD_EARLY + 2):
                    ring_a.load(sp, g)

            @block.gpsimd
            def _(pool):
                pool_steps.step(pool, pool.memset(ident[:], 0.0))
                pool_steps.step(pool, pool.affine_select(out=ident[:], in_=ident[:], compare_op=ALU.not_equal, fill=1.0,
                                                         base=0, pattern=[[-1, P]], channel_multiplier=1))
                for i, v in enumerate((RMS_EPS, LN_EPS, LNX_EPS)):
                    pool_steps.step(pool, pool.memset(eps[:, i:i + 1], v))
                pool_steps.step(pool, pool.memset(ones_mean[:], 1.0 / D))
                pool_steps.step(pool, pool.memset(ones_row, 1.0))
                pool_steps.step(pool, pool.memset(head_ones[:], 0.0))
                for h in range(2):
                    pool_steps.step(pool, pool.memset(head_ones[h * HD:(h + 1) * HD, h * HD:(h + 1) * HD], 1.0))
            constants = pool_steps.n

            @block.scalar
            def _(act):
                for t, r, m, view in param_loads:
                    act.dma_start(prow[r:r + m, t, :], view).then_inc(params_loaded, 16)
                pool_steps.upto(act, constants)
                act.wait_ge(x_loaded, 16)
                rms_scale(act, None, 0, scratch)
                rms_scale(act, None, 1, scratch)
                turned_done.wait(act, "mem")
                for h in range(2):
                    act_out.raised(act.activation(actT[:, 0, 4 * h:4 * h + 4, :], turned[:, 4 * h:4 * h + 4, :],
                                                  ACT.Copy), f"memT{h}")
                for g in range(g0, g0 + 2):
                    ring_a.split_hi(act, g)
                dve_out.wait(act, "params")
                act_out.raised(act.activation(csig, cols("c", KD), ACT.Sigmoid), "csig")
                ring_a.wait_used(act, g0)
                act_out.raised(act.activation(memkT[:], ps[:, 1, :].rearrange("p (n m) -> p n m", n=2), ACT.Copy),
                               "memkT")
                ring_a.wait_used(act, g0 + 1)
                act_out.raised(act.activation(memv[:], ps[:, 2, :].rearrange("p (n m) -> p n m", n=2), ACT.Copy),
                               "memv")
                pe_out.wait(act, "row0")
                act_out.raised(act.activation(mod_row[0:1, 0:D], acc[0][0:1, :], ACT.Copy), "row0")
                act.wait_ge(ring_a.raw_used, ring_a.raw_no[gmod + 7 - MOD_EARLY] + 1)
                act_out.raised(act.activation(mod_row[0:1, D:2 * D], acc[1][0:1, :], ACT.Copy), "row1")
                dve_out.wait(act, "mod")
                affine(act, hT, 0)
                ring_a.split_hi(act, sec["pw1"])

            @block.tensor
            def _(pe):
                pool_steps.upto(pe, constants)
                pe.wait_ge(mem_loaded, 16)
                for t in range(NT):
                    for k in range(KD):
                        ins = pe.transpose(turned[:, k, t * P:(t + 1) * P], tokmem[:, t, k * P:(k + 1) * P], ident[:])
                turned_done.raised(ins, "mem")
                pe.wait_ge(params_loaded, 16 * len(param_loads))
                for i in range(n_rows):
                    n = min(P, n_params - i * P)
                    ins = pe.transpose(ps[:, i // 4, (i % 4) * P:(i % 4) * P + n], prow[0:n, i, :], ident[0:n, 0:n])
                pe_out.raised(ins, "params")
                dve_out.wait(pe, "params")
                dve_out.wait(pe, "memT")
                ring_a.wait_split(pe, g0)
                for n in range(2):
                    for k in range(KD):
                        w = [ring_a.part(g0, s, k * 256 + n * P, k * 256 + n * P + P) for s in range(2)]
                        ins = mm3(pe, ps[:, 1, n * NMEM:(n + 1) * NMEM], w, [actT[:, s, k, :] for s in range(2)],
                                  k == 0, k == KD - 1)
                ins.then_inc(ring_a.used, 1)
                ring_a.wait_split(pe, g0 + 1)
                for t in range(2):
                    for k in range(KD):
                        w = [ring_a.part(g0 + 1, s, k * 256, k * 256 + 256) for s in range(2)]
                        ins = mm3(pe, ps[:, 2, t * 256:(t + 1) * 256],
                                  [actT[:, s, k, t * P:(t + 1) * P] for s in range(2)], w, k == 0, k == KD - 1)
                ins.then_inc(ring_a.used, 1)
                for t in range(NT):
                    dve_out.wait(pe, ("xn", t))
                    turn(pe, scratch, t)
                dve_out.wait(pe, "csilu")
                act_out.wait(pe, "memv")
                for c in range(8):
                    if c < MOD_EARLY:
                        pe.wait_ge(early_loaded[c], 16)
                        w = early[:, c]
                    else:
                        ring_a.wait_raw(pe, gmod + c - MOD_EARLY)
                        w = a_raw[:, (gmod + c - MOD_EARLY) % 2]
                    ins = mod_chunk(pe, w, one_row, acc[c // 4][0:1, (c % 4) * 256:(c % 4) * 256 + 256])
                    if c >= MOD_EARLY:
                        ins.then_inc(ring_a.raw_used, 1)
                    elif c == 3:
                        pe_out.raised(ins, "row0")
                act_out.wait(pe, "row1")
                pe_out.raised(to_columns(pe, mod_row), "columns")

            @block.vector
            def _(dve):
                rms_scale(None, dve, 0, scratch)
                rms_scale(None, dve, 1, scratch)
                act_out.wait(dve, "memT1")
                dve_out.raised(dve.tensor_tensor(actT[:, 1], turned, actT[:, 0].bitcast(F32), ALU.subtract), "memT")
                pe_out.wait(dve, "params")
                n4 = min(n_params, 4 * P)
                dve.tensor_copy(par[:, 0:n4], ps[:, 0, 0:n4])
                dve_out.raised(dve.tensor_copy(par[:, n4:n_params], ps[:, 1, 0:n_params - n4]), "params")
                for g in range(g0, g0 + 2):
                    ring_a.split_lo(dve, g)
                act_out.wait(dve, "csig")
                dve_out.raised(dve.tensor_tensor(csilu, cols("c", KD), csig, ALU.mult), "csilu")
                dve_out.wait(dve, "csilu")
                for k in range(KD):
                    dve_steps.step(dve, dve.tensor_copy(cb[:, k, :], csilu[:, k:k + 1].to_broadcast([P, P])))
                pe_out.wait(dve, "columns")
                mod_finish(dve, 0, ("mod_sh_m", "mod_sc_m"), "norm_pre_mix")
                split_affine(dve, hT)
                ring_a.split_lo(dve, sec["pw1"])

        _, u_pad, conv, sig, prod, csum, mod_row = carve((KD, P), (KD, PAD + SEQ), (KD, SEQ), (2, SEQ), (4, SEQ),
                                                         (2, SEQ), (2 * D,))
        g0, gm, gf, gg = sec["pw1"], sec["mod_gate_m"], sec["mod_ffn"], sec["mod_gate_f"]
        AHEAD = 10
        BY_POOL = [0, 2, 4]
        BY_VECTOR = [j for j in range(KD) if j not in BY_POOL]
        pool_taps = [(j, k) for j in BY_POOL for k in range(CONVW)]
        SHARE = 8
        act_plan = []
        for j in range(KD):
            act_plan.append(("sig", j))
            if j > 0:
                n = len(pool_taps) if j == KD - 1 else j * SHARE
                act_plan += [("tap", i) for i in range((j - 1) * SHARE, n)]
        act_out.events(act_plan + ["row0", "row1"])
        pool_out.events([("tap", i) for i in range(len(pool_taps))])
        pe_out.events(["columns"])
        dve_out.events(["zero"] + [("u", j) for j in range(KD)] + ["gate_m", "mod", "gate_f"])
        rows_count[0] += 64
        gates_row = rows_count[0]
        with nc.Block() as block:
            @block.sync
            def _(sp):
                load_row(sp, 0, A["norm_post_mix"][0])
                load_row(sp, 1, A["norm_post_ffn"][0])
                sp.dma_start(gate_m[:], A["mod_b"][0, 2 * D:3 * D].partition_broadcast(P)).then_inc(rows_loaded, 16)
                sp.dma_start(gate_f[:], A["mod_b"][0, 5 * D:6 * D].partition_broadcast(P)).then_inc(rows_loaded, 16)
                for g in range(g0 + 2, gg + 4 + 2):
                    ring_a.load(sp, g)

            @block.scalar
            def _(act):
                for what, i in act_plan:
                    if what == "sig":
                        if i + 1 < KD:
                            ring_a.split_hi(act, g0 + i + 1)
                        ring_a.wait_used(act, g0 + i)
                        if i >= 2:
                            dve_out.wait(act, ("u", i - 2))
                        act_out.raised(act.activation(sig[:, i % 2], ps[:, 4 + i % 4, SEQ:2 * SEQ], ACT.Sigmoid,
                                                      bias=col("a_pw1_b", KD + i)), ("sig", i))
                    else:
                        j, k = pool_taps[i]
                        if k == 0:
                            dve_out.wait(act, ("u", j))
                        if i >= 4:
                            pool_out.wait(act, ("tap", i - 4))
                        src, w = u_pad[:, j, k:k + SEQ], col("a_dw_w", k * KD + j)
                        if k == 0:
                            ins = act.activation(prod[:, i % 4], src, ACT.Identity, bias=col("a_dw_b", j), scale=w)
                        else:
                            ins = act.activation(prod[:, i % 4], src, ACT.Copy, scale=w)
                        act_out.raised(ins, ("tap", i))
                for h in range(2):
                    act.wait_ge(ring_a.raw_used, ring_a.raw_no[gf + 4 * h + 3] + 1)
                    act_out.raised(act.activation(mod_row[0:1, h * D:(h + 1) * D], acc[h][0:1, :], ACT.Copy),
                                   f"row{h}")

            @block.gpsimd
            def _(pool):
                for i, (j, k) in enumerate(pool_taps):
                    act_out.wait(pool, ("tap", i))
                    if k == 0:
                        ins = pool.tensor_copy(csum[:, 1], prod[:, i % 4])
                    else:
                        pool_out.wait(pool, ("tap", i - 1))
                        dst = conv[:, j] if k == CONVW - 1 else csum[:, (k + 1) % 2]
                        ins = pool.tensor_tensor(dst, csum[:, k % 2], prod[:, i % 4], ALU.add)
                    pool_out.raised(ins, ("tap", i))

            @block.tensor
            def _(pe):
                for j in range(KD):
                    ring_a.wait_split(pe, g0 + j)
                    if j >= 4:
                        dve_out.wait(pe, ("u", j - 4))
                    for n in range(2):
                        for k in range(KD):
                            w = [ring_a.part(g0 + j, s, n * BCH + k * P, n * BCH + k * P + P) for s in range(2)]
                            ins = mm3(pe, ps[:, 4 + j % 4, n * SEQ:(n + 1) * SEQ], w,
                                      [actT[:, s, k] for s in range(2)], k == 0, k == KD - 1)
                    ins.then_inc(ring_a.used, 1)

                def gate(first):
                    for c in range(4):
                        ring_a.wait_raw(pe, first + c)
                        mod_chunk(pe, a_raw[:, (first + c) % 2], lambda k: cb[:, k],
                                  ps[:, 4 + c // 2, (c % 2) * 256:(c % 2) * 256 + 256])\
                            .then_inc(ring_a.raw_used, 1)

                dve_out.wait(pe, ("u", KD - 1))
                gate(gm)
                for c in range(8):
                    ring_a.wait_raw(pe, gf + c)
                    mod_chunk(pe, a_raw[:, (gf + c) % 2], one_row,
                              acc[c // 4][0:1, (c % 4) * 256:(c % 4) * 256 + 256]).then_inc(ring_a.raw_used, 1)
                dve_out.wait(pe, "gate_m")
                gate(gg)
                act_out.wait(pe, "row1")
                pe_out.raised(to_columns(pe, mod_row), "columns")

            @block.vector
            def _(dve):
                dve_out.raised(dve.memset(u_pad[:, :, 0:PAD], 0.0), "zero")
                dve_out.wait(dve, "zero")
                taps = [(j, k) for j in BY_VECTOR for k in range(CONVW)]

                def tap(made):
                    if taps[0][0] >= made:
                        return
                    j, k = taps.pop(0)
                    src, w = u_pad[:, j, k:k + SEQ], col("a_dw_w", k * KD + j)
                    if k == 0:
                        dve_out.wait(dve, ("u", j))
                        ins = dve.tensor_scalar(conv[:, j], src, w, col("a_dw_b", j), ALU.mult, ALU.add)
                    else:
                        ins = dve.scalar_tensor_tensor(conv[:, j], src, w, conv[:, j], ALU.mult, ALU.add)
                    dve_steps.step(dve, ins)

                for i in range(KD):
                    if i + 1 < KD:
                        ring_a.split_lo(dve, g0 + i + 1)
                    act_out.wait(dve, ("sig", i))
                    dve_out.raised(dve.scalar_tensor_tensor(u_pad[:, i, PAD:PAD + SEQ], ps[:, 4 + i % 4, 0:SEQ],
                                                            col("a_pw1_b", i), sig[:, i % 2], ALU.add, ALU.mult),
                                   ("u", i))
                    if i + 1 < KD:
                        for _ in range(AHEAD):
                            tap(i + 1)
                while len(taps) > CONVW:
                    tap(KD)
                dve.wait_ge(ring_a.raw_used, ring_a.raw_no[gm + 3] + 1)
                two = ps[:, 4:6, :].rearrange("p b n -> p (b n)")
                dve.wait_ge(rows_loaded, gates_row)
                dve_steps.step(dve, dve.tensor_tensor(gate_m[:], two, gate_m[:], ALU.add))
                dve_out.raised(dve.tensor_tensor(gate_m[:], gate_m[:], rows[:, 0], ALU.mult), "gate_m")
                while taps:
                    tap(KD)
                dve.wait_ge(ring_a.raw_used, ring_a.raw_no[gg + 3] + 1)
                dve_steps.step(dve, dve.tensor_tensor(gate_f[:], two, gate_f[:], ALU.add))
                pe_out.wait(dve, "columns")
                mod_finish(dve, 2, ("mod_sh_f", "mod_sc_f"), "norm_pre_ffn")
                dve_out.raised(dve.tensor_tensor(gate_f[:], gate_f[:], rows[:, 1], ALU.mult), "gate_f")

        _, _, conv, sq, rstd, yb = carve((KD, P), (KD, PAD + SEQ), (KD, SEQ), (KD, SEQ), (SEQ,), (NT, D))
        scratch = sq.rearrange("p k t -> p (k t)").rearrange("p (t d) -> p t d", t=NT)
        hT = conv
        g0 = sec["pw2"]
        pe_out.events(["mean", "var"])
        dve_out.events(["centred", "normal", ("y", 0), ("y", 1), ("x", 0), ("x", 1), ("xn", 0), ("xn", 1)])
        act_out.events(["square", "std"] + [("silu", h) for h in range(2)] + [("yroot", 0), ("yroot", 1)]
                       + [("root", 0), ("root", 1), ("affine", 0), ("affine", 1)])
        turned_done.events([0, 1])
        rows_count[0] += 16
        b2_row = rows_count[0]
        with nc.Block() as block:
            @block.sync
            def _(sp):
                load_row(sp, 0, A["a_pw2_b"][0])
                for g in range(g0 + 2, g0 + 4 + 2):
                    ring_a.load(sp, g)
                for g in range(2):
                    ring_b.load(sp, g)

            @block.scalar
            def _(act):
                dve_out.wait(act, "centred")
                act_out.raised(act.activation(sq, conv, ACT.Square), "square")
                ring_a.split_hi(act, g0)
                pe_out.wait(act, "var")
                act_out.raised(act.activation(rstd, ps[:, 1, 0:SEQ], ACT.Sqrt, bias=eps[:, 1:2]), "std")
                ring_a.split_hi(act, g0 + 1)
                dve_out.wait(act, "normal")
                for h in range(2):
                    for k in range(4 * h, 4 * h + 4):
                        ins = act.activation(conv[:, k], conv[:, k], ACT.Silu, bias=col("a_ln_b", k),
                                             scale=col("a_ln_g", k))
                    act_out.raised(ins, ("silu", h))
                ring_a.split_hi(act, g0 + 2)
                ring_a.split_hi(act, g0 + 3)
                for t in range(NT):
                    dve_out.wait(act, ("y", t))
                    act_steps.step(act, act.activation(scratch[:, t], yb[:, t], ACT.Square,
                                                       accum_out=stats[:, t, 3:4]))
                    act_out.raised(act.activation(stats[:, t, 4:5], stats[:, t, 3:4], ACT.Sqrt, bias=eps[:, 0:1],
                                                  scale=1.0 / D), ("yroot", t))
                for t in range(NT):
                    dve_out.wait(act, ("x", t))
                    rms_scale(act, None, t, scratch)
                turned_done.wait(act, 1)
                affine(act, hT, 2)

            silu_split = []

            @block.vector
            def _(dve):
                pe_out.wait(dve, "mean")
                dve_out.raised(dve.tensor_tensor(conv, conv, ps[:, 0:1, 0:SEQ].to_broadcast([P, KD, SEQ]),
                                                 ALU.subtract), "centred")
                ring_a.split_lo(dve, g0)
                act_out.wait(dve, "std")
                dve_steps.step(dve, dve.reciprocal(rstd, rstd))
                dve_out.raised(dve.tensor_tensor(conv, conv, rstd.unsqueeze(1).to_broadcast([P, KD, SEQ]), ALU.mult),
                               "normal")
                ring_a.split_lo(dve, g0 + 1)
                for h in range(2):
                    act_out.wait(dve, ("silu", h))
                    half = slice(4 * h, 4 * h + 4)
                    dve_steps.step(dve, dve.tensor_copy(actT[:, 0, half], conv[:, half]))
                    dve_steps.step(dve, dve.tensor_tensor(actT[:, 1, half], conv[:, half],
                                                          actT[:, 0, half].bitcast(F32), ALU.subtract))
                    silu_split.append(dve_steps.n)
                ring_a.split_lo(dve, g0 + 2)
                ring_a.split_lo(dve, g0 + 3)
                ring_a.wait_used(dve, g0 + 3)
                dve.wait_ge(rows_loaded, b2_row)
                for t in range(NT):
                    dve_out.raised(dve.tensor_tensor(yb[:, t], acc[t], rows[:, 0], ALU.add), ("y", t))
                for t in range(NT):
                    act_out.wait(dve, ("yroot", t))
                    dve_steps.step(dve, dve.reciprocal(stats[:, t, 5:6], stats[:, t, 4:5]))
                    dve_steps.step(dve, dve.scalar_tensor_tensor(yb[:, t], yb[:, t], stats[:, t, 5:6], gate_m[:],
                                                                 ALU.mult, ALU.mult))
                    dve_out.raised(dve.tensor_tensor(x_tok[:, t], x_tok[:, t], yb[:, t], ALU.add), ("x", t))
                for t in range(NT):
                    rms_scale(None, dve, t, scratch)
                split_affine(dve, hT)

            @block.tensor
            def _(pe):
                for k in range(KD):
                    ins = pe.matmul(ps[:, 0, 0:SEQ], ones_mean[:], conv[:, k], start=k == 0, stop=k == KD - 1)
                pe_out.raised(ins, "mean")
                act_out.wait(pe, "square")
                for k in range(KD):
                    ins = pe.matmul(ps[:, 1, 0:SEQ], ones_mean[:], sq[:, k], start=k == 0, stop=k == KD - 1)
                pe_out.raised(ins, "var")
                act_out.wait(pe, "std")
                for c in range(4):
                    ring_a.wait_split(pe, g0 + c)
                    if c % 2 == 0:
                        dve_steps.upto(pe, silu_split[c // 2])
                    for k in range(2 * c, 2 * c + 2):
                        for t in range(NT):
                            for n in range(2):
                                w = [ring_a.part(g0 + c, s, (k % 2) * D + n * 512, (k % 2) * D + n * 512 + 512)
                                     for s in range(2)]
                                ins = mm3(pe, acc[t][:, n * 512:(n + 1) * 512],
                                          [actT[:, s, k, t * P:(t + 1) * P] for s in range(2)], w, k == 0, k == KD - 1)
                    ins.then_inc(ring_a.used, 1)
                for t in range(NT):
                    dve_out.wait(pe, ("xn", t))
                    turn(pe, scratch, t)

        h_done, f_step, conv_in, conv_done = sem("h_done"), sem("f_step"), sem("conv_in"), sem("conv_done")
        gated, scaled_x, root_ready = sem("gated"), sem("scaled_x"), sem("root_ready")
        done = {"h": 0, "f_step": 0, "conv": 0, "gated": 0}

        def ffn_stage(name, conv, norm_rows, turn_x, next_a, next_b):
            cg, cu, hf, yb, xs = carve((2, SEQ), (2, SEQ), (2, SEQ), (NT, D), (NT, D))
            ga, gb = sec[name], sec[name, "B"]
            sa, sb_ = ring_a.split_no[ga], ring_b.split_no[gb]
            la, lb = [ring_a.load_no[ga + q] - 32 for q in range(2)], [ring_b.load_no[gb + q] - 16 for q in range(2)]
            h0, f0, c0, s0 = done["h"], done["f_step"], done["conv"], done["gated"]
            per = 4 if conv else 2
            done["h"] += NF
            done["f_step"] += per * NF
            done["conv"] += NF if conv else 0
            done["gated"] += NF
            BODY = NF // 2
            if not conv:
                rows_count[0] += 32
            rows_at = rows_count[0]
            dve_out.events([(n, t) for n in ("stat", "y") for t in range(NT)] if conv else
                           [("stat", 0), ("stat", 1), ("x", 0), ("x", 1)])
            act_out.events([("root", t) for t in range(NT)] + ([("hi", h) for h in range(2)] if turn_x else []))
            if turn_x:
                turned_done.events([0, 1])
            if not conv:
                pool_out.events(["xs"])

            with nc.Block() as block:
                @block.sync
                def _(sp):
                    if norm_rows:
                        load_row(sp, 0, norm_rows[0])
                        load_row(sp, 1, norm_rows[1])
                    gate = chunks_a[ga][0][0][2].tensor, chunks_a[ga][0][1][2].tensor
                    src = FFN_SOURCES[name]
                    with sp.Fori(1, BODY) as j:
                        for q in range(2):
                            sp.wait_ge(ring_a.lo_done, j * 2 + (sa + q - 1))
                            for half in range(2):
                                sp.dma_start(a_raw[:, q, half * BCH:(half + 1) * BCH].rearrange("p (k n) -> p k n", k=KD),
                                             src[half][:, :, bass.ds(j * 256 + q * P, P)])\
                                    .then_inc(ring_a.loaded[q], 16)
                            sp.wait_ge(ring_b.lo_done, j * 2 + (sb_ + q - 1))
                            sp.dma_start(b_raw[:, q], src[2][bass.ds(j * 2 + q, 1), :, :].rearrange("a p n -> (a p) n"))\
                                .then_inc(ring_b.loaded[q], 16)
                    for g in range(next_a, next_a + 2):
                        ring_a.load(sp, g)
                    for g in range(next_b, next_b + 2):
                        ring_b.load(sp, g)

                def split(act_or_none, dve_or_none, q, a_count, b_count, a_load, b_load, first):
                    if act_or_none is not None:
                        act = act_or_none
                        act.wait_ge(ring_a.loaded[q], a_load)
                        if a_count[1] is not None:
                            act.wait_ge(ring_a.used, a_count[1])
                        act.activation(a_parts[:, q, 0], a_raw[:, q], ACT.Copy).then_inc(ring_a.hi_done, 1)
                        act.wait_ge(ring_b.loaded[q], b_load)
                        if b_count[1] is not None:
                            act.wait_ge(ring_b.used, b_count[1])
                        act.activation(b_parts[:, q, 0], b_raw[:, q], ACT.Copy).then_inc(ring_b.hi_done, 1)
                    else:
                        dve = dve_or_none
                        dve.wait_ge(ring_a.hi_done, a_count[0])
                        dve.tensor_tensor(a_parts[:, q, 1], a_raw[:, q], a_parts[:, q, 0].bitcast(F32),
                                          ALU.subtract).then_inc(ring_a.lo_done, 1)
                        dve.wait_ge(ring_b.hi_done, b_count[0])
                        dve.tensor_tensor(b_parts[:, q, 1], b_raw[:, q], b_parts[:, q, 0].bitcast(F32),
                                          ALU.subtract).then_inc(ring_b.lo_done, 1)

                def tile_split(act, dve, q, j):
                    first = isinstance(j, int)
                    a_used = None if first and sa + 2 * j + q < 2 else j * 2 + (sa + q - 1)
                    b_used = None if first and sb_ + 2 * j + q < 2 else j * 2 + (sb_ + q - 1)
                    split(act, dve, q, (j * 2 + (sa + q + 1), a_used), (j * 2 + (sb_ + q + 1), b_used),
                          j * 32 + (la[q] + 32), j * 16 + (lb[q] + 16), first)

                def tile_act(act, q, j):
                    first = isinstance(j, int) and j == 0
                    act.wait_ge(ring_a.used, j * 2 + (sa + q + 1))
                    if not first:
                        act.wait_ge(h_done, j * 2 + (h0 + q - 1))
                    gate, up = ps[:, 4 + q, 0:SEQ], ps[:, 4 + q, SEQ:2 * SEQ]
                    if conv:
                        for buf, src, half in ((cg, gate, 0), (cu, up, NF)):
                            w = col_at("f_dw_w", 2 * 2 * NF + half + q, j)
                            b = col_at("f_dw_b", half + q, j)
                            ins = act.activation(buf[:, q], src, ACT.Identity, bias=b, scale=w)
                        ins.then_inc(conv_in, 1)
                        act.wait_ge(conv_done, j * 2 + (c0 + q + 1))
                        act.activation(cg[:, q], cg[:, q], ACT.Silu).then_inc(gated, 1)
                    else:
                        act.activation(cg[:, q], gate, ACT.Silu).then_inc(gated, 1)

                def col_at(name, i, j):
                    if isinstance(j, int):
                        return col(name, i + 2 * j)
                    return par[:, bass.ds(j * 2 + (first_col[name] + i), 1)]

                def tile_dve(dve, q, j):
                    n = f0 + per * q
                    gate, up = ps[:, 4 + q, 0:SEQ], ps[:, 4 + q, SEQ:2 * SEQ]
                    if conv:
                        dve.wait_ge(conv_in, j * 2 + (c0 + q + 1))
                        for back in (1, 2):
                            for buf, src, half in ((cg, gate, 0), (cu, up, NF)):
                                w = col_at("f_dw_w", (2 - back) * 2 * NF + half + q, j)
                                if back == 2:
                                    dve.wait_ge(f_step, j * (2 * per) + (n + (1 if half == 0 else 2)))
                                ins = dve.scalar_tensor_tensor(buf[:, q, back:SEQ], src[:, 0:SEQ - back], w,
                                                               buf[:, q, back:SEQ], ALU.mult, ALU.add)
                                if back == 1:
                                    ins.then_inc(f_step, 1)
                        ins.then_inc(conv_done, 1)
                        n += 2
                        up = cu[:, q]
                    dve.wait_ge(gated, j * 2 + (s0 + q + 1))
                    dve.tensor_tensor(hf[:, q], cg[:, q], up, ALU.mult).then_inc(f_step, 1)
                    if not (isinstance(j, int) and j == 0 and sb_ + q < 2):
                        dve.wait_ge(ring_b.used, j * 2 + (sb_ + q - 1))
                    dve.wait_ge(f_step, j * (2 * per) + (n + 1))
                    dve.tensor_copy(hid[:, q, 0], hf[:, q]).then_inc(f_step, 1)
                    dve.wait_ge(f_step, j * (2 * per) + (n + 2))
                    dve.tensor_tensor(hid[:, q, 1], hf[:, q], hid[:, q, 0].bitcast(F32),
                                      ALU.subtract).then_inc(h_done, 1)

                def up_pe(pe, q, j):
                    first = isinstance(j, int) and j == 0
                    pe.wait_ge(ring_a.lo_done, j * 2 + (sa + q + 1))
                    if not first:
                        pe.wait_ge(h_done, j * 2 + (h0 + q - 1))
                    for n in range(2):
                        for k in range(KD):
                            w = [a_parts[:, q, s, n * BCH + k * P:n * BCH + (k + 1) * P] for s in range(2)]
                            ins = mm3(pe, ps[:, 4 + q, n * SEQ:(n + 1) * SEQ], w, [actT[:, s, k] for s in range(2)],
                                      k == 0, k == KD - 1)
                    ins.then_inc(ring_a.used, 1)

                def down_pe(pe, q, j, start, stop):
                    pe.wait_ge(ring_b.lo_done, j * 2 + (sb_ + q + 1))
                    pe.wait_ge(h_done, j * 2 + (h0 + q + 1))
                    for t in range(NT):
                        for n in range(2):
                            ins = mm3(pe, acc[t][:, n * 512:(n + 1) * 512],
                                      [hid[:, q, s, t * P:(t + 1) * P] for s in range(2)],
                                      [b_parts[:, q, s, n * 512:(n + 1) * 512] for s in range(2)], start, stop)
                    ins.then_inc(ring_b.used, 1)

                @block.tensor
                def _(pe):
                    up_pe(pe, 0, 0)
                    up_pe(pe, 1, 0)
                    down_pe(pe, 0, 0, True, False)
                    with pe.Fori(1, BODY) as j:
                        up_pe(pe, 0, j)
                        down_pe(pe, 1, j - 1, False, False)
                        up_pe(pe, 1, j)
                        down_pe(pe, 0, j, False, False)
                    down_pe(pe, 1, BODY - 1, False, True)
                    if turn_x:
                        for t in range(NT):
                            dve_out.wait(pe, ("x" if not conv else "y", t))
                            turn(pe, x_tok, t)

                @block.scalar
                def _(act):
                    tile_split(act, None, 0, 0)
                    tile_split(act, None, 1, 0)
                    tile_act(act, 0, 0)
                    with act.Fori(1, BODY) as j:
                        tile_split(act, None, 0, j)
                        tile_act(act, 1, j - 1)
                        tile_split(act, None, 1, j)
                        tile_act(act, 0, j)
                    tile_act(act, 1, BODY - 1)
                    if conv:
                        act.wait_ge(ring_b.used, sb_ + NF)
                        for t in range(NT):
                            act.activation(yb[:, t], acc[t], ACT.Square, accum_out=stats[:, t, 6:7])\
                               .then_inc(act_steps.sem, 1)
                            act_steps.n += 1
                            act_steps.upto(act, act_steps.n)
                            act_out.raised(act.activation(stats[:, t, 7:8], stats[:, t, 6:7], ACT.Sqrt,
                                                          bias=eps[:, 0:1], scale=1.0 / D), ("root", t))
                    else:
                        for t in range(NT):
                            dve_out.wait(act, ("stat", t))
                            act_out.raised(act.activation(stats[:, t, 7:8], stats[:, t, 13:14], ACT.Sqrt,
                                                          bias=eps[:, 1:2]), ("root", t))
                    if turn_x:
                        turned_done.wait(act, 1)
                        split_turned_act(act)

                @block.gpsimd
                def _(pool):
                    if not conv:
                        pool_out.raised(pool.tensor_scalar(xs, x_tok[:], ALPHA, None, ALU.mult), "xs")

                @block.vector
                def _(dve):
                    tile_split(None, dve, 0, 0)
                    tile_split(None, dve, 1, 0)
                    tile_dve(dve, 0, 0)
                    with dve.Fori(1, BODY) as j:
                        tile_split(None, dve, 0, j)
                        tile_dve(dve, 1, j - 1)
                        tile_split(None, dve, 1, j)
                        tile_dve(dve, 0, j)
                    tile_dve(dve, 1, BODY - 1)
                    dve.wait_ge(ring_b.used, sb_ + NF)
                    if conv:
                        for t in range(NT):
                            act_out.wait(dve, ("root", t))
                            dve_out.raised(dve.reciprocal(stats[:, t, 8:9], stats[:, t, 7:8]), ("stat", t))
                        for t in range(NT):
                            dve_out.wait(dve, ("stat", t))
                            dve_steps.step(dve, dve.scalar_tensor_tensor(yb[:, t], acc[t], stats[:, t, 8:9],
                                                                         gate_f[:], ALU.mult, ALU.mult))
                            dve_out.raised(dve.tensor_tensor(x_tok[:, t], x_tok[:, t], yb[:, t], ALU.add), ("y", t))
                    else:
                        layer_norm_dve(dve, yb, xs, 0.5, rows_at)
                    if turn_x:
                        split_turned_dve(dve)

        def layer_norm_dve(dve, yb, xs, scale, rows_at):
            pool_out.wait(dve, "xs")
            for t in range(NT):
                dve_steps.step(dve, dve.scalar_tensor_tensor(yb[:, t], acc[t], scale, xs[:, t], ALU.mult, ALU.add))
                for n in range(2):
                    dve_steps.step(dve, dve.bn_stats(stats[:, t, 6 * n:6 * n + 6], yb[:, t, n * 512:(n + 1) * 512]))
                dve_out.raised(dve.bn_aggr(stats[:, t, 12:14], stats[:, t, 0:12]), ("stat", t))
            dve.wait_ge(rows_loaded, rows_at)
            for t in range(NT):
                act_out.wait(dve, ("root", t))
                dve_steps.step(dve, dve.reciprocal(stats[:, t, 14:15], stats[:, t, 7:8]))
                dve_steps.step(dve, dve.tensor_scalar(yb[:, t], yb[:, t], stats[:, t, 12:13], stats[:, t, 14:15],
                                                      ALU.subtract, ALU.mult))
                dve_steps.step(dve, dve.tensor_tensor(yb[:, t], yb[:, t], rows[:, 0], ALU.mult))
                dve_out.raised(dve.tensor_tensor(x_tok[:, t], yb[:, t], rows[:, 1], ALU.add), ("x", t))

        def ffn_views(gate, up_w, down):
            g, u = (w.rearrange("(k p) n -> p k n", p=P) for w in (gate, up_w))
            return g, u, down.rearrange("(i p) n -> i p n", p=P)

        FFN_SOURCES = {"ffn": ffn_views(A["f_up_w"][0][:, 0:DFF], A["f_up_w"][0][:, DFF:2 * DFF], A["f_down_w"][0])}
        for i in range(2):
            for f in ("ffn1", "ffn2"):
                FFN_SOURCES[f, i] = ffn_views(*(A[f"{f}_w_{n}_2"][i] for n in ("gate", "up", "down")))

        def memory_attention(mqT, probs, probsT):
            n = NMH * NT
            pe_out.events([("scores",), ("probsT",), ("out",)])
            act_out.events([("exp",), ("probsT",), ("hi",)])
            dve_out.events([("max",), ("probs",), ("probsT",), ("lo",)])
            scores = ps[:, 0:4, :].rearrange("p b (t m) -> p (b t) m", t=NT)
            bank = lambda h: 2 * (h % 2) + h // 2
            neg_max, total, inv = small[:, 0:n], small[:, n:2 * n], small[:, 2 * n:3 * n]
            with nc.Block() as block:
                @block.tensor
                def _(pe):
                    for h in range(NMH):
                        r = slice((h % 2) * HD, (h % 2) * HD + HD)
                        for t in range(NT):
                            ins = pe.matmul(scores[:, 2 * bank(h) + t], mqT[r, h // 2, t * P:(t + 1) * P],
                                            memkT[r, h // 2, :], start=True, stop=True)
                    pe_out.raised(ins, ("scores",))
                    dve_out.wait(pe, ("probs",))
                    for h in range(NMH):
                        for m in range(2):
                            for t in range(NT):
                                ins = pe.transpose(turned[:, 2 * h + m, t * P:(t + 1) * P],
                                                   probs[:, 2 * bank(h) + t, m * P:(m + 1) * P], ident[:])
                    pe_out.raised(ins, ("probsT",))
                    act_out.wait(pe, ("probsT",))
                    dve_out.wait(pe, ("probsT",))
                    for h in range(NMH):
                        for m in range(2):
                            ins = pe.matmul(ps[(h % 2) * HD:(h % 2) * HD + HD, h // 2, 0:SEQ],
                                            memv[:, m, h * HD:(h + 1) * HD], probsT[:, 2 * h + m, :],
                                            start=m == 0, stop=m == 1)
                    pe_out.raised(ins, ("out",))

                @block.vector
                def _(dve):
                    pe_out.wait(dve, ("scores",))
                    dve_out.raised(dve.tensor_reduce(neg_max, scores, AX_X, ALU.max, negate=True), ("max",))
                    act_out.wait(dve, ("exp",))
                    dve_steps.step(dve, dve.reciprocal(inv, total))
                    dve_out.raised(dve.tensor_tensor(probs, probs, inv.unsqueeze(2).to_broadcast([P, n, NMEM]),
                                                     ALU.mult), ("probs",))
                    pe_out.wait(dve, ("probsT",))
                    dve_out.raised(dve.tensor_copy(probsT[:, 4:8], turned[:, 4:8]), ("probsT",))
                    act_out.wait(dve, ("hi",))
                    dve_out.raised(dve.tensor_tensor(actT[:, 1, 6:8], ps[:, 0:2, 0:SEQ],
                                                     actT[:, 0, 6:8].bitcast(F32), ALU.subtract), ("lo",))

                @block.scalar
                def _(act):
                    dve_out.wait(act, ("max",))
                    for i in range(n):
                        ins = act.activation(probs[:, i], scores[:, i], ACT.Exp, bias=neg_max[:, i:i + 1],
                                             accum_out=total[:, i:i + 1])
                    act_out.raised(ins, ("exp",))
                    pe_out.wait(act, ("probsT",))
                    act_out.raised(act.activation(probsT[:, 0:4], turned[:, 0:4], ACT.Copy), ("probsT",))
                    pe_out.wait(act, ("out",))
                    act_out.raised(act.activation(actT[:, 0, 6:8], ps[:, 0:2, 0:SEQ], ACT.Copy), ("hi",))

        def output_stage(i):
            yb, xs = carve((NT, D), (NT, D))
            g0, nxt = sec["w_out", i], sec[("ffn2", i), "B"]
            dve_out.events([("stat", 0), ("stat", 1), ("x", 0), ("x", 1)])
            act_out.events([("root", 0), ("root", 1), ("hi", 0), ("hi", 1)])
            turned_done.events([0, 1])
            pool_out.events(["xs"])
            rows_count[0] += 32
            rows_at = rows_count[0]
            with nc.Block() as block:
                @block.sync
                def _(sp):
                    load_row(sp, 0, A["ln_g_2"][i, 1])
                    load_row(sp, 1, A["ln_b_2"][i, 1])
                    for g in range(g0 + 2, g0 + 4 + 2):
                        ring_a.load(sp, g)

                @block.gpsimd
                def _(pool):
                    pool_out.raised(pool.tensor_scalar(xs, x_tok[:], ALPHA, None, ALU.mult), "xs")

                @block.scalar
                def _(act):
                    for c in range(4):
                        ring_a.split_hi(act, g0 + c)
                    for t in range(NT):
                        dve_out.wait(act, ("stat", t))
                        act_out.raised(act.activation(stats[:, t, 7:8], stats[:, t, 13:14], ACT.Sqrt,
                                                      bias=eps[:, 1:2]), ("root", t))
                    turned_done.wait(act, 1)
                    split_turned_act(act)

                @block.vector
                def _(dve):
                    for c in range(4):
                        ring_a.split_lo(dve, g0 + c)
                    ring_a.wait_used(dve, g0 + 3)
                    layer_norm_dve(dve, yb, xs, 1.0, rows_at)
                    split_turned_dve(dve)

                @block.tensor
                def _(pe):
                    for c in range(4):
                        ring_a.wait_split(pe, g0 + c)
                        down_chunk(pe, g0 + c, c)
                    for t in range(NT):
                        dve_out.wait(pe, ("x", t))
                        turn(pe, x_tok, t)

        def down_chunk(pe, g, c):
            for k in range(2 * c, 2 * c + 2):
                for t in range(NT):
                    for n in range(2):
                        w = [ring_a.part(g, s, (k % 2) * D + n * 512, (k % 2) * D + n * 512 + 512) for s in range(2)]
                        ins = mm3(pe, acc[t][:, n * 512:(n + 1) * 512],
                                  [actT[:, s, k, t * P:(t + 1) * P] for s in range(2)], w, k == 0, k == KD - 1)
            ins.then_inc(ring_a.used, 1)

        def rwkv_stages():
            z, mqT, lora, g_up, SIG, CUM, Av, KK, BON = carve(
                (20, SEQ), (2, SEQ), (C,), (C,), (MT6, SEQ), (MT6, SEQ), (MT6, SEQ), (MT6, SEQ), (MT6, SEQ))
            R, K, V = (z[:, MT6 * i:MT6 * (i + 1)] for i in range(3))
            low, lowg = z[:, 18], z[:, 19]
            used = (20 + 2) * SEQ + 2 * C + 5 * MT6 * SEQ
            reset = gate_m[:, C:D]
            mk = rows[:].rearrange("p a (m n) -> p (a m) n", n=P)
            level_mask = [mk[:, l] for l in range(6)]
            pair_mask, below, upto = mk[:, 6], mk[:, 7], mk[:, 8]
            one_minus_mu, one_minus_ka = small[:, 24:44], small[:, 44:50]

            g0 = sec["rwkv_in"]
            act_out.events([("z", m) for m in range(20)] + ["mq"])
            dve_out.events(["mu"] + [("z", m) for m in range(20)])
            load_at = 16 * 3
            lora_loaded = sem("lora_loaded")
            with nc.Block() as block:
                @block.sync
                def _(sp):
                    sp.dma_start(lora[0:HD], A["rwkv_w_up_2"][0]).then_inc(lora_loaded, 16)
                    sp.dma_start(lora[HD:P], A["rwkv_a_up_2"][0]).then_inc(lora_loaded, 16)
                    sp.dma_start(g_up, A["rwkv_g_up_2"][0]).then_inc(lora_loaded, 16)
                    for g in range(g0 + 2, g0 + 12 + 2):
                        ring_a.load(sp, g)

                @block.gpsimd
                def _(pool):
                    def select(view, base, cm, pattern):
                        pool_steps.step(pool, pool.affine_select(out=view, in_=view, compare_op=ALU.is_ge, fill=0.0,
                                                                 base=base, pattern=pattern, channel_multiplier=cm))
                    pool_steps.step(pool, pool.memset(mk[:, 0:9], 0.0))
                    for l in range(6):
                        b = 1 << l
                        view = level_mask[l].rearrange("p (B h w) -> p B h w", h=2, w=b)[:, :, 1]
                        pool_steps.step(pool, pool.memset(view, 1.0))
                        select(view, 0, 1, [[-2 * b, P // (2 * b)], [0, b]])
                        select(view, b - 1, -1, [[2 * b, P // (2 * b)], [0, b]])
                    view = pair_mask.rearrange("p (B h) -> p B h", h=2)[:, :, 0]
                    pool_steps.step(pool, pool.memset(view, 1.0))
                    select(view, -1, 1, [[-2, P // 2]])
                    select(view, 1, -1, [[2, P // 2]])
                    for m, base in ((below, -1), (upto, 0)):
                        view = m.rearrange("p (c w) -> p c w", w=CHUNK)
                        pool_steps.step(pool, pool.memset(m, 1.0))
                        select(view, base, -1, [[CHUNK, 2], [1, CHUNK]])
                        select(view, 0, 1, [[-CHUNK, 2], [0, CHUNK]])
                    pool_steps.step(pool, pool.memset(reset, 1.0))
                    pool_steps.step(pool, pool.memset(reset.rearrange("p (c w) -> p c w", w=CHUNK)[:, :, 0:1], 0.0))

                @block.tensor
                def _(pe):
                    for c in range(12):
                        g = g0 + c
                        ring_a.wait_split(pe, g)
                        if c >= 8:
                            dve_out.wait(pe, ("z", 2 * (c - 8) + 1))
                        width = 256 if c < 10 else P
                        for n in range(width // P):
                            for k in range(KD):
                                w = [ring_a.part(g, s, k * width + n * P, k * width + n * P + P) for s in range(2)]
                                ins = mm3(pe, ps[:, c % 8, n * SEQ:(n + 1) * SEQ], w, [actT[:, s, k] for s in range(2)],
                                          k == 0, k == KD - 1)
                        ins.then_inc(ring_a.used, 1)

                @block.scalar
                def _(act):
                    dve_out.wait(act, "mu")
                    for c in range(13):
                        if c < 12:
                            ring_a.split_hi(act, g0 + c)
                        if 1 <= c <= 10:
                            ring_a.wait_used(act, g0 + c - 1)
                            for n in range(2):
                                m = 2 * (c - 1) + n
                                act_out.raised(act.activation(z[:, m], ps[:, (c - 1) % 8, n * SEQ:(n + 1) * SEQ],
                                                              ACT.Copy, scale=one_minus_mu[:, m:m + 1]), ("z", m))
                    ring_a.wait_used(act, g0 + 11)
                    act_out.raised(act.activation(mqT, ps[:, 2:4, 0:SEQ], ACT.Copy, scale=HD ** -0.5), "mq")

                @block.vector
                def _(dve):
                    dve_steps.mark(dve.tensor_scalar(one_minus_ka, cols("k_a", MT6), -1.0, 1.0, ALU.mult, ALU.add))
                    dve_out.raised(dve.tensor_scalar(one_minus_mu, cols("mu", 20), -1.0, 1.0, ALU.mult, ALU.add), "mu")
                    for c in range(12):
                        ring_a.split_lo(dve, g0 + c)
                        if 1 <= c <= 10:
                            for n in range(2):
                                m = 2 * (c - 1) + n
                                act_out.wait(dve, ("z", m | 1))
                                src = ps[:, (c - 1) % 8, n * SEQ:(n + 1) * SEQ - 1]
                                dve_out.raised(dve.scalar_tensor_tensor(z[:, m, 1:SEQ], src, col("mu", m),
                                                                        z[:, m, 1:SEQ], ALU.mult, ALU.add), ("z", m))

            memory_attention(mqT, arena[:, 22 * SEQ + 2 * C:22 * SEQ + 2 * C + 2048].rearrange("p (a b) -> p a b", a=8),
                             arena[:, 22 * SEQ + 2 * C + 2048:22 * SEQ + 2 * C + 4096].rearrange("p (a b) -> p a b", a=8))

            wv = ps[:, 0:3, :].rearrange("p b (m t) -> p (b m) t", m=2)
            av = ps[:, 3:6, :].rearrange("p b (m t) -> p (b m) t", m=2)
            w_end = small[:, 0:24].rearrange("p (m c) -> p m c", m=MT6)
            pe_out.events(["w", "a", "norm", "bonus"])
            act_out.events(["low", "sig", "kk", "a", "square", "root", "Wex", "Winv", "W"])
            dve_out.events(["cum", "ss", "kk", "k", "rk", "bon", "cumx", "q", "b", "kb"])
            with nc.Block() as block:
                @block.tensor
                def _(pe):
                    act_out.wait(pe, "low")
                    pe.wait_ge(lora_loaded, 48)
                    for m in range(MT6):
                        ins = pe.matmul(wv[:, m], lora[0:HD, m * P:(m + 1) * P], low[0:HD], start=True, stop=True)
                    pe_out.raised(ins, "w")
                    for m in range(MT6):
                        ins = pe.matmul(av[:, m], lora[HD:P, m * P:(m + 1) * P], low[HD:P], start=True, stop=True)
                    pe_out.raised(ins, "a")
                    act_out.wait(pe, "square")
                    for m in range(MT6):
                        ins = pe.matmul(wv[:, m], head_ones[:], BON[:, m], start=True, stop=True)
                    pe_out.raised(ins, "norm")
                    dve_out.wait(pe, "rk")
                    for m in range(MT6):
                        ins = pe.matmul(av[:, m], head_ones[:], BON[:, m], start=True, stop=True)
                    pe_out.raised(ins, "bonus")

                @block.scalar
                def _(act):
                    act_out.raised(act.activation(low[0:HD], low[0:HD], ACT.Tanh), "low")
                    pe_out.wait(act, "w")
                    for m in range(MT6):
                        ins = act.activation(SIG[:, m], wv[:, m], ACT.Sigmoid, bias=col("w0", m))
                    act_out.raised(ins, "sig")
                    for m in range(MT6):
                        ins = act.activation(KK[:, m], K[:, m], ACT.Copy, scale=col("k_k", m))
                    act_out.raised(ins, "kk")
                    pe_out.wait(act, "a")
                    for m in range(MT6):
                        ins = act.activation(Av[:, m], av[:, m], ACT.Sigmoid, bias=col("a0", m))
                    act_out.raised(ins, "a")
                    act_steps.step(act, act.activation(lowg, lowg, ACT.Sigmoid))
                    act_out.wait(act, "kk")
                    act_out.raised(act.activation(BON, KK, ACT.Square), "square")
                    dve_out.wait(act, "ss")
                    act_out.raised(act.activation(BON, BON, ACT.Sqrt), "root")
                    dve_out.wait(act, "cumx")
                    act_out.raised(act.activation(SIG, SIG, ACT.Exp, scale=-DECAY), "Wex")
                    dve_out.wait(act, "b")
                    act_out.raised(act.activation(KK, CUM, ACT.Exp, scale=DECAY), "Winv")
                    act_out.wait(act, "Winv")
                    act_out.raised(act.activation(CUM, CUM, ACT.Exp, scale=-DECAY), "W")

                @block.vector
                def _(dve):
                    act_out.wait(dve, "sig")
                    for m in range(MT6):
                        ins = dve.tensor_tensor_scan(CUM[:, m], reset, SIG[:, m], 0.0, ALU.mult, ALU.add)
                    dve_out.raised(ins, "cum")
                    pe_out.wait(dve, "norm")
                    dve_out.raised(dve.tensor_scalar(BON, wv, 1e-24, None, ALU.max), "ss")
                    act_out.wait(dve, "root")
                    dve_steps.step(dve, dve.reciprocal(BON, BON))
                    dve_out.raised(dve.tensor_tensor(KK, KK, BON, ALU.mult), "kk")
                    dve_out.wait(dve, "kk")
                    act_out.wait(dve, "a")
                    for m in range(MT6):
                        ins = dve.tensor_scalar(BON[:, m], Av[:, m], col("k_a", m), one_minus_ka[:, m:m + 1],
                                                ALU.mult, ALU.add)
                    dve_steps.step(dve, ins)
                    dve_out.raised(dve.tensor_tensor(K, K, BON, ALU.mult), "k")
                    dve_out.wait(dve, "k")
                    for m in range(MT6):
                        ins = dve.scalar_tensor_tensor(BON[:, m], R[:, m], col("r_k", m), K[:, m], ALU.mult, ALU.mult)
                    dve_out.raised(ins, "rk")
                    pe_out.wait(dve, "bonus")
                    dve_out.raised(dve.tensor_tensor(BON, av, V, ALU.mult), "bon")
                    dve_out.raised(dve.tensor_tensor(SIG, CUM, SIG, ALU.subtract), "cumx")
                    act_out.wait(dve, "Wex")
                    dve_out.raised(dve.tensor_tensor(SIG, SIG, KK, ALU.mult), "q")
                    dve_out.raised(dve.scalar_tensor_tensor(Av, KK, -1.0, Av, ALU.mult, ALU.mult), "b")
                    act_out.wait(dve, "Winv")
                    dve_out.wait(dve, "b")
                    dve_steps.step(dve, dve.tensor_tensor(Av, Av, KK, ALU.mult))
                    dve_out.raised(dve.tensor_tensor(K, K, KK, ALU.mult), "kb")
                    act_out.wait(dve, "W")
                    dve_steps.step(dve, dve.tensor_tensor(R, R, CUM, ALU.mult))
                    dve_steps.step(dve, dve.tensor_copy(w_end, CUM.rearrange("p m (c w) -> p m c w", w=CHUNK)
                                                        [:, :, :, CHUNK - 1]))
            rwkv_core(R, K, V, SIG, Av, BON, CUM, KK, lowg, g_up, w_end, level_mask, pair_mask, below, upto, used)

        def rwkv_core(R, K, V, Q, BB, BON, CUM, KK, lowg, g_up, w_end, level_mask, pair_mask, below, upto, used):
            LV = range(1, 6)
            units = [(T, hf) for T in range(NT) for hf in range(2)]
            Vt, Qt = (CUM.rearrange("p m t -> p (m t)")[:, i * C:(i + 1) * C] for i in range(2))
            Kt, Bt = (KK.rearrange("p m t -> p (m t)")[:, i * C:(i + 1) * C] for i in range(2))
            tok = (Vt, Qt, Kt, Bt)

            def piece(at, *shape):
                ap = arena[:, at:at + math.prod(shape)]
                return ap.rearrange("p (a b c) -> p a b c", a=shape[0], b=shape[1]) if len(shape) == 3 else \
                    ap.rearrange("p (a b) -> p a b", a=shape[0])

            free = 20 * SEQ
            LkV, U, S = piece(free, 2, 3, HD), piece(free + 384, 2, 3, HD), piece(free + 768, MT6, HD)
            Z, LT, M0, M1 = (piece(used + i * 768, 2, 3, P) for i in range(4))
            M = (M0, M1)
            O = piece(used + 4 * 768, MT6, 2, HD)
            assert used + 5 * 768 <= arena_words
            Dm = gate_m[:, 0:C].rearrange("p (a b c) -> p a b c", a=2, b=3)
            DT = gate_f[:, 0:C].rearrange("p (a b c) -> p a b c", a=2, b=3)
            A1 = Z[:, 0]
            Oh = O.rearrange("p m a d -> p (m a) d")
            hs = [small[:, 64 + 12 * i:76 + 12 * i] for i in range(4)]

            def bank(b, cols=3 * P):
                return ps[:, b, 0:cols].rearrange("p (m t) -> p m t", m=3)

            def bmask(m):
                return m.unsqueeze(1).to_broadcast([P, 3, P])

            def first_chunk(T, c):
                return T == 0 and c == 0

            def last_chunk(T, c):
                return T == NT - 1 and c == 1

            pe_names, act_names, dve_names, pool_names = [], [], ["zero"], []
            for T in range(NT):
                pe_names += [("tr", T, i) for i in range(4)]
                act_names += [("tok", T, i) for i in range(2)]
                dve_names += [("tok", T, i) for i in range(2, 4)]
                for hf in range(2):
                    u = (T, hf)
                    pe_names += [(n, u, p) for p in range(2) for n in ("LbT", "Lb", "LkT")]
                    pe_names += [("LkV", u, p) for p in range(2)]
                    act_names += [("LT", u, p) for p in range(2)] + [("LkV", u, p) for p in range(2)]
                    dve_names += [(n, u, p) for p in range(2) for n in ("D1", ("D", 0), "LkT")]
                    pool_names += [(n, u, p) for p in range(2) for n in ("DT1", ("DT", 0))]
                    for l in LV:
                        pe_names += [(("Z", l), u, p) for p in range(2)]
                        pe_names += [(n, u, p) for p in range(2) for n in ((("dD", l), ("dDT", l)) if l < 5 else (("dDT", l),))]
                        act_names += [(("Z", l), u, p) for p in range(2)]
                        dve_names += [(n, u, p) for p in range(2) for n in ((("D", l), ("DT", l)) if l < 5 else (("DT", l),))]
                        pool_names += [(("M", l), u, p) for p in range(2)]
                    pe_names += [(n, u, p) for p in range(2) for n in ("A1", "U0")]
                    pe_names += [(n, u, p) for p in range(2) for n in ("Lrk", "Lrb")]
                    act_names += [(n, u, p) for p in range(2) for n in ("A1", "U0")]
                    dve_names += [(n, u, p) for p in range(2) for n in ("Lrk", "Lrb")]
                    for c in range(2):
                        if not first_chunk(T, c):
                            pe_names += [(("U", c), u, p) for p in range(2)] + [(("RS", c), u, p) for p in range(2)]
                            act_names += [(("RS", c), u, p) for p in range(2)]
                            dve_names += [(("U", c), u, p) for p in range(2)]
                        if not last_chunk(T, c):
                            pe_names += [(("S", c), u)]
                            dve_names += ([] if first_chunk(T, c) else [(("S1", c), u)]) + [(("S", c), u)]
                    pe_names += [("O", u)]
                    dve_names += [("O", u)]
                pe_names += [("nt", T)]
                act_names += [("sq", T), ("std", T), ("ln", T)]
                dve_names += [("sum", T), ("mean", T), ("cen", T), ("var", T), ("inv", T), ("normal", T)]
            pe_names += ["G"]
            act_names += ["hi"]
            dve_names += ["y", "yg"]
            pe_out.events(pe_names)
            act_out.events(act_names)
            dve_out.events(dve_names)
            pool_out.events(pool_names)

            with nc.Block() as block:
                @block.tensor
                def _(pe):
                    for T in range(NT):
                        tt = slice(T * P, (T + 1) * P)
                        if T:
                            act_out.wait(pe, ("ln", T - 1))
                        for i, src in enumerate((V, Q, K, BB)):
                            two = ps[:, 2 * i:2 * i + 2, :].rearrange("p b n -> p (b n)")
                            for m in range(MT6):
                                ins = pe.transpose(two[:, m * P:(m + 1) * P], src[:, m, tt], ident[:])
                            pe_out.raised(ins, ("tr", T, i))
                        act_out.wait(pe, ("tok", T, 1))
                        dve_out.wait(pe, ("tok", T, 3))
                        for hf in range(2):
                            u = (T, hf)
                            if hf:
                                dve_out.wait(pe, ("O", (T, 0)))
                            for p in range(2):
                                r = slice(p * HD, p * HD + HD)
                                for name, b, lhs, rhs in (("LbT", 0, BB, Q), ("Lb", 2, Q, BB), ("LkT", 4, K, Q)):
                                    for mm in range(3):
                                        m = 3 * hf + mm
                                        ins = pe.matmul(bank(b + p)[:, mm], lhs[r, m, tt], rhs[r, m, tt],
                                                        start=True, stop=True)
                                    pe_out.raised(ins, (name, u, p))
                            for p in range(2):
                                dve_out.wait(pe, ("LkT", u, p))
                                for mm in range(3):
                                    h = 2 * (3 * hf + mm) + p
                                    ins = pe.matmul(bank(6 + p, 3 * HD)[:, mm], Z[:, p, mm], Vt[:, h * HD:(h + 1) * HD],
                                                    start=True, stop=True)
                                pe_out.raised(ins, ("LkV", u, p))
                            for l in LV:
                                for p in range(2):
                                    pool_out.wait(pe, (("M", l), u, p))
                                    dve_out.wait(pe, (("D", l - 1), u, p))
                                    for mm in range(3):
                                        ins = pe.matmul(bank(p)[:, mm], M[l % 2][:, p, mm], Dm[:, p, mm],
                                                        start=True, stop=True)
                                    pe_out.raised(ins, (("Z", l), u, p))
                                for p in range(2):
                                    act_out.wait(pe, (("Z", l), u, p))
                                    (dve_out if l > 1 else pool_out).wait(pe, (("DT", l - 1), u, p))
                                    if l < 5:
                                        for mm in range(3):
                                            ins = pe.matmul(bank(2 + p)[:, mm], DT[:, p, mm], Z[:, p, mm],
                                                            start=True, stop=True)
                                        pe_out.raised(ins, (("dD", l), u, p))
                                    for mm in range(3):
                                        ins = pe.matmul(bank(4 + p)[:, mm], Z[:, p, mm], DT[:, p, mm],
                                                        start=True, stop=True)
                                    pe_out.raised(ins, (("dDT", l), u, p))
                            for p in range(2):
                                r = slice(p * HD, p * HD + HD)
                                dve_out.wait(pe, (("DT", 5), u, p))
                                act_out.wait(pe, ("LkV", u, p))
                                for mm in range(3):
                                    h = 2 * (3 * hf + mm) + p
                                    ins = pe.matmul(bank(p)[r, mm], Qt[:, h * HD:(h + 1) * HD], DT[:, p, mm],
                                                    start=True, stop=True)
                                pe_out.raised(ins, ("A1", u, p))
                                for mm in range(3):
                                    ins = pe.matmul(ps[:, 6 + p, 192 + mm * HD:192 + (mm + 1) * HD], DT[:, p, mm],
                                                    LkV[:, p, mm], start=True, stop=True)
                                pe_out.raised(ins, ("U0", u, p))
                            for p in range(2):
                                r = slice(p * HD, p * HD + HD)
                                for name, b, lhs in (("Lrk", 2, K), ("Lrb", 4, BB)):
                                    for mm in range(3):
                                        m = 3 * hf + mm
                                        ins = pe.matmul(bank(b + p)[:, mm], lhs[r, m, tt], R[r, m, tt],
                                                        start=True, stop=True)
                                    pe_out.raised(ins, (name, u, p))
                            for c in range(2):
                                rc = slice(c * CHUNK, (c + 1) * CHUNK)
                                if not first_chunk(T, c):
                                    for p in range(2):
                                        r = slice(p * HD, p * HD + HD)
                                        act_out.wait(pe, ("U0", u, p))
                                        dve_out.wait(pe, (("S", 0), u) if c else (("S", 1), (T - 1, hf)))
                                        for mm in range(3):
                                            ins = pe.matmul(bank(6 + p, 3 * HD)[rc, mm], A1[r, mm, rc],
                                                            S[r, 3 * hf + mm, :], start=True, stop=True)
                                        pe_out.raised(ins, (("U", c), u, p))
                                    for p in range(2):
                                        r = slice(p * HD, p * HD + HD)
                                        if c:
                                            if not first_chunk(T, 0):
                                                act_out.wait(pe, (("RS", 0), u, p))
                                        for mm in range(3):
                                            m = 3 * hf + mm
                                            ins = pe.matmul(bank(p, 3 * HD)[rc, mm],
                                                            R[r, m, T * P + c * CHUNK:T * P + (c + 1) * CHUNK],
                                                            S[r, m, :], start=True, stop=True)
                                        pe_out.raised(ins, (("RS", c), u, p))
                                if not last_chunk(T, c):
                                    for p in range(2):
                                        r = slice(p * HD, p * HD + HD)
                                        if first_chunk(T, c):
                                            act_out.wait(pe, ("U0", u, p))
                                        else:
                                            dve_out.wait(pe, (("U", c), u, p))
                                        dve_out.wait(pe, ("Lrk", u, 0))
                                        for mm in range(3):
                                            h = 2 * (3 * hf + mm) + p
                                            hc = slice(h * HD, (h + 1) * HD)
                                            pe.matmul(bank(2, 3 * HD)[r, mm], Kt[rc, hc], Vt[rc, hc],
                                                      start=True, stop=False)
                                            ins = pe.matmul(bank(2, 3 * HD)[r, mm], Bt[rc, hc], U[rc, p, mm],
                                                            start=False, stop=True)
                                    pe_out.raised(ins, (("S", c), u))
                            for p in range(2):
                                dve_out.wait(pe, ("Lrb", u, p))
                                dve_out.wait(pe, (("U", 1), u, p))
                                for mm in range(3):
                                    h = 2 * (3 * hf + mm) + p
                                    o = ps[:, 3, (2 * mm + p) * HD:(2 * mm + p + 1) * HD]
                                    pe.matmul(o, M0[:, p, mm], Vt[:, h * HD:(h + 1) * HD], start=True, stop=False)
                                    ins = pe.matmul(o, M1[:, p, mm], U[:, p, mm], start=False, stop=True)
                            pe_out.raised(ins, ("O", u))
                        dve_out.wait(pe, ("normal", T))
                        two = ps[:, 0:2, :].rearrange("p b n -> p (b n)")
                        for m in range(MT6):
                            ins = pe.transpose(two[:, m * P:(m + 1) * P], O[:, m], ident[:])
                        pe_out.raised(ins, ("nt", T))
                    for m in range(MT6):
                        ins = pe.matmul(ps[:, 4 + m // 2, (m % 2) * SEQ:(m % 2 + 1) * SEQ], g_up[:, m * P:(m + 1) * P],
                                        lowg, start=True, stop=True)
                    pe_out.raised(ins, "G")

                @block.scalar
                def _(act):
                    for T in range(NT):
                        for i in range(2):
                            pe_out.wait(act, ("tr", T, i))
                            two = ps[:, 2 * i:2 * i + 2, :].rearrange("p b n -> p (b n)")
                            act_out.raised(act.activation(tok[i], two[:, 0:C], ACT.Copy), ("tok", T, i))
                        for hf in range(2):
                            u = (T, hf)
                            for p in range(2):
                                pe_out.wait(act, ("LbT", u, p))
                                if units.index(u):
                                    prev = units[units.index(u) - 1]
                                    pool_out.wait(act, (("M", 5), prev, p))
                                act_out.raised(act.activation(LT[:, p], bank(p), ACT.Copy), ("LT", u, p))
                            for p in range(2):
                                pe_out.wait(act, ("LkV", u, p))
                                act_out.raised(act.activation(LkV[:, p], bank(6 + p, 3 * HD), ACT.Copy), ("LkV", u, p))
                            for l in LV:
                                for p in range(2):
                                    pe_out.wait(act, (("Z", l), u, p))
                                    act_out.raised(act.activation(Z[:, p], bank(p), ACT.Copy), (("Z", l), u, p))
                            for p in range(2):
                                r = slice(p * HD, p * HD + HD)
                                pe_out.wait(act, ("A1", u, 1) if p == 0 else ("A1", u, p))
                                act_out.raised(act.activation(A1[r], bank(p)[r], ACT.Copy), ("A1", u, p))
                                pe_out.wait(act, ("U0", u, p))
                                act_out.raised(act.activation(U[:, p], ps[:, 6 + p, 192:384].rearrange(
                                    "p (m t) -> p m t", m=3), ACT.Copy), ("U0", u, p))
                            for c in range(2):
                                rc = slice(c * CHUNK, (c + 1) * CHUNK)
                                if not first_chunk(T, c):
                                    for p in range(2):
                                        pe_out.wait(act, (("RS", c), u, p))
                                        if hf == 0:
                                            if T:
                                                act_out.wait(act, ("ln", T - 1))
                                            else:
                                                dve_out.wait(act, "zero")
                                        act_out.raised(act.activation(O[rc, 3 * hf:3 * hf + 3, p],
                                                                      bank(p, 3 * HD)[rc], ACT.Copy),
                                                       (("RS", c), u, p))
                        dve_out.wait(act, ("cen", T))
                        act_out.raised(act.activation(M0.rearrange("p a b c -> p (a b c)"),
                                                      O.rearrange("p m a d -> p (m a d)"), ACT.Square), ("sq", T))
                        dve_out.wait(act, ("var", T))
                        act_out.raised(act.activation(hs[2], hs[1], ACT.Sqrt, bias=eps[:, 2:3], scale=1.0 / HD),
                                       ("std", T))
                        pe_out.wait(act, ("nt", T))
                        two = ps[:, 0:2, :].rearrange("p b n -> p (b n)")
                        for m in range(MT6):
                            ins = act.activation(V[:, m, T * P:(T + 1) * P], two[:, m * P:(m + 1) * P], ACT.Identity,
                                                 bias=col("lnx_b", m), scale=col("lnx_g", m))
                        act_out.raised(ins, ("ln", T))
                    dve_out.wait(act, "yg")
                    act_out.raised(act.activation(actT[:, 0, 0:MT6], V, ACT.Copy), "hi")

                @block.gpsimd
                def _(pool):
                    for T, hf in units:
                        u = (T, hf)
                        for p in range(2):
                            act_out.wait(pool, ("LT", u, p))
                            if units.index(u):
                                pe_out.wait(pool, ("U0", units[units.index(u) - 1], p))
                            pool_out.raised(pool.tensor_tensor(DT[:, p], LT[:, p], bmask(level_mask[0]), ALU.mult),
                                            ("DT1", u, p))
                            pool_out.wait(pool, ("DT1", u, p))
                            pool_out.raised(pool.tensor_tensor(DT[:, p], DT[:, p], bmask(ident[:]), ALU.add),
                                            (("DT", 0), u, p))
                        for l in LV:
                            for p in range(2):
                                if l > 2:
                                    pe_out.wait(pool, (("Z", l - 2), u, p))
                                elif units.index(u):
                                    pe_out.wait(pool, ("O", units[units.index(u) - 1]))
                                    if hf == 0:
                                        dve_out.wait(pool, ("var", T - 1))
                                pool_out.raised(pool.tensor_tensor(M[l % 2][:, p], LT[:, p], bmask(level_mask[l]),
                                                                   ALU.mult), (("M", l), u, p))

                @block.vector
                def _(dve):
                    dve_out.raised(dve.memset(O[0:CHUNK], 0.0), "zero")
                    for T in range(NT):
                        for i in range(2, 4):
                            pe_out.wait(dve, ("tr", T, i))
                            two = ps[:, 2 * i:2 * i + 2, :].rearrange("p b n -> p (b n)")
                            dve_out.raised(dve.tensor_copy(tok[i], two[:, 0:C]), ("tok", T, i))
                        for hf in range(2):
                            u = (T, hf)
                            for p in range(2):
                                pe_out.wait(dve, ("Lb", u, p))
                                dve_out.raised(dve.tensor_tensor(Dm[:, p], bank(2 + p), bmask(pair_mask), ALU.mult),
                                               ("D1", u, p))
                                dve_out.wait(dve, ("D1", u, p))
                                dve_out.raised(dve.tensor_tensor(Dm[:, p], Dm[:, p], bmask(ident[:]), ALU.add),
                                               (("D", 0), u, p))
                                pe_out.wait(dve, ("LkT", u, p))
                                if units.index(u) and p == 0:
                                    prev = units[units.index(u) - 1]
                                    pe_out.wait(dve, ("O", prev))
                                dve_out.raised(dve.tensor_tensor(Z[:, p], bank(4 + p), bmask(below), ALU.mult),
                                               ("LkT", u, p))
                            for l in LV:
                                for p in range(2):
                                    if l < 5:
                                        pe_out.wait(dve, (("dD", l), u, p))
                                        dve_out.raised(dve.tensor_tensor(Dm[:, p], Dm[:, p], bank(2 + p), ALU.add),
                                                       (("D", l), u, p))
                                    pe_out.wait(dve, (("dDT", l), u, p))
                                    dve_out.raised(dve.tensor_tensor(DT[:, p], DT[:, p], bank(4 + p), ALU.add),
                                                   (("DT", l), u, p))
                            for p in range(2):
                                for name, b, dst in (("Lrk", 2, M0), ("Lrb", 4, M1)):
                                    pe_out.wait(dve, (name, u, p))
                                    dve_out.raised(dve.tensor_tensor(dst[:, p], bank(b + p), bmask(upto), ALU.mult),
                                                   (name, u, p))
                            Sh = S[:, 3 * hf:3 * hf + 3]
                            for c in range(2):
                                rc = slice(c * CHUNK, (c + 1) * CHUNK)
                                if not first_chunk(T, c):
                                    for p in range(2):
                                        pe_out.wait(dve, (("U", c), u, p))
                                        act_out.wait(dve, ("U0", u, p))
                                        dve_out.raised(dve.tensor_tensor(U[rc, p], U[rc, p], bank(6 + p, 3 * HD)[rc],
                                                                         ALU.add), (("U", c), u, p))
                                if not last_chunk(T, c):
                                    pe_out.wait(dve, (("S", c), u))
                                    w = w_end[:, 3 * hf:3 * hf + 3, 2 * T + c:2 * T + c + 1].to_broadcast([P, 3, HD])
                                    if first_chunk(T, c):
                                        ins = dve.tensor_tensor(Sh, bank(2, 3 * HD), w, ALU.mult)
                                    else:
                                        dve_out.raised(dve.tensor_tensor(Sh, Sh, bank(2, 3 * HD), ALU.add),
                                                       (("S1", c), u))
                                        dve_out.wait(dve, (("S1", c), u))
                                        ins = dve.tensor_tensor(Sh, Sh, w, ALU.mult)
                                    dve_out.raised(ins, (("S", c), u))
                            pe_out.wait(dve, ("O", u))
                            act_out.wait(dve, (("RS", 1), u, 1))
                            Ou = Oh[:, 6 * hf:6 * hf + 6]
                            dve_out.raised(dve.tensor_tensor(Ou, Ou, ps[:, 3, 0:6 * HD].rearrange("p (h d) -> p h d", h=6),
                                                             ALU.add), ("O", u))
                        wide = lambda s: s.unsqueeze(2).to_broadcast([P, NH, HD])
                        dve_out.wait(dve, ("O", (T, 1)))
                        dve_out.raised(dve.tensor_reduce(hs[0], Oh, AX_X, ALU.add), ("sum", T))
                        dve_out.wait(dve, ("sum", T))
                        dve_out.raised(dve.tensor_scalar(hs[0], hs[0], 1.0 / HD, None, ALU.mult), ("mean", T))
                        dve_out.wait(dve, ("mean", T))
                        dve_out.raised(dve.tensor_tensor(Oh, Oh, wide(hs[0]), ALU.subtract), ("cen", T))
                        act_out.wait(dve, ("sq", T))
                        dve_out.raised(dve.tensor_reduce(hs[1], M0.rearrange("p a b c -> p (a b c)").rearrange(
                            "p (h d) -> p h d", h=NH), AX_X, ALU.add), ("var", T))
                        act_out.wait(dve, ("std", T))
                        dve_out.raised(dve.reciprocal(hs[3], hs[2]), ("inv", T))
                        dve_out.wait(dve, ("inv", T))
                        dve_out.raised(dve.tensor_tensor(Oh, Oh, wide(hs[3]), ALU.mult), ("normal", T))
                    act_out.wait(dve, ("ln", NT - 1))
                    dve_out.raised(dve.tensor_tensor(V, V, BON, ALU.add), "y")
                    pe_out.wait(dve, "G")
                    dve_out.wait(dve, "y")
                    dve_out.raised(dve.tensor_tensor(V, V, ps[:, 4:7, :].rearrange("p b (m t) -> p (b m) t", m=2),
                                                     ALU.mult), "yg")
                    act_out.wait(dve, "hi")
                    dve_steps.step(dve, dve.tensor_tensor(actT[:, 1, 0:MT6], V, actT[:, 0, 0:MT6].bitcast(F32),
                                                          ALU.subtract))

        def stick_stages():
            W = SEQ + P
            QT, KT, Vt, mqT, sg, kp, later, attT = carve((MT6, SEQ), (MT6, SEQ), (NT, C), (2, SEQ),
                                                         (2, 2, W), (2, 2, W), (2, 2, W), (2, 2, W))
            mem_at = (2 * MT6 + 2) * SEQ + NT * C
            before, not_before = gate_m[:, 0:P], gate_m[:, P:2 * P]
            ones = gate_m[:, 2 * P:2 * P + SEQ]
            g0 = sec["sb_in"]
            act_at = [act_steps.n + 1 + c for c in range(10)]
            with nc.Block() as block:
                @block.sync
                def _(sp):
                    for g in range(g0 + 2, g0 + 10 + 2):
                        ring_a.load(sp, g)

                @block.gpsimd
                def _(pool):
                    pool_steps.mark(pool.memset(ones, 1.0))
                    pool_steps.mark(pool.memset(before, 1.0))
                    pool_steps.step(pool, pool.memset(not_before, 1.0))
                    pool_steps.step(pool, pool.affine_select(out=before, in_=before, compare_op=ALU.is_gt, fill=0.0,
                                                             base=0, pattern=[[-1, P]], channel_multiplier=1))
                    pool_steps.step(pool, pool.affine_select(out=not_before, in_=not_before, compare_op=ALU.is_ge,
                                                             fill=0.0, base=0, pattern=[[1, P]], channel_multiplier=-1))

                @block.tensor
                def _(pe):
                    for c in range(10):
                        g = g0 + c
                        ring_a.wait_split(pe, g)
                        if c >= 8:
                            act_steps.upto(pe, act_at[c - 8])
                        for n in range(2):
                            for k in range(KD):
                                out_ = ps[:, c % 8, n * SEQ:(n + 1) * SEQ]
                                if 6 <= c < 9:
                                    w = [ring_a.part(g, s, k * 256, k * 256 + 256) for s in range(2)]
                                    ins = mm3(pe, out_, [actT[:, s, k, n * P:(n + 1) * P] for s in range(2)], w,
                                              k == 0, k == KD - 1)
                                else:
                                    w = [ring_a.part(g, s, k * 256 + n * P, k * 256 + n * P + P) for s in range(2)]
                                    ins = mm3(pe, out_, w, [actT[:, s, k] for s in range(2)], k == 0, k == KD - 1)
                        ins.then_inc(ring_a.used, 1)

                @block.scalar
                def _(act):
                    for c in range(11):
                        if c < 10:
                            ring_a.split_hi(act, g0 + c)
                        if c >= 1:
                            i = c - 1
                            ring_a.wait_used(act, g0 + i)
                            src = ps[:, i % 8, :].rearrange("p (n t) -> p n t", n=2)
                            scale = HD ** -0.5 if i < 3 or i == 9 else 1.0
                            dst = (QT[:, 2 * i:2 * i + 2] if i < 3 else KT[:, 2 * i - 6:2 * i - 4] if i < 6 else
                                   Vt[:, :, (i - 6) * 256:(i - 5) * 256] if i < 9 else mqT)
                            assert act_steps.mark(act.activation(dst, src, ACT.Copy, scale=scale)) == act_at[i]

                @block.vector
                def _(dve):
                    for c in range(10):
                        ring_a.split_lo(dve, g0 + c)

            memory_attention(mqT, arena[:, mem_at:mem_at + 2048].rearrange("p (a b) -> p a b", a=8),
                             arena[:, mem_at + 2048:mem_at + 4096].rearrange("p (a b) -> p a b", a=8))

            pe_out.events([("scores", 0)] + [e for m in range(MT6) for e in
                                             ([("scores", m + 1)] if m + 1 < MT6 else []) + [("attT", m), ("out", m)]])
            act_out.events([("sig", 0)] + [e for m in range(MT6) for e in
                                           ([("sig", m + 1)] if m + 1 < MT6 else []) + [("attT", m), ("hi", m)]])
            dve_out.events(["last"] + [e for m in range(MT6) for e in
                                       [("keep", m), ("later", m), ("att", m)] + ([("lo", m - 1)] if m else [])]
                           + [("lo", MT6 - 1)])
            pool_out.events([("sg", m) for m in range(MT6)])
            with nc.Block() as block:
                @block.tensor
                def _(pe):
                    def scores(m):
                        if m >= 2:
                            dve_out.wait(pe, ("lo", m - 2))
                        for p in range(2):
                            r = slice(p * HD, p * HD + HD)
                            b = ps[:, 2 * (m % 2) + p, :]
                            pe.matmul(b[:, 0:SEQ], QT[r, m, P:SEQ], KT[r, m, :], start=True, stop=True)
                            ins = pe.matmul(b[:, SEQ:W], QT[r, m, 0:P], KT[r, m, 0:P], start=True, stop=True)
                        pe_out.raised(ins, ("scores", m))

                    scores(0)
                    for m in range(MT6):
                        if m + 1 < MT6:
                            scores(m + 1)
                        dve_out.wait(pe, ("att", m))
                        if m >= 2:
                            act_out.wait(pe, ("attT", m - 2))
                        for p in range(2):
                            for i in range(3):
                                ins = pe.transpose(ps[:, 4 + 2 * (m % 2) + p, i * P:(i + 1) * P],
                                                   later[:, m % 2, p, i * P:(i + 1) * P], ident[:])
                        pe_out.raised(ins, ("attT", m))
                        act_out.wait(pe, ("attT", m))
                        for p in range(2):
                            r, h = slice(p * HD, p * HD + HD), 2 * m + p
                            v = [Vt[:, t, h * HD:(h + 1) * HD] for t in range(NT)]
                            a = attT[:, m % 2, p]
                            pe.matmul(ps[r, 2 * (m % 2), W:512], v[0], a[:, SEQ:W], start=True, stop=True)
                            pe.matmul(ps[r, 2 * (m % 2) + 1, W:512], v[0], a[:, 0:P], start=True, stop=False)
                            ins = pe.matmul(ps[r, 2 * (m % 2) + 1, W:512], v[1], a[:, P:SEQ], start=False, stop=True)
                        pe_out.raised(ins, ("out", m))

                @block.scalar
                def _(act):
                    def sigmoids(m):
                        b = 2 * (m % 2)
                        pe_out.wait(act, ("scores", m))
                        if m >= 2:
                            dve_out.wait(act, ("att", m - 2))
                        act.activation(kp[:, m % 2], ps[:, b:b + 2, 0:W], ACT.Sigmoid, scale=-1.0)
                        act_out.raised(act.activation(sg[:, m % 2], ps[:, b:b + 2, 0:W], ACT.Sigmoid), ("sig", m))

                    sigmoids(0)
                    for m in range(MT6):
                        if m + 1 < MT6:
                            sigmoids(m + 1)
                        pe_out.wait(act, ("attT", m))
                        b = 4 + 2 * (m % 2)
                        act_out.raised(act.activation(attT[:, m % 2], ps[:, b:b + 2, 0:W], ACT.Copy), ("attT", m))
                        pe_out.wait(act, ("out", m))
                        b = 2 * (m % 2)
                        act_out.raised(act.activation(actT[:, 0, m].rearrange("p (t n) -> p t n", t=NT),
                                                      ps[:, b:b + 2, W:512], ACT.Copy), ("hi", m))

                @block.gpsimd
                def _(pool):
                    for m in range(MT6):
                        act_out.wait(pool, ("sig", m))
                        diag = sg[:, m % 2, :, P:W]
                        for p in range(2):
                            d = diag[:, p].rearrange("p (a s) -> p a s", a=2)
                            ins = pool.tensor_tensor(d, d, before.unsqueeze(1).to_broadcast([P, 2, P]), ALU.mult)
                        pool_out.raised(ins, ("sg", m))

                @block.vector
                def _(dve):
                    dve_out.raised(dve.memset(later[:, :, :, SEQ - 1:W:P], 1.0), "last")
                    dve_out.wait(dve, "last")

                    def lo(m):
                        act_out.wait(dve, ("hi", m))
                        b = 2 * (m % 2)
                        two = lambda ap: ap.rearrange("p (t n) -> p t n", t=NT)
                        dve_out.raised(dve.tensor_tensor(two(actT[:, 1, m]), ps[:, b:b + 2, W:512],
                                                         two(actT[:, 0, m].bitcast(F32)), ALU.subtract), ("lo", m))

                    for m in range(MT6):
                        q = m % 2
                        act_out.wait(dve, ("sig", m))
                        for p in range(2):
                            d = kp[:, q, p, P:W].rearrange("p (a s) -> p a s", a=2)
                            ins = dve.tensor_tensor(d, d, not_before.unsqueeze(1).to_broadcast([P, 2, P]), ALU.max)
                        dve_out.raised(ins, ("keep", m))
                        dve_out.wait(dve, ("keep", m))
                        if m >= 2:
                            pe_out.wait(dve, ("attT", m - 2))
                            dve_steps.step(dve, dve.memset(later[:, q, :, SEQ - 1:W:P], 1.0))
                        for p in range(2):
                            for a, b in ((0, SEQ), (SEQ, W)):
                                ins = dve.tensor_tensor_scan(later[:, q, p, a:b - 1][:, ::-1],
                                                             kp[:, q, p, a + 1:b][:, ::-1], ones[:, 0:b - a - 1],
                                                             1.0, ALU.mult, ALU.mult)
                        dve_out.raised(ins, ("later", m))
                        dve_out.wait(dve, ("later", m))
                        pool_out.wait(dve, ("sg", m))
                        dve_out.raised(dve.tensor_tensor(later[:, q], later[:, q], sg[:, q], ALU.mult), ("att", m))
                        if m:
                            lo(m - 1)
                    lo(MT6 - 1)

        def norm_rows(i, n):
            return A["ln_g_2"][i, n], A["ln_b_2"][i, n]

        ffn_stage("ffn", True, None, True, sec["ffn1", 0], sec[("ffn1", 0), "B"])
        ffn_stage(("ffn1", 0), False, norm_rows(0, 0), True, sec["rwkv_in"], sec[("ffn2", 0), "B"])
        rwkv_stages()
        output_stage(0)
        ffn_stage(("ffn2", 0), False, norm_rows(0, 2), True, sec["ffn1", 1], sec[("ffn1", 1), "B"])
        ffn_stage(("ffn1", 1), False, norm_rows(1, 0), True, sec["sb_in"], sec[("ffn2", 1), "B"])
        stick_stages()
        output_stage(1)
        ffn_stage(("ffn2", 1), False, norm_rows(1, 2), False, len(chunks_a), len(chunks_b))

        with nc.Block() as block:
            @block.sync
            def _(sp):
                sp.dma_start(out[0].rearrange("(t p) d -> p t d", p=P), x_tok[:]).then_inc(rows_loaded, 16)
                sp.wait_ge(rows_loaded, rows_count[0] + 16)


INPUTS = ["x", "c", "mod_w", "mod_b", "norm_pre_mix", "norm_post_mix", "norm_pre_ffn", "norm_post_ffn", "a_pw1_w",
          "a_pw1_b", "a_dw_w", "a_dw_b", "a_ln_g", "a_ln_b", "a_pw2_w", "a_pw2_b", "f_up_w", "f_dw_w", "f_dw_b",
          "f_down_w", "mem_2", "ffn1_w_gate_2", "ffn1_w_up_2", "ffn1_w_down_2", "ffn2_w_gate_2", "ffn2_w_up_2",
          "ffn2_w_down_2", "ln_g_2", "ln_b_2", "w_out_2", "w_mem_kv_2", "rwkv_w_in_2", "rwkv_mu_2", "rwkv_w0_2",
          "rwkv_w_up_2", "rwkv_a0_2", "rwkv_a_up_2", "rwkv_g_up_2", "rwkv_k_k_2", "rwkv_k_a_2", "rwkv_r_k_2",
          "rwkv_lnx_g_2", "rwkv_lnx_b_2", "sb_w_in_2"]


def kernel(**inputs):
    import numpy as np
    import concourse.bacc as bacc
    from concourse.bass_utils import run_bass_kernel_spmd

    nc = bacc.Bacc("TRN2", target_bir_lowering=False, num_devices=1)
    arrays, aps = {}, {}
    for name in INPUTS:
        a = np.ascontiguousarray(inputs[name])
        arrays[f"in_{name}"] = a
        aps[name] = nc.dram_tensor(f"in_{name}", a.shape, mybir.dt.from_np(a.dtype), kind="ExternalInput").ap()
    out = nc.dram_tensor("out_x", (1, SEQ, D), F32, kind="ExternalOutput").ap()
    build_program(nc, aps, out)
    return run_bass_kernel_spmd(nc, [arrays], core_ids=[0]).results[0]["out_x"]
```

```python
import math
from contextlib import ExitStack

import concourse.bass as bass
from concourse import mybir

F32 = mybir.dt.float32
F32R = mybir.dt.float32r
ALU = mybir.AluOpType
ACT = mybir.ActivationFunctionType
AX_X = mybir.AxisListType.X

P = 128
SEQ, D, DFF = 256, 1024, 2816
NT = SEQ // P
KD = D // P
NF = DFF // P
CONVW, FCONVW = 31, 3
PAD = CONVW - 1
C = 768
MT6 = C // P
HD = 64
NH, NMH = C // HD, 4
NMEM = 256
CHUNK = 64
ALPHA = 4.0 ** 0.25
DECAY = math.exp(-0.5)
RMS_EPS, LN_EPS, LNX_EPS = 1e-6, 1e-5, 64e-5
MOD_COLS = 256
MOD_SLOTS = 6
MOD_LATE = 4
ACH, BCH = 2048, 1024


class Signal:

    def __init__(self, sem):
        self.sem, self.total, self.count, self.todo = sem, 0, {}, []

    def events(self, names):
        assert not self.todo, self.todo
        self.todo = list(names)
        self.count = {n: self.total + i + 1 for i, n in enumerate(self.todo)}
        self.total += len(self.todo)
        assert len(self.count) == len(self.todo)

    def up(self, name):
        assert self.todo and self.todo[0] == name, (self.todo[:1], name)
        self.todo.pop(0)
        return self.sem

    def at(self, name):
        return self.count[name]


class Steps:

    def __init__(self, sem):
        self.sem, self.n = sem, 0

    def mark(self, ins):
        self.n += 1
        ins.then_inc(self.sem, 1)
        return self.n

    def step(self, eng, ins):
        self.mark(ins)
        eng.wait_ge(self.sem, self.n)


class Ring:

    def __init__(self, raw, parts, sems, chunks):
        self.raw, self.parts, self.chunks = raw, parts, chunks
        self.loaded, self.hi_done, self.lo_done, self.used = sems
        self.load_no, loads = [], [0, 0]
        for g, dmas in enumerate(chunks):
            loads[g % 2] += 16 * len(dmas)
            self.load_no.append(loads[g % 2])

    def load(self, sp, g):
        if g >= len(self.chunks):
            return
        if g >= 2:
            sp.wait_ge(self.lo_done, g - 1)
        for cols, view, src in self.chunks[g]:
            dst = self.raw[:, g % 2, cols[0]:cols[1]]
            sp.dma_start(dst.rearrange(view[0], **view[1]) if view else dst, src).then_inc(self.loaded[g % 2], 16)

    def split_hi(self, act, g):
        act.wait_ge(self.loaded[g % 2], self.load_no[g])
        if g >= 2:
            act.wait_ge(self.used, g - 1)
        act.activation(self.parts[:, g % 2, 0], self.raw[:, g % 2], ACT.Copy).then_inc(self.hi_done, 1)

    def split_lo(self, dve, g):
        dve.wait_ge(self.hi_done, g + 1)
        dve.tensor_tensor(self.parts[:, g % 2, 1], self.raw[:, g % 2], self.parts[:, g % 2, 0].bitcast(F32),
                          ALU.subtract).then_inc(self.lo_done, 1)

    def wait_split(self, pe, g):
        pe.wait_ge(self.lo_done, g + 1)

    def wait_used(self, eng, g):
        eng.wait_ge(self.used, g + 1)

    def part(self, g, which, lo, hi):
        return self.parts[:, g % 2, which, lo:hi]


def mm3(pe, out, lhs, rhs, start, stop):
    pe.matmul(out, lhs[0], rhs[0], start=start, stop=False)
    pe.matmul(out, lhs[0], rhs[1], start=False, stop=False)
    return pe.matmul(out, lhs[1], rhs[0], start=False, stop=stop)


def param_columns(A):
    def rows(ap):
        return ap.rearrange("(r p) -> r p", p=P)

    parts = [("c", rows(A["c"][0])), ("norm_pre_mix", rows(A["norm_pre_mix"][0])),
             ("norm_pre_ffn", rows(A["norm_pre_ffn"][0])), ("a_pw1_b", rows(A["a_pw1_b"][0])),
             ("a_dw_b", rows(A["a_dw_b"][0])), ("a_ln_g", rows(A["a_ln_g"][0])), ("a_ln_b", rows(A["a_ln_b"][0])),
             ("mod_sh_m", rows(A["mod_b"][0, 0:D])), ("mod_sc_m", rows(A["mod_b"][0, D:2 * D])),
             ("mod_sh_f", rows(A["mod_b"][0, 3 * D:4 * D])), ("mod_sc_f", rows(A["mod_b"][0, 4 * D:5 * D]))]
    parts += [("a_dw_w", A["a_dw_w"][0].rearrange("k (r p) -> (k r) p", p=P))]
    parts += [("f_dw_w", A["f_dw_w"][0].rearrange("k (r p) -> (k r) p", p=P)), ("f_dw_b", rows(A["f_dw_b"][0])),
              ("mu", rows(A["rwkv_mu_2"][0]))]
    for n in ("w0", "a0", "k_k", "k_a"):
        parts.append((n, rows(A[f"rwkv_{n}_2"][0])))
    parts.append(("r_k", A["rwkv_r_k_2"][0].rearrange("(a b) d -> a (b d)", b=2)))
    parts += [("lnx_g", rows(A["rwkv_lnx_g_2"][0])), ("lnx_b", rows(A["rwkv_lnx_b_2"][0]))]
    at, first, loads = 0, {}, []
    for name, view in parts:
        first[name] = at
        n, done = view.shape[0], 0
        while done < n:
            m = min(n - done, P - at % P)
            loads.append((at // P, at % P, m, view[done:done + m, :]))
            done, at = done + m, at + m
    return first, loads, at


def weight_chunks(A):
    ring_a, ring_b, first = [], [], {}

    def up(name, w, cols):
        first[name] = len(ring_a)
        v = w.rearrange("(k p) n -> p k n", p=P)
        for ranges in cols:
            at, dmas = 0, []
            for a, b in ranges:
                dmas.append(((at, at + KD * (b - a)), ("p (k n) -> p k n", {"k": KD}), v[:, :, a:b]))
                at += KD * (b - a)
            ring_a.append(dmas)

    def rows2(name, w):
        first[name] = len(ring_a)
        for c in range(KD // 2):
            src = w[2 * c * P:(2 * c + 2) * P, :].rearrange("(k p) n -> p k n", p=P)
            ring_a.append([((0, ACH), ("p (k n) -> p k n", {"k": 2}), src)])

    def ffn(name, gate, up_w, down):
        first[name] = len(ring_a)
        first[name, "B"] = len(ring_b)
        g, u = (w.rearrange("(k p) n -> p k n", p=P) for w in (gate, up_w))
        for i in range(NF):
            ring_a.append([((0, BCH), ("p (k n) -> p k n", {"k": KD}), g[:, :, i * P:(i + 1) * P]),
                           ((BCH, ACH), ("p (k n) -> p k n", {"k": KD}), u[:, :, i * P:(i + 1) * P])])
            ring_b.append([((0, BCH), None, down[i * P:(i + 1) * P, :])])

    wide = lambda n: [[(256 * c, 256 * c + 256)] for c in range(n)]
    up("mem_kv", A["w_mem_kv_2"], wide(2))
    up("pw1", A["a_pw1_w"][0], [[(j * P, j * P + P), (D + j * P, D + j * P + P)] for j in range(KD)])
    rows2("pw2", A["a_pw2_w"][0])
    ffn("ffn", A["f_up_w"][0][:, 0:DFF], A["f_up_w"][0][:, DFF:2 * DFF], A["f_down_w"][0])
    for i in range(2):
        ffn(("ffn1", i), A["ffn1_w_gate_2"][i], A["ffn1_w_up_2"][i], A["ffn1_w_down_2"][i])
        if i == 0:
            w = A["rwkv_w_in_2"][0]
            up("rwkv_in", w, wide(10) + [[(2560, 2688)], [(2688, 2816)]])
        else:
            up("sb_in", A["sb_w_in_2"][0], wide(10))
        rows2(("w_out", i), A["w_out_2"][i])
        ffn(("ffn2", i), A["ffn2_w_gate_2"][i], A["ffn2_w_up_2"][i], A["ffn2_w_down_2"][i])
    return ring_a, ring_b, first


def build_program(nc, A, out):
    with ExitStack() as ctx:
        def sb(name, shape, dt=F32):
            return ctx.enter_context(nc.sbuf_tensor(name, shape, dt))

        def sem(name):
            return ctx.enter_context(nc.semaphore(name))

        def signal(name):
            return Signal(sem(name))

        a_raw, a_parts = sb("a_raw", [P, 2, ACH]), sb("a_parts", [P, 2, 2, ACH], F32R)
        b_raw, b_parts = sb("b_raw", [P, 2, BCH]), sb("b_parts", [P, 2, 2, BCH], F32R)
        x_tok = sb("x_tok", [P, NT, D])
        actT = sb("actT", [P, 2, KD, SEQ], F32R)
        hid = sb("hid", [P, 2, 2, SEQ], F32R)
        gate_m, gate_f = sb("gate_m", [P, D]), sb("gate_f", [P, D])
        rows = sb("rows", [P, 2, D])
        memkT = sb("memkT", [P, 2, NMEM])
        memv = sb("memv", [P, 2, 256])
        ident = sb("ident", [P, P])
        ones_mean = sb("ones_mean", [P, P])
        head_ones = sb("head_ones", [P, P])
        mod_cols = sb("mod_cols", [P, 4, KD])
        eps = sb("eps", [P, 3])
        stats = sb("stats", [P, NT, 16])
        small = sb("small", [P, 112])
        first_col, param_loads, n_params = param_columns(A)
        par = sb("par", [P, n_params])
        arena_words = nc.sbuf_bytes_remaining // 4 - 16
        arena = sb("arena", [P, arena_words])
        ps = ctx.enter_context(nc.psum_tensor("ps", [P, 8, 512], F32))

        def carve(*shapes, limit=arena_words):
            at, got = 0, []
            for shape in shapes:
                n = math.prod(shape)
                ap = arena[:, at:at + n]
                if len(shape) == 2:
                    ap = ap.rearrange("p (a b) -> p a b", a=shape[0])
                elif len(shape) == 3:
                    ap = ap.rearrange("p (a b c) -> p a b c", a=shape[0], b=shape[1])
                got.append(ap)
                at += n
            assert at <= limit, (at, limit)
            return got

        def col(name, i=0):
            return par[:, first_col[name] + i:first_col[name] + i + 1]

        def cols(name, n):
            return par[:, first_col[name]:first_col[name] + n]

        turned = ps[:, 4:8, :].rearrange("p b (k t) -> p (b k) t", k=2)
        turned_tok = ps[:, 4:8, :].rearrange("p (t b) (k n) -> p t (b k) n", t=NT, k=4)
        acc = [ps[:, 2 * t:2 * t + 2, :].rearrange("p b n -> p (b n)") for t in range(NT)]

        chunks_a, chunks_b, sec = weight_chunks(A)
        ring_a = Ring(a_raw, a_parts, ([sem("a_loaded0"), sem("a_loaded1")], sem("a_hi_done"), sem("a_lo_done"),
                                       sem("a_used")), chunks_a)
        ring_b = Ring(b_raw, b_parts, ([sem("b_loaded0"), sem("b_loaded1")], sem("b_hi_done"), sem("b_lo_done"),
                                       sem("b_used")), chunks_b)
        dve_steps, act_steps, pool_steps = Steps(sem("dve_steps")), Steps(sem("act_steps")), Steps(sem("pool_steps"))
        params_loaded = sem("params_loaded")
        rows_loaded = sem("rows_loaded")
        rows_count = [0]
        turned_done = signal("turned_done")
        turned_read = signal("turned_read")
        stat_ready, stat_root = signal("stat_ready"), signal("stat_root")
        input_hi, input_lo = signal("input_hi"), signal("input_lo")
        acc_ready = signal("acc_ready")
        pe_out, pe_in = signal("pe_out"), signal("pe_in")
        act_out, dve_out = signal("act_out"), signal("dve_out")
        pool_out = signal("pool_out")

        def load_row(eng, slot, vec):
            eng.dma_start(rows[:, slot], vec.partition_broadcast(P)).then_inc(rows_loaded, 16)


        def loads(sp, name, n_a, n_b=0):
            for g in range(sec[name] + 2, sec[name] + 2 + n_a):
                ring_a.load(sp, g)

        def rms_scale(act, dve, t, scratch):
            if act is not None:
                act_steps.step(act, act.activation(scratch[:, t], x_tok[:, t], ACT.Square,
                                                   accum_out=stats[:, t, 0:1]))
                act.activation(stats[:, t, 1:2], stats[:, t, 0:1], ACT.Sqrt, bias=eps[:, 0:1],
                               scale=1.0 / D).then_inc(act_out.up(("root", t)), 1)
            if dve is not None:
                dve.wait_ge(act_out.sem, act_out.at(("root", t)))
                dve_steps.step(dve, dve.reciprocal(stats[:, t, 2:3], stats[:, t, 1:2]))
                dve.tensor_scalar(scratch[:, t], x_tok[:, t], stats[:, t, 2:3], None, ALU.mult)\
                    .then_inc(dve_out.up(("xn", t)), 1)

        def turn(pe, src, t, k0=0, k1=KD):
            for k in range(k0, k1):
                ins = pe.transpose(turned[:, k, t * P:(t + 1) * P], src[:, t, k * P:(k + 1) * P], ident[:])
            ins.then_inc(turned_done.up(t), 1)

        def affine(act, hT, shift):
            for h in range(2):
                for k in range(4 * h, 4 * h + 4):
                    ins = act.activation(hT[:, k], turned[:, k], ACT.Identity, bias=mod_cols[:, shift, k:k + 1],
                                         scale=mod_cols[:, shift + 1, k:k + 1])
                ins.then_inc(input_hi.up(h), 1)

        def split_affine(dve, hT):
            for h in range(2):
                dve.wait_ge(input_hi.sem, input_hi.at(h))
                half = slice(4 * h, 4 * h + 4)
                dve_steps.step(dve, dve.tensor_copy(actT[:, 0, half], hT[:, half]))
                dve.tensor_tensor(actT[:, 1, half], hT[:, half], actT[:, 0, half].bitcast(F32), ALU.subtract)\
                    .then_inc(input_lo.up(h), 1)

        X_PARTS = [(0, 0, KD), (1, 0, KD // 2), (1, KD // 2, KD)]

        def turn_x_pe(pe):
            for part in X_PARTS:
                t, k0, k1 = part
                pe.wait_ge(dve_out.sem, dve_out.at(("x", part)))
                for k in range(k0, k1):
                    ins = pe.transpose(turned_tok[:, t, k], x_tok[:, t, k * P:(k + 1) * P], ident[:])
                ins.then_inc(turned_done.up(part), 1)

        def first_hi(act):
            act.wait_ge(turned_done.sem, turned_done.at(X_PARTS[0]))
            act.activation(actT[:, 0, :, 0:P], turned_tok[:, 0], ACT.Copy).then_inc(act_out.up("hi"), 1)

        def first_lo(dve):
            dve.wait_ge(act_out.sem, act_out.at("hi"))
            dve_steps.step(dve, dve.tensor_tensor(actT[:, 1, :, 0:P], turned_tok[:, 0],
                                                  actT[:, 0, :, 0:P].bitcast(F32), ALU.subtract))

        def take_x():
            turned_at = [turned_done.at(part) for part in X_PARTS[1:]]

            def on_act(act):
                for h in range(2):
                    act.wait_ge(turned_done.sem, turned_at[h])
                    act.activation(actT[:, 0, 4 * h:4 * h + 4, P:SEQ], turned_tok[:, 1, 4 * h:4 * h + 4],
                                   ACT.Copy).then_inc(input_hi.up(h), 1)

            def on_dve(dve):
                for h in range(2):
                    dve.wait_ge(input_hi.sem, input_hi.at(h))
                    dve.tensor_tensor(actT[:, 1, 4 * h:4 * h + 4, P:SEQ], turned_tok[:, 1, 4 * h:4 * h + 4],
                                      actT[:, 0, 4 * h:4 * h + 4, P:SEQ].bitcast(F32),
                                      ALU.subtract).then_inc(input_lo.up(h), 1)
            return on_act, on_dve

        def wait_input(pe, k):
            if k % 4 == 0:
                pe.wait_ge(input_lo.sem, input_lo.at(k // 4))

        def expect_input():
            input_hi.events([0, 1])
            input_lo.events([0, 1])

        def mod_chunk(pe, weights, lhs, out_, n=KD):
            for k in range(n):
                ins = pe.matmul(out_, lhs(k), weights[:, k * MOD_COLS:(k + 1) * MOD_COLS], start=k == 0,
                                stop=k == KD - 1)
            return ins

        def one_row(k):
            return csilu[:, k:k + 1]

        def to_columns(pe, mod_row, h):
            for j in range(KD * h, KD * h + KD):
                ins = pe.matmul(ps[:, 0, j:j + 1], mod_row[0:1, j * P:(j + 1) * P], ones_col[0:1], start=True,
                                stop=True)
            return ins

        def mod_finish(dve, shift, names, norm):
            sh, scl = names
            dve_steps.mark(dve.tensor_tensor(mod_cols[:, shift], ps[:, 0, 0:KD], cols(sh, KD), ALU.add))
            dve_steps.step(dve, dve.tensor_tensor(mod_cols[:, shift + 1], ps[:, 0, KD:2 * KD], cols(scl, KD),
                                                  ALU.add))
            dve.scalar_tensor_tensor(mod_cols[:, shift + 1], mod_cols[:, shift + 1], 1.0,
                                     cols(norm, KD), ALU.add, ALU.mult).then_inc(dve_out.up("mod"), 1)

        slots_at = arena_words - MOD_SLOTS * ACH
        mod_slots = arena[:, slots_at:arena_words].rearrange("p (s n) -> p s n", s=MOD_SLOTS)
        late_slots, late_at = mod_slots[:, MOD_SLOTS - MOD_LATE:], arena_words - MOD_LATE * ACH
        cb, prow, tokmem, scratch = carve((KD, P), (5, P), (NT, D), (NT, D), limit=slots_at)
        csilu, csig = small[:, 0:KD], small[:, KD:2 * KD]
        ones_col = small[:, 50:51]
        mod_row = scratch.rearrange("p t d -> p (t d)")
        n_rows = (n_params + P - 1) // P
        g0 = sec["mem_kv"]
        N_MIX = 2 * D // MOD_COLS
        MOD_PE = 3
        mix_w = [mod_slots[:, c] for c in range(MOD_SLOTS)] + [rows[:].rearrange("p a b -> p (a b)"),
                                                               b_raw[:].rearrange("p a b -> p (a b)")]
        sums = [g[:, c * MOD_COLS:(c + 1) * MOD_COLS] for g in (gate_m, gate_f) for c in range(N_MIX // 2)]
        mix_loaded = [sem(f"mix_loaded{c}") for c in range(N_MIX)]
        x_loaded, mem_loaded = sem("x_loaded"), sem("mem_loaded")
        mod_v = A["mod_w"][0].rearrange("(k p) n -> p k n", p=P)

        def load_mod(eng, dst, c, done):
            eng.dma_start(dst.rearrange("p (k n) -> p k n", k=KD), mod_v[:, :, c * MOD_COLS:(c + 1) * MOD_COLS])\
               .then_inc(done, 16)

        turned_done.events(["mem", 0, 1])
        pe_out.events(["params", "shift", "scale", "columns"])
        act_out.events([("root", 0), ("root", 1), "memT0", "memT1", "csig", "memkT", "memv", "shift", "scale"])
        dve_out.events([("xn", 0), ("xn", 1), "memT", "params", "csilu"] + [("sum", c) for c in range(N_MIX)]
                       + ["mod"])

        with nc.Block() as block:
            @block.sync
            def _(sp):
                sp.dma_start(x_tok[:], A["x"][0].rearrange("(t p) d -> p t d", p=P)).then_inc(x_loaded, 16)
                sp.dma_start(tokmem, A["mem_2"][0].rearrange("(t p) d -> p t d", p=P)).then_inc(mem_loaded, 16)
                ring_a.load(sp, g0)
                ring_a.load(sp, g0 + 1)
                for t, r, m, view in param_loads:
                    sp.dma_start(prow[r:r + m, t, :], view).then_inc(params_loaded, 16)
                for c in range(N_MIX):
                    load_mod(sp, mix_w[c], c, mix_loaded[c])
                for g in range(2, 4):
                    ring_a.load(sp, g0 + g)

            @block.gpsimd
            def _(pool):
                pool_steps.step(pool, pool.memset(ident[:], 0.0))
                pool_steps.step(pool, pool.affine_select(out=ident[:], in_=ident[:], compare_op=ALU.not_equal, fill=1.0,
                                                         base=0, pattern=[[-1, P]], channel_multiplier=1))
                for i, v in enumerate((RMS_EPS, LN_EPS, LNX_EPS)):
                    pool_steps.step(pool, pool.memset(eps[:, i:i + 1], v))
                pool_steps.step(pool, pool.memset(ones_mean[:], 1.0 / D))
                pool_steps.step(pool, pool.memset(ones_col, 1.0))
                pool_steps.step(pool, pool.memset(head_ones[:], 0.0))
                for h in range(2):
                    pool_steps.step(pool, pool.memset(head_ones[h * HD:(h + 1) * HD, h * HD:(h + 1) * HD], 1.0))
            constants = pool_steps.n

            @block.scalar
            def _(act):
                act.wait_ge(pool_steps.sem, constants)
                act.wait_ge(x_loaded, 16)
                rms_scale(act, None, 0, scratch)
                rms_scale(act, None, 1, scratch)
                act.wait_ge(turned_done.sem, turned_done.at("mem"))
                for h in range(2):
                    act.activation(actT[:, 0, 4 * h:4 * h + 4, :], turned[:, 4 * h:4 * h + 4, :],
                                   ACT.Copy).then_inc(act_out.up(f"memT{h}"), 1)
                for g in range(g0, g0 + 2):
                    ring_a.split_hi(act, g)
                act.wait_ge(dve_out.sem, dve_out.at("params"))
                act.activation(csig, cols("c", KD), ACT.Sigmoid).then_inc(act_out.up("csig"), 1)
                ring_a.wait_used(act, g0)
                act.activation(memkT[:], ps[:, 1, :].rearrange("p (n m) -> p n m", n=2), ACT.Copy)\
                    .then_inc(act_out.up("memkT"), 1)
                ring_a.wait_used(act, g0 + 1)
                act.activation(memv[:], ps[:, 2, :].rearrange("p (n m) -> p n m", n=2), ACT.Copy)\
                    .then_inc(act_out.up("memv"), 1)
                ring_a.split_hi(act, sec["pw1"])
                for h, name in enumerate(("shift", "scale")):
                    act.wait_ge(pe_out.sem, pe_out.at(name))
                    act.activation(mod_row[0:1, h * D:(h + 1) * D], acc[h][0:1, :], ACT.Copy)\
                        .then_inc(act_out.up(name), 1)

            @block.tensor
            def _(pe):
                pe.wait_ge(pool_steps.sem, constants)
                pe.wait_ge(mem_loaded, 16)
                for t in range(NT):
                    for k in range(KD):
                        ins = pe.transpose(turned[:, k, t * P:(t + 1) * P], tokmem[:, t, k * P:(k + 1) * P], ident[:])
                ins.then_inc(turned_done.up("mem"), 1)
                pe.wait_ge(dve_out.sem, dve_out.at("memT"))
                ring_a.wait_split(pe, g0)
                for n in range(2):
                    for k in range(KD):
                        w = [ring_a.part(g0, s, k * 256 + n * P, k * 256 + n * P + P) for s in range(2)]
                        ins = mm3(pe, ps[:, 1, n * NMEM:(n + 1) * NMEM], w, [actT[:, s, k, :] for s in range(2)],
                                  k == 0, k == KD - 1)
                ins.then_inc(ring_a.used, 1)
                pe.wait_ge(params_loaded, 16 * len(param_loads))
                for i in range(n_rows):
                    n = min(P, n_params - i * P)
                    ins = pe.transpose(ps[:, 3 * (i // 4), (i % 4) * P:(i % 4) * P + n], prow[0:n, i, :],
                                       ident[0:n, 0:n])
                ins.then_inc(pe_out.up("params"), 1)
                ring_a.wait_split(pe, g0 + 1)
                for t in range(2):
                    for k in range(KD):
                        w = [ring_a.part(g0 + 1, s, k * 256, k * 256 + 256) for s in range(2)]
                        ins = mm3(pe, ps[:, 2, t * 256:(t + 1) * 256],
                                  [actT[:, s, k, t * P:(t + 1) * P] for s in range(2)], w, k == 0, k == KD - 1)
                ins.then_inc(ring_a.used, 1)
                for t in range(NT):
                    pe.wait_ge(dve_out.sem, dve_out.at(("xn", t)))
                    turn(pe, scratch, t)
                pe.wait_ge(dve_out.sem, dve_out.at("csilu"))
                pe.wait_ge(act_out.sem, act_out.at("memv"))
                for c in range(N_MIX):
                    out_ = acc[c // 4][0:1, (c % 4) * MOD_COLS:(c % 4 + 1) * MOD_COLS]
                    pe.wait_ge(mix_loaded[c], 16)
                    mod_chunk(pe, mix_w[c], one_row, out_, MOD_PE)
                    pe.wait_ge(dve_out.sem, dve_out.at(("sum", c)))
                    ins = pe.matmul(out_, ones_col, sums[c], start=False, stop=True)
                    if c % 4 == 3:
                        ins.then_inc(pe_out.up(("shift", "scale")[c // 4]), 1)
                    if c == 5:
                        pe.wait_ge(act_out.sem, act_out.at("shift"))
                        to_columns(pe, mod_row, 0)
                pe.wait_ge(act_out.sem, act_out.at("scale"))
                to_columns(pe, mod_row, 1).then_inc(pe_out.up("columns"), 1)

            @block.vector
            def _(dve):
                rms_scale(None, dve, 0, scratch)
                rms_scale(None, dve, 1, scratch)
                dve.wait_ge(act_out.sem, act_out.at("memT1"))
                dve.tensor_tensor(actT[:, 1], turned, actT[:, 0].bitcast(F32), ALU.subtract)\
                    .then_inc(dve_out.up("memT"), 1)
                for g in range(g0, g0 + 2):
                    ring_a.split_lo(dve, g)
                dve.wait_ge(pe_out.sem, pe_out.at("params"))
                n4 = min(n_params, 4 * P)
                dve.tensor_copy(par[:, 0:n4], ps[:, 0, 0:n4])
                dve.tensor_copy(par[:, n4:n_params], ps[:, 3, 0:n_params - n4]).then_inc(dve_out.up("params"), 1)
                dve.wait_ge(act_out.sem, act_out.at("csig"))
                dve.tensor_tensor(csilu, cols("c", KD), csig, ALU.mult).then_inc(dve_out.up("csilu"), 1)
                dve.wait_ge(dve_out.sem, dve_out.at("csilu"))
                for c in range(N_MIX):
                    dve.wait_ge(mix_loaded[c], 16)
                    for k in range(MOD_PE, KD):
                        w = mix_w[c][:, k * MOD_COLS:(k + 1) * MOD_COLS]
                        if k == MOD_PE:
                            ins = dve.tensor_scalar(sums[c], w, csilu[:, k:k + 1], None, ALU.mult)
                        else:
                            ins = dve.scalar_tensor_tensor(sums[c], w, csilu[:, k:k + 1], sums[c], ALU.mult, ALU.add)
                        if k < KD - 1:
                            dve_steps.step(dve, ins)
                    ins.then_inc(dve_out.up(("sum", c)), 1)
                ring_a.split_lo(dve, sec["pw1"])
                for k in range(KD):
                    dve_steps.step(dve, dve.tensor_copy(cb[:, k, :], csilu[:, k:k + 1].to_broadcast([P, P])))
                dve.wait_ge(pe_out.sem, pe_out.at("columns"))
                mod_finish(dve, 0, ("mod_sh_m", "mod_sc_m"), "norm_pre_mix")

        _, u_pad, conv, sig, prod, csum, mod_row = carve((KD, P), (KD, PAD + SEQ), (KD, SEQ), (2, SEQ), (4, SEQ),
                                                         (2, SEQ), (2 * D,), limit=late_at)
        hT = conv
        g0 = sec["pw1"]
        first_m, first_f, first_g = (i * D // MOD_COLS for i in (2, 3, 5))
        N_GATE = D // MOD_COLS
        late = [*range(first_f, first_f + 2 * N_GATE), *range(first_m, first_m + N_GATE),
                *range(first_g, first_g + N_GATE)]
        late_loaded, late_used = [sem(f"late_loaded{i}") for i in range(MOD_LATE)], signal("late_used")
        late_used.events(range(len(late)))

        def load_late(sp, i):
            if i >= MOD_LATE:
                sp.wait_ge(late_used.sem, late_used.at(i - MOD_LATE))
            load_mod(sp, late_slots[:, i % MOD_LATE], late[i], late_loaded[i % MOD_LATE])

        def late_chunk(pe, i, lhs, out_):
            pe.wait_ge(late_loaded[i % MOD_LATE], 16 * (i // MOD_LATE + 1))
            mod_chunk(pe, late_slots[:, i % MOD_LATE], lhs, out_).then_inc(late_used.up(i), 1)

        AHEAD = 10
        BY_POOL = [0, 2, 4]
        BY_VECTOR = [j for j in range(KD) if j not in BY_POOL]
        pool_taps = [(j, k) for j in BY_POOL for k in range(CONVW)]
        SHARE = 8
        act_plan = []
        for j in range(KD):
            act_plan.append(("sig", j))
            if j > 0:
                n = len(pool_taps) if j == KD - 1 else j * SHARE
                act_plan += [("tap", i) for i in range((j - 1) * SHARE, n)]
        expect_input()
        act_out.events(act_plan + ["shift", "scale"])
        pool_out.events([("tap", i) for i in range(len(pool_taps))])
        pe_out.events(["columns", "mean"])
        dve_out.events(["zero"] + [("u", j) for j in range(KD)] + ["mod", "gate_m"])
        rows_count[0] += 64
        gates_row = rows_count[0]
        conv_done = {}
        MEAN_ORDER = [*BY_POOL, *BY_VECTOR]
        with nc.Block() as block:
            @block.sync
            def _(sp):
                load_row(sp, 0, A["norm_post_mix"][0])
                load_row(sp, 1, A["norm_post_ffn"][0])
                sp.dma_start(gate_m[:], A["mod_b"][0, 2 * D:3 * D].partition_broadcast(P)).then_inc(rows_loaded, 16)
                sp.dma_start(gate_f[:], A["mod_b"][0, 5 * D:6 * D].partition_broadcast(P)).then_inc(rows_loaded, 16)
                for i in range(MOD_LATE):
                    ring_a.load(sp, g0 + 2 + i)
                    load_late(sp, i)
                for g in range(g0 + 2 + MOD_LATE, g0 + KD + 2):
                    ring_a.load(sp, g)
                for i in range(MOD_LATE, len(late)):
                    load_late(sp, i)

            @block.scalar
            def _(act):
                affine(act, hT, 0)
                for what, i in act_plan:
                    if what == "sig":
                        if i + 1 < KD:
                            ring_a.split_hi(act, g0 + i + 1)
                        ring_a.wait_used(act, g0 + i)
                        if i >= 2:
                            act.wait_ge(dve_out.sem, dve_out.at(("u", i - 2)))
                        act.activation(sig[:, i % 2], ps[:, 4 + i % 4, SEQ:2 * SEQ], ACT.Sigmoid,
                                       bias=col("a_pw1_b", KD + i)).then_inc(act_out.up(("sig", i)), 1)
                    else:
                        j, k = pool_taps[i]
                        if k == 0:
                            act.wait_ge(dve_out.sem, dve_out.at(("u", j)))
                        if i >= 4:
                            act.wait_ge(pool_out.sem, pool_out.at(("tap", i - 4)))
                        src, w = u_pad[:, j, k:k + SEQ], col("a_dw_w", k * KD + j)
                        if k == 0:
                            ins = act.activation(prod[:, i % 4], src, ACT.Identity, bias=col("a_dw_b", j), scale=w)
                        else:
                            ins = act.activation(prod[:, i % 4], src, ACT.Copy, scale=w)
                        ins.then_inc(act_out.up(("tap", i)), 1)
                for h, name in enumerate(("shift", "scale")):
                    act.wait_ge(late_used.sem, late_used.at(N_GATE * h + N_GATE - 1))
                    act.activation(mod_row[0:1, h * D:(h + 1) * D], acc[h][0:1, :], ACT.Copy)\
                        .then_inc(act_out.up(name), 1)

            @block.gpsimd
            def _(pool):
                for i, (j, k) in enumerate(pool_taps):
                    pool.wait_ge(act_out.sem, act_out.at(("tap", i)))
                    if k == 0:
                        ins = pool.tensor_copy(csum[:, 1], prod[:, i % 4])
                    else:
                        pool.wait_ge(pool_out.sem, pool_out.at(("tap", i - 1)))
                        dst = conv[:, j] if k == CONVW - 1 else csum[:, (k + 1) % 2]
                        ins = pool.tensor_tensor(dst, csum[:, k % 2], prod[:, i % 4], ALU.add)
                    ins.then_inc(pool_out.up(("tap", i)), 1)

            @block.vector
            def _(dve):
                dve.memset(u_pad[:, :, 0:PAD], 0.0).then_inc(dve_out.up("zero"), 1)
                dve.wait_ge(dve_out.sem, dve_out.at("zero"))
                split_affine(dve, hT)
                taps = [(j, k) for j in BY_VECTOR for k in range(CONVW)]

                def tap(made):
                    if taps[0][0] >= made:
                        return
                    j, k = taps.pop(0)
                    src, w = u_pad[:, j, k:k + SEQ], col("a_dw_w", k * KD + j)
                    if k == 0:
                        dve.wait_ge(dve_out.sem, dve_out.at(("u", j)))
                        ins = dve.tensor_scalar(conv[:, j], src, w, col("a_dw_b", j), ALU.mult, ALU.add)
                    else:
                        ins = dve.scalar_tensor_tensor(conv[:, j], src, w, conv[:, j], ALU.mult, ALU.add)
                    dve_steps.step(dve, ins)
                    conv_done[j] = dve_steps.n

                for i in range(KD):
                    if i + 1 < KD:
                        ring_a.split_lo(dve, g0 + i + 1)
                    dve.wait_ge(act_out.sem, act_out.at(("sig", i)))
                    dve.scalar_tensor_tensor(u_pad[:, i, PAD:PAD + SEQ], ps[:, 4 + i % 4, 0:SEQ],
                                             col("a_pw1_b", i), sig[:, i % 2], ALU.add, ALU.mult)\
                                                 .then_inc(dve_out.up(("u", i)), 1)
                    if i + 1 < KD:
                        for _ in range(AHEAD):
                            tap(i + 1)
                while taps:
                    tap(KD)
                dve.wait_ge(pe_out.sem, pe_out.at("columns"))
                mod_finish(dve, 2, ("mod_sh_f", "mod_sc_f"), "norm_pre_ffn")
                dve.wait_ge(late_used.sem, late_used.at(3 * N_GATE - 1))
                two = ps[:, 4:6, :].rearrange("p b n -> p (b n)")
                dve.wait_ge(rows_loaded, gates_row)
                dve_steps.step(dve, dve.tensor_tensor(gate_m[:], two, gate_m[:], ALU.add))
                dve.tensor_tensor(gate_m[:], gate_m[:], rows[:, 0], ALU.mult).then_inc(dve_out.up("gate_m"), 1)

            @block.tensor
            def _(pe):
                for j in range(KD):
                    ring_a.wait_split(pe, g0 + j)
                    if j >= 4:
                        pe.wait_ge(dve_out.sem, dve_out.at(("u", j - 4)))
                    for n in range(2):
                        for k in range(KD):
                            if j == 0 and n == 0:
                                wait_input(pe, k)
                            w = [ring_a.part(g0 + j, s, n * BCH + k * P, n * BCH + k * P + P) for s in range(2)]
                            ins = mm3(pe, ps[:, 4 + j % 4, n * SEQ:(n + 1) * SEQ], w,
                                      [actT[:, s, k] for s in range(2)], k == 0, k == KD - 1)
                    ins.then_inc(ring_a.used, 1)
                for i in range(2 * N_GATE):
                    late_chunk(pe, i, one_row, acc[i // 4][0:1, (i % 4) * MOD_COLS:(i % 4 + 1) * MOD_COLS])
                pe.wait_ge(dve_out.sem, dve_out.at(("u", KD - 1)))
                for i in range(N_GATE):
                    late_chunk(pe, 2 * N_GATE + i, lambda k: cb[:, k],
                               ps[:, 4 + i // 2, (i % 2) * MOD_COLS:(i % 2 + 1) * MOD_COLS])
                pe.wait_ge(act_out.sem, act_out.at("scale"))
                to_columns(pe, mod_row, 0)
                to_columns(pe, mod_row, 1).then_inc(pe_out.up("columns"), 1)
                for n, j in enumerate(MEAN_ORDER):
                    if j in BY_POOL:
                        pe.wait_ge(pool_out.sem, pool_out.at(("tap", CONVW * BY_POOL.index(j) + CONVW - 1)))
                    else:
                        pe.wait_ge(dve_steps.sem, conv_done[j])
                    ins = pe.matmul(ps[:, 6, 0:SEQ], ones_mean[:], conv[:, j], start=n == 0, stop=n == KD - 1)
                ins.then_inc(pe_out.up("mean"), 1)

        _, _, conv, sq, rstd, yb = carve((KD, P), (KD, PAD + SEQ), (KD, SEQ), (KD, SEQ), (SEQ,), (NT, D),
                                         limit=late_at)
        scratch = sq.rearrange("p k t -> p (k t)").rearrange("p (t d) -> p t d", t=NT)
        hT = conv
        g0 = sec["pw2"]
        pe_out.events(["var"])
        dve_out.events([("centred", k) for k in range(KD)] + [("normal", q) for q in range(4)]
                       + [("y", 0), ("y", 1), ("x", 0), ("x", 1), ("xn", 0), ("xn", 1)])
        act_out.events([("square", k) for k in range(KD)] + ["std"] + [("silu", q) for q in range(4)]
                       + [("yroot", 0), ("yroot", 1), ("root", 0), ("root", 1)])
        turned_done.events([0, 1])
        rows_count[0] += 16
        b2_row = rows_count[0]
        with nc.Block() as block:
            @block.sync
            def _(sp):
                load_row(sp, 0, A["a_pw2_b"][0])
                for g in range(g0 + 2, g0 + 4 + 2):
                    ring_a.load(sp, g)
                for g in range(2):
                    ring_b.load(sp, g)

            @block.scalar
            def _(act):
                for k in range(KD):
                    act.wait_ge(dve_out.sem, dve_out.at(("centred", k)))
                    act.activation(sq[:, k], conv[:, k], ACT.Square).then_inc(act_out.up(("square", k)), 1)
                ring_a.split_hi(act, g0)
                ring_a.split_hi(act, g0 + 1)
                act.wait_ge(pe_out.sem, pe_out.at("var"))
                act.activation(rstd, ps[:, 7, 0:SEQ], ACT.Sqrt, bias=eps[:, 1:2]).then_inc(act_out.up("std"), 1)
                for q in range(4):
                    act.wait_ge(dve_out.sem, dve_out.at(("normal", q)))
                    for k in range(2 * q, 2 * q + 2):
                        ins = act.activation(conv[:, k], conv[:, k], ACT.Silu, bias=col("a_ln_b", k),
                                             scale=col("a_ln_g", k))
                    ins.then_inc(act_out.up(("silu", q)), 1)
                for c in range(2, 5):
                    ring_a.split_hi(act, g0 + c)
                for t in range(NT):
                    act.wait_ge(dve_out.sem, dve_out.at(("y", t)))
                    act_steps.step(act, act.activation(scratch[:, t], yb[:, t], ACT.Square,
                                                       accum_out=stats[:, t, 3:4]))
                    act.activation(stats[:, t, 4:5], stats[:, t, 3:4], ACT.Sqrt, bias=eps[:, 0:1],
                                   scale=1.0 / D).then_inc(act_out.up(("yroot", t)), 1)
                for t in range(NT):
                    act.wait_ge(dve_out.sem, dve_out.at(("x", t)))
                    rms_scale(act, None, t, scratch)

            silu_split, gate_half = [], []

            @block.vector
            def _(dve):
                for k in range(KD):
                    dve.tensor_tensor(conv[:, k], conv[:, k], ps[:, 6, 0:SEQ], ALU.subtract)\
                        .then_inc(dve_out.up(("centred", k)), 1)
                ring_a.split_lo(dve, g0)
                ring_a.split_lo(dve, g0 + 1)
                dve.wait_ge(act_out.sem, act_out.at("std"))
                dve_steps.step(dve, dve.reciprocal(rstd, rstd))

                def normal(q):
                    pair = slice(2 * q, 2 * q + 2)
                    dve.tensor_tensor(conv[:, pair], conv[:, pair],
                                      rstd.unsqueeze(1).to_broadcast([P, 2, SEQ]), ALU.mult)\
                                          .then_inc(dve_out.up(("normal", q)), 1)

                def split_silu(q):
                    pair = slice(2 * q, 2 * q + 2)
                    dve.wait_ge(act_out.sem, act_out.at(("silu", q)))
                    dve_steps.step(dve, dve.tensor_copy(actT[:, 0, pair], conv[:, pair]))
                    dve_steps.step(dve, dve.tensor_tensor(actT[:, 1, pair], conv[:, pair],
                                                          actT[:, 0, pair].bitcast(F32), ALU.subtract))
                    silu_split.append(dve_steps.n)

                normal(0)
                normal(1)
                split_silu(0)
                normal(2)
                split_silu(1)
                normal(3)
                split_silu(2)
                split_silu(3)
                for c in range(2, 5):
                    ring_a.split_lo(dve, g0 + c)
                dve.wait_ge(late_used.sem, late_used.at(3 * N_GATE + 1))
                dve_steps.step(dve, dve.tensor_tensor(gate_f[:, 0:512], ps[:, 4], gate_f[:, 0:512], ALU.add))
                gate_half.append(dve_steps.n)
                ring_a.wait_used(dve, g0 + 3)
                dve.wait_ge(rows_loaded, b2_row)
                for t in range(NT):
                    dve.tensor_tensor(yb[:, t], acc[t], rows[:, 0], ALU.add).then_inc(dve_out.up(("y", t)), 1)
                for t in range(NT):
                    dve.wait_ge(act_out.sem, act_out.at(("yroot", t)))
                    dve_steps.step(dve, dve.reciprocal(stats[:, t, 5:6], stats[:, t, 4:5]))
                    dve_steps.step(dve, dve.scalar_tensor_tensor(yb[:, t], yb[:, t], stats[:, t, 5:6], gate_m[:],
                                                                 ALU.mult, ALU.mult))
                    dve.tensor_tensor(x_tok[:, t], x_tok[:, t], yb[:, t], ALU.add).then_inc(dve_out.up(("x", t)), 1)
                for t in range(NT):
                    rms_scale(None, dve, t, scratch)
                dve.wait_ge(late_used.sem, late_used.at(4 * N_GATE - 1))
                dve_steps.step(dve, dve.tensor_tensor(gate_f[:, 512:D], ps[:, 0], gate_f[:, 512:D], ALU.add))
                dve_steps.step(dve, dve.tensor_tensor(gate_f[:], gate_f[:], rows[:, 1], ALU.mult))

            @block.tensor
            def _(pe):
                def gate_chunk(i, bank):
                    late_chunk(pe, 3 * N_GATE + i, lambda k: cb[:, k],
                               ps[:, bank, (i % 2) * MOD_COLS:(i % 2 + 1) * MOD_COLS])

                gate_chunk(0, 4)
                for k in range(KD):
                    pe.wait_ge(act_out.sem, act_out.at(("square", k)))
                    ins = pe.matmul(ps[:, 7, 0:SEQ], ones_mean[:], sq[:, k], start=k == 0, stop=k == KD - 1)
                ins.then_inc(pe_out.up("var"), 1)
                gate_chunk(1, 4)
                for c in range(4):
                    ring_a.wait_split(pe, g0 + c)
                    pe.wait_ge(dve_steps.sem, silu_split[c])
                    for k in range(2 * c, 2 * c + 2):
                        for t in range(NT):
                            for n in range(2):
                                w = [ring_a.part(g0 + c, s, (k % 2) * D + n * 512, (k % 2) * D + n * 512 + 512)
                                     for s in range(2)]
                                ins = mm3(pe, acc[t][:, n * 512:(n + 1) * 512],
                                          [actT[:, s, k, t * P:(t + 1) * P] for s in range(2)], w, k == 0, k == KD - 1)
                    ins.then_inc(ring_a.used, 1)
                pe.wait_ge(dve_out.sem, dve_out.at(("y", 0)))
                gate_chunk(2, 0)
                gate_chunk(3, 0)
                pe.wait_ge(dve_steps.sem, gate_half[0])
                for t in range(NT):
                    pe.wait_ge(dve_out.sem, dve_out.at(("xn", t)))
                    turn(pe, scratch, t)

        modulated_at = turned_done.at(1)

        def take_modulated(hT=hT):
            def on_act(act):
                act.wait_ge(turned_done.sem, modulated_at)
                affine(act, hT, 2)

            return on_act, lambda dve: split_affine(dve, hT)

        h_done, f_step, conv_in, conv_done = sem("h_done"), sem("f_step"), sem("conv_in"), sem("conv_done")
        gated, scaled_x, root_ready = sem("gated"), sem("scaled_x"), sem("root_ready")
        done = {"h": 0, "f_step": 0, "conv": 0, "gated": 0}

        def ffn_stage(name, conv, norm_rows, turn_x, next_a, next_b, take):
            cg, cu, hf, yb, xs = carve((2, SEQ), (2, SEQ), (2, SEQ), (NT, D), (NT, D))
            ga, gb = sec[name], sec[name, "B"]
            sa, sb_ = ga, gb
            la, lb = [ring_a.load_no[ga + q] - 32 for q in range(2)], [ring_b.load_no[gb + q] - 16 for q in range(2)]
            h0, f0, c0, s0 = done["h"], done["f_step"], done["conv"], done["gated"]
            per = 4 if conv else 2
            done["h"] += NF
            done["f_step"] += per * NF
            done["conv"] += NF if conv else 0
            done["gated"] += NF
            BODY = NF // 2
            if not conv:
                rows_count[0] += 32
            rows_at = rows_count[0]
            dve_out.events([e for part in X_PARTS for e in ([("stat", part[0])] if part[1] == 0 else [])
                            + [("x", part)]])
            act_out.events([("root", 0)] + (["hi"] if turn_x and not conv else []) + [("root", 1)]
                           + (["hi"] if turn_x and conv else []))
            acc_ready.events([0])
            expect_input()
            if turn_x:
                turned_done.events(X_PARTS)
            if not conv:
                pool_out.events(["xs"])

            with nc.Block() as block:
                @block.sync
                def _(sp):
                    if norm_rows:
                        load_row(sp, 0, norm_rows[0])
                        load_row(sp, 1, norm_rows[1])
                    src = FFN_SOURCES[name]
                    with sp.Fori(1, BODY) as j:
                        for q in range(2):
                            sp.wait_ge(ring_a.lo_done, j * 2 + (sa + q - 1))
                            for half in range(2):
                                sp.dma_start(a_raw[:, q, half * BCH:(half + 1) * BCH].rearrange("p (k n) -> p k n", k=KD),
                                             src[half][:, :, bass.ds(j * 256 + q * P, P)])\
                                    .then_inc(ring_a.loaded[q], 16)
                            sp.wait_ge(ring_b.lo_done, j * 2 + (sb_ + q - 1))
                            sp.dma_start(b_raw[:, q], src[2][bass.ds(j * 2 + q, 1), :, :].rearrange("a p n -> (a p) n"))\
                                .then_inc(ring_b.loaded[q], 16)
                    for g in range(next_a, next_a + 2):
                        ring_a.load(sp, g)
                    for g in range(next_b, next_b + 2):
                        ring_b.load(sp, g)

                def split(act_or_none, dve_or_none, q, a_count, b_count, a_load, b_load, first):
                    if act_or_none is not None:
                        act = act_or_none
                        act.wait_ge(ring_a.loaded[q], a_load)
                        if a_count[1] is not None:
                            act.wait_ge(ring_a.used, a_count[1])
                        act.activation(a_parts[:, q, 0], a_raw[:, q], ACT.Copy).then_inc(ring_a.hi_done, 1)
                        act.wait_ge(ring_b.loaded[q], b_load)
                        if b_count[1] is not None:
                            act.wait_ge(ring_b.used, b_count[1])
                        act.activation(b_parts[:, q, 0], b_raw[:, q], ACT.Copy).then_inc(ring_b.hi_done, 1)
                    else:
                        dve = dve_or_none
                        dve.wait_ge(ring_a.hi_done, a_count[0])
                        dve.tensor_tensor(a_parts[:, q, 1], a_raw[:, q], a_parts[:, q, 0].bitcast(F32),
                                          ALU.subtract).then_inc(ring_a.lo_done, 1)
                        dve.wait_ge(ring_b.hi_done, b_count[0])
                        dve.tensor_tensor(b_parts[:, q, 1], b_raw[:, q], b_parts[:, q, 0].bitcast(F32),
                                          ALU.subtract).then_inc(ring_b.lo_done, 1)

                def tile_split(act, dve, q, j):
                    first = isinstance(j, int)
                    a_used = None if first and sa + 2 * j + q < 2 else j * 2 + (sa + q - 1)
                    b_used = None if first and sb_ + 2 * j + q < 2 else j * 2 + (sb_ + q - 1)
                    split(act, dve, q, (j * 2 + (sa + q + 1), a_used), (j * 2 + (sb_ + q + 1), b_used),
                          j * 32 + (la[q] + 32), j * 16 + (lb[q] + 16), first)

                def first_splits(act, dve):
                    if act is not None:
                        ring_a.split_hi(act, ga + 1)
                        ring_b.split_hi(act, gb)
                        ring_b.split_hi(act, gb + 1)
                    else:
                        ring_a.split_lo(dve, ga + 1)
                        ring_b.split_lo(dve, gb)
                        ring_b.split_lo(dve, gb + 1)

                def tile_act(act, q, j):
                    first = isinstance(j, int) and j == 0
                    act.wait_ge(ring_a.used, j * 2 + (sa + q + 1))
                    if not first:
                        act.wait_ge(h_done, j * 2 + (h0 + q - 1))
                    gate, up = ps[:, 4 + q, 0:SEQ], ps[:, 4 + q, SEQ:2 * SEQ]
                    if conv:
                        for buf, src, half in ((cg, gate, 0), (cu, up, NF)):
                            w = col_at("f_dw_w", 2 * 2 * NF + half + q, j)
                            b = col_at("f_dw_b", half + q, j)
                            ins = act.activation(buf[:, q], src, ACT.Identity, bias=b, scale=w)
                        ins.then_inc(conv_in, 1)
                        act.wait_ge(conv_done, j * 2 + (c0 + q + 1))
                        act.activation(cg[:, q], cg[:, q], ACT.Silu).then_inc(gated, 1)
                    else:
                        act.activation(cg[:, q], gate, ACT.Silu).then_inc(gated, 1)

                def col_at(name, i, j):
                    if isinstance(j, int):
                        return col(name, i + 2 * j)
                    return par[:, bass.ds(j * 2 + (first_col[name] + i), 1)]

                def tile_dve(dve, q, j):
                    n = f0 + per * q
                    gate, up = ps[:, 4 + q, 0:SEQ], ps[:, 4 + q, SEQ:2 * SEQ]
                    if conv:
                        dve.wait_ge(conv_in, j * 2 + (c0 + q + 1))
                        for back in (1, 2):
                            for buf, src, half in ((cg, gate, 0), (cu, up, NF)):
                                w = col_at("f_dw_w", (2 - back) * 2 * NF + half + q, j)
                                if back == 2:
                                    dve.wait_ge(f_step, j * (2 * per) + (n + (1 if half == 0 else 2)))
                                ins = dve.scalar_tensor_tensor(buf[:, q, back:SEQ], src[:, 0:SEQ - back], w,
                                                               buf[:, q, back:SEQ], ALU.mult, ALU.add)
                                if back == 1:
                                    ins.then_inc(f_step, 1)
                        ins.then_inc(conv_done, 1)
                        n += 2
                        up = cu[:, q]
                    dve.wait_ge(gated, j * 2 + (s0 + q + 1))
                    dve.tensor_tensor(hf[:, q], cg[:, q], up, ALU.mult).then_inc(f_step, 1)
                    if not (isinstance(j, int) and j == 0 and sb_ + q < 2):
                        dve.wait_ge(ring_b.used, j * 2 + (sb_ + q - 1))
                    dve.wait_ge(f_step, j * (2 * per) + (n + 1))
                    dve.tensor_copy(hid[:, q, 0], hf[:, q]).then_inc(f_step, 1)
                    dve.wait_ge(f_step, j * (2 * per) + (n + 2))
                    dve.tensor_tensor(hid[:, q, 1], hf[:, q], hid[:, q, 0].bitcast(F32),
                                      ALU.subtract).then_inc(h_done, 1)

                def up_pe(pe, q, j):
                    first = isinstance(j, int) and j == 0
                    pe.wait_ge(ring_a.lo_done, j * 2 + (sa + q + 1))
                    if not first:
                        pe.wait_ge(h_done, j * 2 + (h0 + q - 1))
                    for n in range(2):
                        for k in range(KD):
                            if first and q == 0 and n == 0:
                                wait_input(pe, k)
                            w = [a_parts[:, q, s, n * BCH + k * P:n * BCH + (k + 1) * P] for s in range(2)]
                            ins = mm3(pe, ps[:, 4 + q, n * SEQ:(n + 1) * SEQ], w, [actT[:, s, k] for s in range(2)],
                                      k == 0, k == KD - 1)
                    ins.then_inc(ring_a.used, 1)

                def down_pe(pe, q, j, start, stop):
                    pe.wait_ge(ring_b.lo_done, j * 2 + (sb_ + q + 1))
                    pe.wait_ge(h_done, j * 2 + (h0 + q + 1))
                    for t in range(NT):
                        for n in range(2):
                            ins = mm3(pe, acc[t][:, n * 512:(n + 1) * 512],
                                      [hid[:, q, s, t * P:(t + 1) * P] for s in range(2)],
                                      [b_parts[:, q, s, n * 512:(n + 1) * 512] for s in range(2)], start, stop)
                        if stop and t == 0:
                            ins.then_inc(acc_ready.up(0), 1)
                    ins.then_inc(ring_b.used, 1)

                @block.tensor
                def _(pe):
                    up_pe(pe, 0, 0)
                    up_pe(pe, 1, 0)
                    down_pe(pe, 0, 0, True, False)
                    with pe.Fori(1, BODY) as j:
                        up_pe(pe, 0, j)
                        down_pe(pe, 1, j - 1, False, False)
                        up_pe(pe, 1, j)
                        down_pe(pe, 0, j, False, False)
                    down_pe(pe, 1, BODY - 1, False, True)
                    if turn_x:
                        turn_x_pe(pe)

                @block.scalar
                def _(act):
                    take[0](act)
                    first_splits(act, None)
                    tile_act(act, 0, 0)
                    with act.Fori(1, BODY) as j:
                        tile_split(act, None, 0, j)
                        tile_act(act, 1, j - 1)
                        tile_split(act, None, 1, j)
                        tile_act(act, 0, j)
                    if turn_x:
                        ring_a.split_hi(act, next_a)
                    tile_act(act, 1, BODY - 1)
                    for t in range(NT):
                        if conv:
                            if t == 0:
                                act.wait_ge(acc_ready.sem, acc_ready.at(0))
                            else:
                                act.wait_ge(ring_b.used, sb_ + NF)
                            act_steps.step(act, act.activation(yb[:, t], acc[t], ACT.Square,
                                                               accum_out=stats[:, t, 6:7]))
                            act.activation(stats[:, t, 7:8], stats[:, t, 6:7], ACT.Sqrt,
                                           bias=eps[:, 0:1], scale=1.0 / D).then_inc(act_out.up(("root", t)), 1)
                        else:
                            act.wait_ge(dve_out.sem, dve_out.at(("stat", t)))
                            act.activation(stats[:, t, 7:8], stats[:, t, 13:14], ACT.Sqrt,
                                           bias=eps[:, 1:2]).then_inc(act_out.up(("root", t)), 1)
                        if turn_x and t == 0 and not conv:
                            first_hi(act)
                    if turn_x and conv:
                        first_hi(act)

                @block.gpsimd
                def _(pool):
                    if not conv:
                        pool.tensor_scalar(xs, x_tok[:], ALPHA, None, ALU.mult).then_inc(pool_out.up("xs"), 1)

                @block.vector
                def _(dve):
                    take[1](dve)
                    first_splits(None, dve)
                    tile_dve(dve, 0, 0)
                    with dve.Fori(1, BODY) as j:
                        tile_split(None, dve, 0, j)
                        tile_dve(dve, 1, j - 1)
                        tile_split(None, dve, 1, j)
                        tile_dve(dve, 0, j)
                    if turn_x:
                        ring_a.split_lo(dve, next_a)
                    tile_dve(dve, 1, BODY - 1)
                    if conv:
                        for t in range(NT):
                            dve.wait_ge(act_out.sem, act_out.at(("root", t)))
                            dve.reciprocal(stats[:, t, 8:9], stats[:, t, 7:8]).then_inc(dve_out.up(("stat", t)), 1)
                            dve.wait_ge(dve_out.sem, dve_out.at(("stat", t)))
                            dve_steps.step(dve, dve.scalar_tensor_tensor(yb[:, t], acc[t], stats[:, t, 8:9],
                                                                         gate_f[:], ALU.mult, ALU.mult))
                            for part in X_PARTS:
                                if part[0] == t:
                                    w = slice(part[1] * P, part[2] * P)
                                    dve.tensor_tensor(x_tok[:, t, w], x_tok[:, t, w], yb[:, t, w], ALU.add)\
                                       .then_inc(dve_out.up(("x", part)), 1)
                    else:
                        layer_norm_dve(dve, yb, xs, 0.5, rows_at, ring_b.used, sb_ + NF)
                    if turn_x:
                        first_lo(dve)
            if turn_x:
                return take_x()

        def layer_norm_dve(dve, yb, xs, scale, rows_at, used, acc_at):
            dve.wait_ge(pool_out.sem, pool_out.at("xs"))
            dve.wait_ge(rows_loaded, rows_at)
            for t in range(NT):
                if t == 0:
                    dve.wait_ge(acc_ready.sem, acc_ready.at(0))
                else:
                    dve.wait_ge(used, acc_at)
                dve_steps.step(dve, dve.scalar_tensor_tensor(yb[:, t], acc[t], scale, xs[:, t], ALU.mult, ALU.add))
                for n in range(2):
                    ins = dve.bn_stats(stats[:, t, 6 * n:6 * n + 6], yb[:, t, n * 512:(n + 1) * 512])
                    dve_steps.mark(ins) if n == 0 else dve_steps.step(dve, ins)
                dve.bn_aggr(stats[:, t, 12:14], stats[:, t, 0:12]).then_inc(dve_out.up(("stat", t)), 1)
                dve.wait_ge(dve_out.sem, dve_out.at(("stat", t)))
                dve_steps.step(dve, dve.scalar_tensor_tensor(yb[:, t], yb[:, t], stats[:, t, 12:13], rows[:, 0],
                                                             ALU.subtract, ALU.mult))
                dve.wait_ge(act_out.sem, act_out.at(("root", t)))
                dve_steps.step(dve, dve.reciprocal(stats[:, t, 14:15], stats[:, t, 7:8]))
                for part in X_PARTS:
                    if part[0] == t:
                        w = slice(part[1] * P, part[2] * P)
                        dve.scalar_tensor_tensor(x_tok[:, t, w], yb[:, t, w], stats[:, t, 14:15], rows[:, 1, w],
                                                 ALU.mult, ALU.add).then_inc(dve_out.up(("x", part)), 1)

        def ffn_views(gate, up_w, down):
            g, u = (w.rearrange("(k p) n -> p k n", p=P) for w in (gate, up_w))
            return g, u, down.rearrange("(i p) n -> i p n", p=P)

        FFN_SOURCES = {"ffn": ffn_views(A["f_up_w"][0][:, 0:DFF], A["f_up_w"][0][:, DFF:2 * DFF], A["f_down_w"][0])}
        for i in range(2):
            for f in ("ffn1", "ffn2"):
                FFN_SOURCES[f, i] = ffn_views(*(A[f"{f}_w_{n}_2"][i] for n in ("gate", "up", "down")))

        def memory_attention(mqT, probs, probsT, nxt):
            n = NMH * NT
            pe_out.events([("scores",), ("probsT",), ("out",)])
            act_out.events([("exp",), ("probsT",), ("hi",)])
            dve_out.events([("max",), ("probs",), ("probsT",), ("lo",)])
            scores = ps[:, 0:4, :].rearrange("p b (t m) -> p (b t) m", t=NT)
            bank = lambda h: 2 * (h % 2) + h // 2
            neg_max, total, inv = small[:, 0:n], small[:, n:2 * n], small[:, 2 * n:3 * n]
            with nc.Block() as block:
                @block.tensor
                def _(pe):
                    for h in range(NMH):
                        r = slice((h % 2) * HD, (h % 2) * HD + HD)
                        for t in range(NT):
                            ins = pe.matmul(scores[:, 2 * bank(h) + t], mqT[r, h // 2, t * P:(t + 1) * P],
                                            memkT[r, h // 2, :], start=True, stop=True)
                    ins.then_inc(pe_out.up(("scores",)), 1)
                    pe.wait_ge(dve_out.sem, dve_out.at(("probs",)))
                    for h in range(NMH):
                        for m in range(2):
                            for t in range(NT):
                                ins = pe.transpose(turned[:, 2 * h + m, t * P:(t + 1) * P],
                                                   probs[:, 2 * bank(h) + t, m * P:(m + 1) * P], ident[:])
                    ins.then_inc(pe_out.up(("probsT",)), 1)
                    pe.wait_ge(act_out.sem, act_out.at(("probsT",)))
                    pe.wait_ge(dve_out.sem, dve_out.at(("probsT",)))
                    for h in range(NMH):
                        for m in range(2):
                            ins = pe.matmul(ps[(h % 2) * HD:(h % 2) * HD + HD, h // 2, 0:SEQ],
                                            memv[:, m, h * HD:(h + 1) * HD], probsT[:, 2 * h + m, :],
                                            start=m == 0, stop=m == 1)
                    ins.then_inc(pe_out.up(("out",)), 1)

                @block.vector
                def _(dve):
                    dve.wait_ge(pe_out.sem, pe_out.at(("scores",)))
                    dve.tensor_reduce(neg_max, scores, AX_X, ALU.max, negate=True).then_inc(dve_out.up(("max",)), 1)
                    ring_a.split_lo(dve, nxt)
                    dve.wait_ge(act_out.sem, act_out.at(("exp",)))
                    dve_steps.step(dve, dve.reciprocal(inv, total))
                    dve.tensor_tensor(probs, probs, inv.unsqueeze(2).to_broadcast([P, n, NMEM]),
                                      ALU.mult).then_inc(dve_out.up(("probs",)), 1)
                    ring_a.split_lo(dve, nxt + 1)
                    dve.wait_ge(pe_out.sem, pe_out.at(("probsT",)))
                    dve.tensor_copy(probsT[:, 4:8], turned[:, 4:8]).then_inc(dve_out.up(("probsT",)), 1)
                    dve.wait_ge(act_out.sem, act_out.at(("hi",)))
                    dve.tensor_tensor(actT[:, 1, 6:8], ps[:, 0:2, 0:SEQ],
                                      actT[:, 0, 6:8].bitcast(F32), ALU.subtract).then_inc(dve_out.up(("lo",)), 1)

                @block.scalar
                def _(act):
                    ring_a.split_hi(act, nxt)
                    act.wait_ge(dve_out.sem, dve_out.at(("max",)))
                    for i in range(n):
                        ins = act.activation(probs[:, i], scores[:, i], ACT.Exp, bias=neg_max[:, i:i + 1],
                                             accum_out=total[:, i:i + 1])
                    ins.then_inc(act_out.up(("exp",)), 1)
                    ring_a.split_hi(act, nxt + 1)
                    act.wait_ge(pe_out.sem, pe_out.at(("probsT",)))
                    act.activation(probsT[:, 0:4], turned[:, 0:4], ACT.Copy).then_inc(act_out.up(("probsT",)), 1)
                    act.wait_ge(pe_out.sem, pe_out.at(("out",)))
                    act.activation(actT[:, 0, 6:8], ps[:, 0:2, 0:SEQ], ACT.Copy).then_inc(act_out.up(("hi",)), 1)

        def output_stage(i):
            yb, xs = carve((NT, D), (NT, D))
            g0, nxt = sec["w_out", i], sec[("ffn2", i), "B"]
            dve_out.events([e for part in X_PARTS for e in ([("stat", part[0])] if part[1] == 0 else [])
                            + [("x", part)]])
            act_out.events([("root", 0), "hi", ("root", 1)])
            acc_ready.events([0])
            turned_done.events(X_PARTS)
            pool_out.events(["xs"])
            rows_count[0] += 32
            rows_at = rows_count[0]
            with nc.Block() as block:
                @block.sync
                def _(sp):
                    load_row(sp, 0, A["ln_g_2"][i, 1])
                    load_row(sp, 1, A["ln_b_2"][i, 1])
                    for g in range(g0 + 2, g0 + 4 + 2):
                        ring_a.load(sp, g)

                @block.gpsimd
                def _(pool):
                    pool.tensor_scalar(xs, x_tok[:], ALPHA, None, ALU.mult).then_inc(pool_out.up("xs"), 1)

                @block.scalar
                def _(act):
                    for c in range(2, 5):
                        ring_a.split_hi(act, g0 + c)
                    for t in range(NT):
                        act.wait_ge(dve_out.sem, dve_out.at(("stat", t)))
                        act.activation(stats[:, t, 7:8], stats[:, t, 13:14], ACT.Sqrt,
                                       bias=eps[:, 1:2]).then_inc(act_out.up(("root", t)), 1)
                        if t == 0:
                            first_hi(act)

                @block.vector
                def _(dve):
                    for c in range(2, 5):
                        ring_a.split_lo(dve, g0 + c)
                    layer_norm_dve(dve, yb, xs, 1.0, rows_at, ring_a.used, g0 + 4)
                    first_lo(dve)

                @block.tensor
                def _(pe):
                    for c in range(4):
                        ring_a.wait_split(pe, g0 + c)
                        down_chunk(pe, g0 + c, c)
                    turn_x_pe(pe)
            return take_x()

        def down_chunk(pe, g, c):
            for t in range(NT):
                for k in range(2 * c, 2 * c + 2):
                    for n in range(2):
                        w = [ring_a.part(g, s, (k % 2) * D + n * 512, (k % 2) * D + n * 512 + 512) for s in range(2)]
                        ins = mm3(pe, acc[t][:, n * 512:(n + 1) * 512],
                                  [actT[:, s, k, t * P:(t + 1) * P] for s in range(2)], w, k == 0, k == KD - 1)
                if c == 3 and t == 0:
                    ins.then_inc(acc_ready.up(0), 1)
            ins.then_inc(ring_a.used, 1)

        def rwkv_stages(take):
            z, mqT, lora, g_up, SIG, CUM, Av, KK, BON = carve(
                (20, SEQ), (2, SEQ), (C,), (C,), (MT6, SEQ), (MT6, SEQ), (MT6, SEQ), (MT6, SEQ), (MT6, SEQ))
            R, K, V = (z[:, MT6 * i:MT6 * (i + 1)] for i in range(3))
            low, lowg = z[:, 18], z[:, 19]
            used = (20 + 2) * SEQ + 2 * C + 5 * MT6 * SEQ
            reset = gate_m[:, C:D]
            mk = rows[:].rearrange("p a (m n) -> p (a m) n", n=P)
            level_mask = [mk[:, l] for l in range(6)]
            pair_mask, below, upto = mk[:, 6], mk[:, 7], mk[:, 8]
            one_minus_mu, one_minus_ka = small[:, 24:44], small[:, 44:50]

            g0 = sec["rwkv_in"]
            expect_input()
            act_out.events([("z", m) for m in range(20)] + ["mq"])
            dve_out.events(["mu"] + [("z", m) for m in range(20)])
            load_at = 16 * 3
            lora_loaded = sem("lora_loaded")
            with nc.Block() as block:
                @block.sync
                def _(sp):
                    sp.dma_start(lora[0:HD], A["rwkv_w_up_2"][0]).then_inc(lora_loaded, 16)
                    sp.dma_start(lora[HD:P], A["rwkv_a_up_2"][0]).then_inc(lora_loaded, 16)
                    sp.dma_start(g_up, A["rwkv_g_up_2"][0]).then_inc(lora_loaded, 16)
                    for g in range(g0 + 2, g0 + 12 + 2):
                        ring_a.load(sp, g)

                @block.gpsimd
                def _(pool):
                    def select(view, base, cm, pattern):
                        pool_steps.step(pool, pool.affine_select(out=view, in_=view, compare_op=ALU.is_ge, fill=0.0,
                                                                 base=base, pattern=pattern, channel_multiplier=cm))
                    pool_steps.step(pool, pool.memset(mk[:, 0:9], 0.0))
                    for l in range(6):
                        b = 1 << l
                        view = level_mask[l].rearrange("p (B h w) -> p B h w", h=2, w=b)[:, :, 1]
                        pool_steps.step(pool, pool.memset(view, 1.0))
                        select(view, 0, 1, [[-2 * b, P // (2 * b)], [0, b]])
                        select(view, b - 1, -1, [[2 * b, P // (2 * b)], [0, b]])
                    view = pair_mask.rearrange("p (B h) -> p B h", h=2)[:, :, 0]
                    pool_steps.step(pool, pool.memset(view, 1.0))
                    select(view, -1, 1, [[-2, P // 2]])
                    select(view, 1, -1, [[2, P // 2]])
                    for m, base in ((below, -1), (upto, 0)):
                        view = m.rearrange("p (c w) -> p c w", w=CHUNK)
                        pool_steps.step(pool, pool.memset(m, 1.0))
                        select(view, base, -1, [[CHUNK, 2], [1, CHUNK]])
                        select(view, 0, 1, [[-CHUNK, 2], [0, CHUNK]])
                    pool_steps.step(pool, pool.memset(reset, 1.0))
                    pool_steps.step(pool, pool.memset(reset.rearrange("p (c w) -> p c w", w=CHUNK)[:, :, 0:1], 0.0))

                @block.tensor
                def _(pe):
                    for c in range(12):
                        g = g0 + c
                        ring_a.wait_split(pe, g)
                        if c >= 8:
                            pe.wait_ge(dve_out.sem, dve_out.at(("z", 2 * (c - 8) + 1)))
                        width = 256 if c < 10 else P
                        for n in range(width // P):
                            for k in range(KD):
                                if c == 0 and n == 0:
                                    wait_input(pe, k)
                                w = [ring_a.part(g, s, k * width + n * P, k * width + n * P + P) for s in range(2)]
                                ins = mm3(pe, ps[:, c % 8, n * SEQ:(n + 1) * SEQ], w, [actT[:, s, k] for s in range(2)],
                                          k == 0, k == KD - 1)
                        ins.then_inc(ring_a.used, 1)

                @block.scalar
                def _(act):
                    take[0](act)
                    act.wait_ge(dve_out.sem, dve_out.at("mu"))
                    for c in range(13):
                        if 1 <= c < 12:
                            ring_a.split_hi(act, g0 + c)
                        if 1 <= c <= 10:
                            ring_a.wait_used(act, g0 + c - 1)
                            for n in range(2):
                                m = 2 * (c - 1) + n
                                act.activation(z[:, m], ps[:, (c - 1) % 8, n * SEQ:(n + 1) * SEQ],
                                               ACT.Copy, scale=one_minus_mu[:, m:m + 1])\
                                                   .then_inc(act_out.up(("z", m)), 1)
                    ring_a.wait_used(act, g0 + 11)
                    act.activation(mqT, ps[:, 2:4, 0:SEQ], ACT.Copy, scale=HD ** -0.5).then_inc(act_out.up("mq"), 1)

                @block.vector
                def _(dve):
                    take[1](dve)
                    dve_steps.mark(dve.tensor_scalar(one_minus_ka, cols("k_a", MT6), -1.0, 1.0, ALU.mult, ALU.add))
                    dve.tensor_scalar(one_minus_mu, cols("mu", 20), -1.0, 1.0, ALU.mult, ALU.add)\
                        .then_inc(dve_out.up("mu"), 1)
                    for c in range(1, 12):
                        ring_a.split_lo(dve, g0 + c)
                        if c <= 10:
                            for n in range(2):
                                m = 2 * (c - 1) + n
                                dve.wait_ge(act_out.sem, act_out.at(("z", m | 1)))
                                src = ps[:, (c - 1) % 8, n * SEQ:(n + 1) * SEQ - 1]
                                dve.scalar_tensor_tensor(z[:, m, 1:SEQ], src, col("mu", m),
                                                         z[:, m, 1:SEQ], ALU.mult, ALU.add)\
                                                             .then_inc(dve_out.up(("z", m)), 1)

            memory_attention(mqT, arena[:, 22 * SEQ + 2 * C:22 * SEQ + 2 * C + 2048].rearrange("p (a b) -> p a b", a=8),
                             arena[:, 22 * SEQ + 2 * C + 2048:22 * SEQ + 2 * C + 4096].rearrange("p (a b) -> p a b", a=8),
                             sec["w_out", 0])

            wv = ps[:, 0:3, :].rearrange("p b (m t) -> p (b m) t", m=2)
            av = ps[:, 3:6, :].rearrange("p b (m t) -> p (b m) t", m=2)
            w_end = small[:, 0:24].rearrange("p (m c) -> p m c", m=MT6)
            pe_out.events(["w", "a", "norm", "bonus"])
            act_out.events(["low", "sig", "kk", "a", "square", "root", "Wex", "Winv", "W"])
            dve_out.events(["cum", "ss", "kk", "k", "rk", "bon", "cumx", "q", "b", "kb"])
            with nc.Block() as block:
                @block.tensor
                def _(pe):
                    pe.wait_ge(act_out.sem, act_out.at("low"))
                    pe.wait_ge(lora_loaded, 48)
                    for m in range(MT6):
                        ins = pe.matmul(wv[:, m], lora[0:HD, m * P:(m + 1) * P], low[0:HD], start=True, stop=True)
                    ins.then_inc(pe_out.up("w"), 1)
                    for m in range(MT6):
                        ins = pe.matmul(av[:, m], lora[HD:P, m * P:(m + 1) * P], low[HD:P], start=True, stop=True)
                    ins.then_inc(pe_out.up("a"), 1)
                    pe.wait_ge(act_out.sem, act_out.at("square"))
                    for m in range(MT6):
                        ins = pe.matmul(wv[:, m], head_ones[:], BON[:, m], start=True, stop=True)
                    ins.then_inc(pe_out.up("norm"), 1)
                    pe.wait_ge(dve_out.sem, dve_out.at("rk"))
                    for m in range(MT6):
                        ins = pe.matmul(av[:, m], head_ones[:], BON[:, m], start=True, stop=True)
                    ins.then_inc(pe_out.up("bonus"), 1)

                @block.scalar
                def _(act):
                    act.activation(low[0:HD], low[0:HD], ACT.Tanh).then_inc(act_out.up("low"), 1)
                    act.wait_ge(pe_out.sem, pe_out.at("w"))
                    for m in range(MT6):
                        ins = act.activation(SIG[:, m], wv[:, m], ACT.Sigmoid, bias=col("w0", m))
                    ins.then_inc(act_out.up("sig"), 1)
                    for m in range(MT6):
                        ins = act.activation(KK[:, m], K[:, m], ACT.Copy, scale=col("k_k", m))
                    ins.then_inc(act_out.up("kk"), 1)
                    act.wait_ge(pe_out.sem, pe_out.at("a"))
                    for m in range(MT6):
                        ins = act.activation(Av[:, m], av[:, m], ACT.Sigmoid, bias=col("a0", m))
                    ins.then_inc(act_out.up("a"), 1)
                    act_steps.step(act, act.activation(lowg, lowg, ACT.Sigmoid))
                    act.wait_ge(act_out.sem, act_out.at("kk"))
                    act.activation(BON, KK, ACT.Square).then_inc(act_out.up("square"), 1)
                    act.wait_ge(dve_out.sem, dve_out.at("ss"))
                    act.activation(BON, BON, ACT.Sqrt).then_inc(act_out.up("root"), 1)
                    act.wait_ge(dve_out.sem, dve_out.at("cumx"))
                    act.activation(SIG, SIG, ACT.Exp, scale=-DECAY).then_inc(act_out.up("Wex"), 1)
                    act.wait_ge(dve_out.sem, dve_out.at("b"))
                    act.activation(KK, CUM, ACT.Exp, scale=DECAY).then_inc(act_out.up("Winv"), 1)
                    act.wait_ge(act_out.sem, act_out.at("Winv"))
                    act.activation(CUM, CUM, ACT.Exp, scale=-DECAY).then_inc(act_out.up("W"), 1)

                @block.vector
                def _(dve):
                    dve.wait_ge(act_out.sem, act_out.at("sig"))
                    for m in range(MT6):
                        ins = dve.tensor_tensor_scan(CUM[:, m], reset, SIG[:, m], 0.0, ALU.mult, ALU.add)
                    ins.then_inc(dve_out.up("cum"), 1)
                    dve.wait_ge(pe_out.sem, pe_out.at("norm"))
                    dve.tensor_scalar(BON, wv, 1e-24, None, ALU.max).then_inc(dve_out.up("ss"), 1)
                    dve.wait_ge(act_out.sem, act_out.at("root"))
                    dve_steps.step(dve, dve.reciprocal(BON, BON))
                    dve.tensor_tensor(KK, KK, BON, ALU.mult).then_inc(dve_out.up("kk"), 1)
                    dve.wait_ge(dve_out.sem, dve_out.at("kk"))
                    dve.wait_ge(act_out.sem, act_out.at("a"))
                    for m in range(MT6):
                        ins = dve.tensor_scalar(BON[:, m], Av[:, m], col("k_a", m), one_minus_ka[:, m:m + 1],
                                                ALU.mult, ALU.add)
                    dve_steps.step(dve, ins)
                    dve.tensor_tensor(K, K, BON, ALU.mult).then_inc(dve_out.up("k"), 1)
                    dve.wait_ge(dve_out.sem, dve_out.at("k"))
                    for m in range(MT6):
                        ins = dve.scalar_tensor_tensor(BON[:, m], R[:, m], col("r_k", m), K[:, m], ALU.mult, ALU.mult)
                    ins.then_inc(dve_out.up("rk"), 1)
                    dve.wait_ge(pe_out.sem, pe_out.at("bonus"))
                    dve.tensor_tensor(BON, av, V, ALU.mult).then_inc(dve_out.up("bon"), 1)
                    dve.tensor_tensor(SIG, CUM, SIG, ALU.subtract).then_inc(dve_out.up("cumx"), 1)
                    dve.wait_ge(act_out.sem, act_out.at("Wex"))
                    dve.tensor_tensor(SIG, SIG, KK, ALU.mult).then_inc(dve_out.up("q"), 1)
                    dve.scalar_tensor_tensor(Av, KK, -1.0, Av, ALU.mult, ALU.mult).then_inc(dve_out.up("b"), 1)
                    dve.wait_ge(act_out.sem, act_out.at("Winv"))
                    dve.wait_ge(dve_out.sem, dve_out.at("b"))
                    dve_steps.step(dve, dve.tensor_tensor(Av, Av, KK, ALU.mult))
                    dve.tensor_tensor(K, K, KK, ALU.mult).then_inc(dve_out.up("kb"), 1)
                    dve.wait_ge(act_out.sem, act_out.at("W"))
                    dve_steps.step(dve, dve.tensor_tensor(R, R, CUM, ALU.mult))
                    dve_steps.step(dve, dve.tensor_copy(w_end, CUM.rearrange("p m (c w) -> p m c w", w=CHUNK)
                                                        [:, :, :, CHUNK - 1]))
            rwkv_core(R, K, V, SIG, Av, BON, CUM, KK, lowg, g_up, w_end, level_mask, pair_mask, below, upto, used)

        def rwkv_core(R, K, V, Q, BB, BON, CUM, KK, lowg, g_up, w_end, level_mask, pair_mask, below, upto, used):
            LV = range(1, 6)
            units = [(T, hf) for T in range(NT) for hf in range(2)]
            Vt, Qt = (CUM.rearrange("p m t -> p (m t)")[:, i * C:(i + 1) * C] for i in range(2))
            Kt, Bt = (KK.rearrange("p m t -> p (m t)")[:, i * C:(i + 1) * C] for i in range(2))
            tok = (Vt, Qt, Kt, Bt)

            def piece(at, *shape):
                ap = arena[:, at:at + math.prod(shape)]
                return ap.rearrange("p (a b c) -> p a b c", a=shape[0], b=shape[1]) if len(shape) == 3 else \
                    ap.rearrange("p (a b) -> p a b", a=shape[0])

            free = 20 * SEQ
            LkV, U, S = piece(free, 2, 3, HD), piece(free + 384, 2, 3, HD), piece(free + 768, MT6, HD)
            Z, LT, M0, M1 = (piece(used + i * 768, 2, 3, P) for i in range(4))
            M = (M0, M1)
            O = piece(used + 4 * 768, MT6, 2, HD)
            assert used + 5 * 768 <= arena_words
            Dm = gate_m[:, 0:C].rearrange("p (a b c) -> p a b c", a=2, b=3)
            DT = gate_f[:, 0:C].rearrange("p (a b c) -> p a b c", a=2, b=3)
            A1 = Z[:, 0]
            Oh = O.rearrange("p m a d -> p (m a) d")
            hs = [small[:, 64 + 12 * i:76 + 12 * i] for i in range(4)]

            def bank(b, cols=3 * P):
                return ps[:, b, 0:cols].rearrange("p (m t) -> p m t", m=3)

            def bmask(m):
                return m.unsqueeze(1).to_broadcast([P, 3, P])

            def first_chunk(T, c):
                return T == 0 and c == 0

            def last_chunk(T, c):
                return T == NT - 1 and c == 1

            pe_names, act_names, dve_names, pool_names = [], [], ["zero"], []
            for T in range(NT):
                pe_names += [("tr", T, i) for i in range(4)]
                act_names += [("tok", T, i) for i in range(2)]
                dve_names += [("tok", T, i) for i in range(2, 4)]
                for hf in range(2):
                    u = (T, hf)
                    pe_names += [(n, u, p) for p in range(2) for n in ("LbT", "Lb", "LkT")]
                    pe_names += [("LkV", u, p) for p in range(2)]
                    act_names += [("LT", u, p) for p in range(2)] + [("LkV", u, p) for p in range(2)]
                    dve_names += [(n, u, p) for p in range(2) for n in ("D1", ("D", 0), "LkT")]
                    pool_names += [(n, u, p) for p in range(2) for n in ("DT1", ("DT", 0))]
                    for l in LV:
                        pe_names += [(("Z", l), u, p) for p in range(2)]
                        pe_names += [(n, u, p) for p in range(2) for n in ((("dD", l), ("dDT", l)) if l < 5 else (("dDT", l),))]
                        act_names += [(("Z", l), u, p) for p in range(2)]
                        dve_names += [(n, u, p) for p in range(2) for n in ((("D", l), ("DT", l)) if l < 5 else (("DT", l),))]
                        pool_names += [(("M", l), u, p) for p in range(2)]
                    pe_names += [(n, u, p) for p in range(2) for n in ("A1", "U0")]
                    pe_names += [(n, u, p) for p in range(2) for n in ("Lrk", "Lrb")]
                    act_names += [(n, u, p) for p in range(2) for n in ("A1", "U0")]
                    dve_names += [(n, u, p) for p in range(2) for n in ("Lrk", "Lrb")]
                    for c in range(2):
                        if not first_chunk(T, c):
                            pe_names += [(("U", c), u, p) for p in range(2)] + [(("RS", c), u, p) for p in range(2)]
                            act_names += [(("RS", c), u, p) for p in range(2)]
                            dve_names += [(("U", c), u, p) for p in range(2)]
                        if not last_chunk(T, c):
                            pe_names += [(("S", c), u)]
                            dve_names += ([] if first_chunk(T, c) else [(("S1", c), u)]) + [(("S", c), u)]
                    pe_names += [("O", u)]
                    dve_names += [("O", u)]
                pe_names += [("nt", T)]
                act_names += [("sq", T), ("std", T), ("ln", T)]
                dve_names += [("sum", T), ("mean", T), ("cen", T), ("var", T), ("inv", T), ("normal", T)]
            pe_names += ["G"]
            act_names += ["hi"]
            dve_names += ["y", "yg"]
            pe_out.events(pe_names)
            act_out.events(act_names)
            dve_out.events(dve_names)
            pool_out.events(pool_names)

            with nc.Block() as block:
                @block.tensor
                def _(pe):
                    for T in range(NT):
                        tt = slice(T * P, (T + 1) * P)
                        if T:
                            pe.wait_ge(act_out.sem, act_out.at(("ln", T - 1)))
                        for i, src in enumerate((V, Q, K, BB)):
                            two = ps[:, 2 * i:2 * i + 2, :].rearrange("p b n -> p (b n)")
                            for m in range(MT6):
                                ins = pe.transpose(two[:, m * P:(m + 1) * P], src[:, m, tt], ident[:])
                            ins.then_inc(pe_out.up(("tr", T, i)), 1)
                        pe.wait_ge(act_out.sem, act_out.at(("tok", T, 1)))
                        pe.wait_ge(dve_out.sem, dve_out.at(("tok", T, 3)))
                        for hf in range(2):
                            u = (T, hf)
                            if hf:
                                pe.wait_ge(dve_out.sem, dve_out.at(("O", (T, 0))))
                            for p in range(2):
                                r = slice(p * HD, p * HD + HD)
                                for name, b, lhs, rhs in (("LbT", 0, BB, Q), ("Lb", 2, Q, BB), ("LkT", 4, K, Q)):
                                    for mm in range(3):
                                        m = 3 * hf + mm
                                        ins = pe.matmul(bank(b + p)[:, mm], lhs[r, m, tt], rhs[r, m, tt],
                                                        start=True, stop=True)
                                    ins.then_inc(pe_out.up((name, u, p)), 1)
                            for p in range(2):
                                pe.wait_ge(dve_out.sem, dve_out.at(("LkT", u, p)))
                                for mm in range(3):
                                    h = 2 * (3 * hf + mm) + p
                                    ins = pe.matmul(bank(6 + p, 3 * HD)[:, mm], Z[:, p, mm], Vt[:, h * HD:(h + 1) * HD],
                                                    start=True, stop=True)
                                ins.then_inc(pe_out.up(("LkV", u, p)), 1)
                            for l in LV:
                                for p in range(2):
                                    pe.wait_ge(pool_out.sem, pool_out.at((("M", l), u, p)))
                                    pe.wait_ge(dve_out.sem, dve_out.at((("D", l - 1), u, p)))
                                    for mm in range(3):
                                        ins = pe.matmul(bank(p)[:, mm], M[l % 2][:, p, mm], Dm[:, p, mm],
                                                        start=True, stop=True)
                                    ins.then_inc(pe_out.up((("Z", l), u, p)), 1)
                                for p in range(2):
                                    pe.wait_ge(act_out.sem, act_out.at((("Z", l), u, p)))
                                    made = dve_out if l > 1 else pool_out
                                    pe.wait_ge(made.sem, made.at((("DT", l - 1), u, p)))
                                    if l < 5:
                                        for mm in range(3):
                                            ins = pe.matmul(bank(2 + p)[:, mm], DT[:, p, mm], Z[:, p, mm],
                                                            start=True, stop=True)
                                        ins.then_inc(pe_out.up((("dD", l), u, p)), 1)
                                    for mm in range(3):
                                        ins = pe.matmul(bank(4 + p)[:, mm], Z[:, p, mm], DT[:, p, mm],
                                                        start=True, stop=True)
                                    ins.then_inc(pe_out.up((("dDT", l), u, p)), 1)
                            for p in range(2):
                                r = slice(p * HD, p * HD + HD)
                                pe.wait_ge(dve_out.sem, dve_out.at((("DT", 5), u, p)))
                                pe.wait_ge(act_out.sem, act_out.at(("LkV", u, p)))
                                for mm in range(3):
                                    h = 2 * (3 * hf + mm) + p
                                    ins = pe.matmul(bank(p)[r, mm], Qt[:, h * HD:(h + 1) * HD], DT[:, p, mm],
                                                    start=True, stop=True)
                                ins.then_inc(pe_out.up(("A1", u, p)), 1)
                                for mm in range(3):
                                    ins = pe.matmul(ps[:, 6 + p, 192 + mm * HD:192 + (mm + 1) * HD], DT[:, p, mm],
                                                    LkV[:, p, mm], start=True, stop=True)
                                ins.then_inc(pe_out.up(("U0", u, p)), 1)
                            for p in range(2):
                                r = slice(p * HD, p * HD + HD)
                                for name, b, lhs in (("Lrk", 2, K), ("Lrb", 4, BB)):
                                    for mm in range(3):
                                        m = 3 * hf + mm
                                        ins = pe.matmul(bank(b + p)[:, mm], lhs[r, m, tt], R[r, m, tt],
                                                        start=True, stop=True)
                                    ins.then_inc(pe_out.up((name, u, p)), 1)
                            for c in range(2):
                                rc = slice(c * CHUNK, (c + 1) * CHUNK)
                                if not first_chunk(T, c):
                                    for p in range(2):
                                        r = slice(p * HD, p * HD + HD)
                                        pe.wait_ge(act_out.sem, act_out.at(("U0", u, p)))
                                        pe.wait_ge(dve_out.sem, dve_out.at((("S", 0), u) if c else (("S", 1), (T - 1, hf))))
                                        for mm in range(3):
                                            ins = pe.matmul(bank(6 + p, 3 * HD)[rc, mm], A1[r, mm, rc],
                                                            S[r, 3 * hf + mm, :], start=True, stop=True)
                                        ins.then_inc(pe_out.up((("U", c), u, p)), 1)
                                    for p in range(2):
                                        r = slice(p * HD, p * HD + HD)
                                        if c:
                                            if not first_chunk(T, 0):
                                                pe.wait_ge(act_out.sem, act_out.at((("RS", 0), u, p)))
                                        for mm in range(3):
                                            m = 3 * hf + mm
                                            ins = pe.matmul(bank(p, 3 * HD)[rc, mm],
                                                            R[r, m, T * P + c * CHUNK:T * P + (c + 1) * CHUNK],
                                                            S[r, m, :], start=True, stop=True)
                                        ins.then_inc(pe_out.up((("RS", c), u, p)), 1)
                                if not last_chunk(T, c):
                                    for p in range(2):
                                        r = slice(p * HD, p * HD + HD)
                                        if first_chunk(T, c):
                                            pe.wait_ge(act_out.sem, act_out.at(("U0", u, p)))
                                        else:
                                            pe.wait_ge(dve_out.sem, dve_out.at((("U", c), u, p)))
                                        pe.wait_ge(dve_out.sem, dve_out.at(("Lrk", u, 0)))
                                        for mm in range(3):
                                            h = 2 * (3 * hf + mm) + p
                                            hc = slice(h * HD, (h + 1) * HD)
                                            pe.matmul(bank(2, 3 * HD)[r, mm], Kt[rc, hc], Vt[rc, hc],
                                                      start=True, stop=False)
                                            ins = pe.matmul(bank(2, 3 * HD)[r, mm], Bt[rc, hc], U[rc, p, mm],
                                                            start=False, stop=True)
                                    ins.then_inc(pe_out.up((("S", c), u)), 1)
                            for p in range(2):
                                pe.wait_ge(dve_out.sem, dve_out.at(("Lrb", u, p)))
                                pe.wait_ge(dve_out.sem, dve_out.at((("U", 1), u, p)))
                                for mm in range(3):
                                    h = 2 * (3 * hf + mm) + p
                                    o = ps[:, 3, (2 * mm + p) * HD:(2 * mm + p + 1) * HD]
                                    pe.matmul(o, M0[:, p, mm], Vt[:, h * HD:(h + 1) * HD], start=True, stop=False)
                                    ins = pe.matmul(o, M1[:, p, mm], U[:, p, mm], start=False, stop=True)
                            ins.then_inc(pe_out.up(("O", u)), 1)
                        pe.wait_ge(dve_out.sem, dve_out.at(("normal", T)))
                        two = ps[:, 0:2, :].rearrange("p b n -> p (b n)")
                        for m in range(MT6):
                            ins = pe.transpose(two[:, m * P:(m + 1) * P], O[:, m], ident[:])
                        ins.then_inc(pe_out.up(("nt", T)), 1)
                    for m in range(MT6):
                        ins = pe.matmul(ps[:, 4 + m // 2, (m % 2) * SEQ:(m % 2 + 1) * SEQ], g_up[:, m * P:(m + 1) * P],
                                        lowg, start=True, stop=True)
                    ins.then_inc(pe_out.up("G"), 1)

                @block.scalar
                def _(act):
                    for T in range(NT):
                        for i in range(2):
                            act.wait_ge(pe_out.sem, pe_out.at(("tr", T, i)))
                            two = ps[:, 2 * i:2 * i + 2, :].rearrange("p b n -> p (b n)")
                            act.activation(tok[i], two[:, 0:C], ACT.Copy).then_inc(act_out.up(("tok", T, i)), 1)
                        for hf in range(2):
                            u = (T, hf)
                            for p in range(2):
                                act.wait_ge(pe_out.sem, pe_out.at(("LbT", u, p)))
                                if units.index(u):
                                    prev = units[units.index(u) - 1]
                                    act.wait_ge(pool_out.sem, pool_out.at((("M", 5), prev, p)))
                                act.activation(LT[:, p], bank(p), ACT.Copy).then_inc(act_out.up(("LT", u, p)), 1)
                            for p in range(2):
                                act.wait_ge(pe_out.sem, pe_out.at(("LkV", u, p)))
                                act.activation(LkV[:, p], bank(6 + p, 3 * HD), ACT.Copy)\
                                    .then_inc(act_out.up(("LkV", u, p)), 1)
                            for l in LV:
                                for p in range(2):
                                    act.wait_ge(pe_out.sem, pe_out.at((("Z", l), u, p)))
                                    act.activation(Z[:, p], bank(p), ACT.Copy).then_inc(act_out.up((("Z", l), u, p)), 1)
                            for p in range(2):
                                r = slice(p * HD, p * HD + HD)
                                act.wait_ge(pe_out.sem, pe_out.at(("A1", u, 1) if p == 0 else ("A1", u, p)))
                                act.activation(A1[r], bank(p)[r], ACT.Copy).then_inc(act_out.up(("A1", u, p)), 1)
                                act.wait_ge(pe_out.sem, pe_out.at(("U0", u, p)))
                                act.activation(U[:, p], ps[:, 6 + p, 192:384].rearrange(
                     "p (m t) -> p m t", m=3), ACT.Copy).then_inc(act_out.up(("U0", u, p)), 1)
                            for c in range(2):
                                rc = slice(c * CHUNK, (c + 1) * CHUNK)
                                if not first_chunk(T, c):
                                    for p in range(2):
                                        act.wait_ge(pe_out.sem, pe_out.at((("RS", c), u, p)))
                                        if hf == 0:
                                            if T:
                                                act.wait_ge(act_out.sem, act_out.at(("ln", T - 1)))
                                            else:
                                                act.wait_ge(dve_out.sem, dve_out.at("zero"))
                                        act.activation(O[rc, 3 * hf:3 * hf + 3, p],
                                                       bank(p, 3 * HD)[rc], ACT.Copy)\
                                                           .then_inc(act_out.up((("RS", c), u, p)), 1)
                        act.wait_ge(dve_out.sem, dve_out.at(("cen", T)))
                        act.activation(M0.rearrange("p a b c -> p (a b c)"),
                                       O.rearrange("p m a d -> p (m a d)"), ACT.Square)\
                                           .then_inc(act_out.up(("sq", T)), 1)
                        act.wait_ge(dve_out.sem, dve_out.at(("var", T)))
                        act.activation(hs[2], hs[1], ACT.Sqrt, bias=eps[:, 2:3], scale=1.0 / HD)\
                            .then_inc(act_out.up(("std", T)), 1)
                        act.wait_ge(pe_out.sem, pe_out.at(("nt", T)))
                        two = ps[:, 0:2, :].rearrange("p b n -> p (b n)")
                        for m in range(MT6):
                            ins = act.activation(V[:, m, T * P:(T + 1) * P], two[:, m * P:(m + 1) * P], ACT.Identity,
                                                 bias=col("lnx_b", m), scale=col("lnx_g", m))
                        ins.then_inc(act_out.up(("ln", T)), 1)
                    act.wait_ge(dve_out.sem, dve_out.at("yg"))
                    act.activation(actT[:, 0, 0:MT6], V, ACT.Copy).then_inc(act_out.up("hi"), 1)

                @block.gpsimd
                def _(pool):
                    for T, hf in units:
                        u = (T, hf)
                        for p in range(2):
                            pool.wait_ge(act_out.sem, act_out.at(("LT", u, p)))
                            if units.index(u):
                                pool.wait_ge(pe_out.sem, pe_out.at(("U0", units[units.index(u) - 1], p)))
                            pool.tensor_tensor(DT[:, p], LT[:, p], bmask(level_mask[0]), ALU.mult)\
                                .then_inc(pool_out.up(("DT1", u, p)), 1)
                            pool.wait_ge(pool_out.sem, pool_out.at(("DT1", u, p)))
                            pool.tensor_tensor(DT[:, p], DT[:, p], bmask(ident[:]), ALU.add)\
                                .then_inc(pool_out.up((("DT", 0), u, p)), 1)
                        for l in LV:
                            for p in range(2):
                                if l > 2:
                                    pool.wait_ge(pe_out.sem, pe_out.at((("Z", l - 2), u, p)))
                                elif units.index(u):
                                    pool.wait_ge(pe_out.sem, pe_out.at(("O", units[units.index(u) - 1])))
                                    if hf == 0:
                                        pool.wait_ge(dve_out.sem, dve_out.at(("var", T - 1)))
                                pool.tensor_tensor(M[l % 2][:, p], LT[:, p], bmask(level_mask[l]),
                                                   ALU.mult).then_inc(pool_out.up((("M", l), u, p)), 1)

                @block.vector
                def _(dve):
                    dve.memset(O[0:CHUNK], 0.0).then_inc(dve_out.up("zero"), 1)
                    for T in range(NT):
                        for i in range(2, 4):
                            dve.wait_ge(pe_out.sem, pe_out.at(("tr", T, i)))
                            two = ps[:, 2 * i:2 * i + 2, :].rearrange("p b n -> p (b n)")
                            dve.tensor_copy(tok[i], two[:, 0:C]).then_inc(dve_out.up(("tok", T, i)), 1)
                        for hf in range(2):
                            u = (T, hf)
                            for p in range(2):
                                dve.wait_ge(pe_out.sem, pe_out.at(("Lb", u, p)))
                                dve.tensor_tensor(Dm[:, p], bank(2 + p), bmask(pair_mask), ALU.mult)\
                                    .then_inc(dve_out.up(("D1", u, p)), 1)
                                dve.wait_ge(dve_out.sem, dve_out.at(("D1", u, p)))
                                dve.tensor_tensor(Dm[:, p], Dm[:, p], bmask(ident[:]), ALU.add)\
                                    .then_inc(dve_out.up((("D", 0), u, p)), 1)
                                dve.wait_ge(pe_out.sem, pe_out.at(("LkT", u, p)))
                                if units.index(u) and p == 0:
                                    prev = units[units.index(u) - 1]
                                    dve.wait_ge(pe_out.sem, pe_out.at(("O", prev)))
                                dve.tensor_tensor(Z[:, p], bank(4 + p), bmask(below), ALU.mult)\
                                    .then_inc(dve_out.up(("LkT", u, p)), 1)
                            for l in LV:
                                for p in range(2):
                                    if l < 5:
                                        dve.wait_ge(pe_out.sem, pe_out.at((("dD", l), u, p)))
                                        dve.tensor_tensor(Dm[:, p], Dm[:, p], bank(2 + p), ALU.add)\
                                            .then_inc(dve_out.up((("D", l), u, p)), 1)
                                    dve.wait_ge(pe_out.sem, pe_out.at((("dDT", l), u, p)))
                                    dve.tensor_tensor(DT[:, p], DT[:, p], bank(4 + p), ALU.add)\
                                        .then_inc(dve_out.up((("DT", l), u, p)), 1)
                            for p in range(2):
                                for name, b, dst in (("Lrk", 2, M0), ("Lrb", 4, M1)):
                                    dve.wait_ge(pe_out.sem, pe_out.at((name, u, p)))
                                    dve.tensor_tensor(dst[:, p], bank(b + p), bmask(upto), ALU.mult)\
                                        .then_inc(dve_out.up((name, u, p)), 1)
                            Sh = S[:, 3 * hf:3 * hf + 3]
                            for c in range(2):
                                rc = slice(c * CHUNK, (c + 1) * CHUNK)
                                if not first_chunk(T, c):
                                    for p in range(2):
                                        dve.wait_ge(pe_out.sem, pe_out.at((("U", c), u, p)))
                                        dve.wait_ge(act_out.sem, act_out.at(("U0", u, p)))
                                        dve.tensor_tensor(U[rc, p], U[rc, p], bank(6 + p, 3 * HD)[rc],
                                                          ALU.add).then_inc(dve_out.up((("U", c), u, p)), 1)
                                if not last_chunk(T, c):
                                    dve.wait_ge(pe_out.sem, pe_out.at((("S", c), u)))
                                    w = w_end[:, 3 * hf:3 * hf + 3, 2 * T + c:2 * T + c + 1].to_broadcast([P, 3, HD])
                                    if first_chunk(T, c):
                                        ins = dve.tensor_tensor(Sh, bank(2, 3 * HD), w, ALU.mult)
                                    else:
                                        dve.tensor_tensor(Sh, Sh, bank(2, 3 * HD), ALU.add)\
                                            .then_inc(dve_out.up((("S1", c), u)), 1)
                                        dve.wait_ge(dve_out.sem, dve_out.at((("S1", c), u)))
                                        ins = dve.tensor_tensor(Sh, Sh, w, ALU.mult)
                                    ins.then_inc(dve_out.up((("S", c), u)), 1)
                            dve.wait_ge(pe_out.sem, pe_out.at(("O", u)))
                            dve.wait_ge(act_out.sem, act_out.at((("RS", 1), u, 1)))
                            Ou = Oh[:, 6 * hf:6 * hf + 6]
                            dve.tensor_tensor(Ou, Ou, ps[:, 3, 0:6 * HD].rearrange("p (h d) -> p h d", h=6),
                                              ALU.add).then_inc(dve_out.up(("O", u)), 1)
                        wide = lambda s: s.unsqueeze(2).to_broadcast([P, NH, HD])
                        dve.wait_ge(dve_out.sem, dve_out.at(("O", (T, 1))))
                        dve.tensor_reduce(hs[0], Oh, AX_X, ALU.add).then_inc(dve_out.up(("sum", T)), 1)
                        dve.wait_ge(dve_out.sem, dve_out.at(("sum", T)))
                        dve.tensor_scalar(hs[0], hs[0], 1.0 / HD, None, ALU.mult).then_inc(dve_out.up(("mean", T)), 1)
                        dve.wait_ge(dve_out.sem, dve_out.at(("mean", T)))
                        dve.tensor_tensor(Oh, Oh, wide(hs[0]), ALU.subtract).then_inc(dve_out.up(("cen", T)), 1)
                        dve.wait_ge(act_out.sem, act_out.at(("sq", T)))
                        dve.tensor_reduce(hs[1], M0.rearrange("p a b c -> p (a b c)").rearrange(
             "p (h d) -> p h d", h=NH), AX_X, ALU.add).then_inc(dve_out.up(("var", T)), 1)
                        dve.wait_ge(act_out.sem, act_out.at(("std", T)))
                        dve.reciprocal(hs[3], hs[2]).then_inc(dve_out.up(("inv", T)), 1)
                        dve.wait_ge(dve_out.sem, dve_out.at(("inv", T)))
                        dve.tensor_tensor(Oh, Oh, wide(hs[3]), ALU.mult).then_inc(dve_out.up(("normal", T)), 1)
                    dve.wait_ge(act_out.sem, act_out.at(("ln", NT - 1)))
                    dve.tensor_tensor(V, V, BON, ALU.add).then_inc(dve_out.up("y"), 1)
                    dve.wait_ge(pe_out.sem, pe_out.at("G"))
                    dve.wait_ge(dve_out.sem, dve_out.at("y"))
                    dve.tensor_tensor(V, V, ps[:, 4:7, :].rearrange("p b (m t) -> p (b m) t", m=2),
                                      ALU.mult).then_inc(dve_out.up("yg"), 1)
                    dve.wait_ge(act_out.sem, act_out.at("hi"))
                    dve_steps.step(dve, dve.tensor_tensor(actT[:, 1, 0:MT6], V, actT[:, 0, 0:MT6].bitcast(F32),
                                                          ALU.subtract))

        def stick_stages(take):
            W = SEQ + P
            QT, KT, Vt, mqT, sg, kp, later, attT = carve((MT6, SEQ), (MT6, SEQ), (NT, C), (2, SEQ),
                                                         (2, 2, W), (2, 2, W), (2, 2, W), (2, 2, W))
            mem_at = (2 * MT6 + 2) * SEQ + NT * C
            before, not_before = gate_m[:, 0:P], gate_m[:, P:2 * P]
            ones = gate_m[:, 2 * P:2 * P + SEQ]
            g0 = sec["sb_in"]
            act_at = [act_steps.n + 1 + c for c in range(10)]
            expect_input()
            with nc.Block() as block:
                @block.sync
                def _(sp):
                    for g in range(g0 + 2, g0 + 10 + 2):
                        ring_a.load(sp, g)

                @block.gpsimd
                def _(pool):
                    pool_steps.mark(pool.memset(ones, 1.0))
                    pool_steps.mark(pool.memset(before, 1.0))
                    pool_steps.step(pool, pool.memset(not_before, 1.0))
                    pool_steps.step(pool, pool.affine_select(out=before, in_=before, compare_op=ALU.is_gt, fill=0.0,
                                                             base=0, pattern=[[-1, P]], channel_multiplier=1))
                    pool_steps.step(pool, pool.affine_select(out=not_before, in_=not_before, compare_op=ALU.is_ge,
                                                             fill=0.0, base=0, pattern=[[1, P]], channel_multiplier=-1))

                @block.tensor
                def _(pe):
                    for c in range(10):
                        g = g0 + c
                        ring_a.wait_split(pe, g)
                        if c >= 8:
                            pe.wait_ge(act_steps.sem, act_at[c - 8])
                        for n in range(2):
                            for k in range(KD):
                                if c == 0 and n == 0:
                                    wait_input(pe, k)
                                out_ = ps[:, c % 8, n * SEQ:(n + 1) * SEQ]
                                if 6 <= c < 9:
                                    w = [ring_a.part(g, s, k * 256, k * 256 + 256) for s in range(2)]
                                    ins = mm3(pe, out_, [actT[:, s, k, n * P:(n + 1) * P] for s in range(2)], w,
                                              k == 0, k == KD - 1)
                                else:
                                    w = [ring_a.part(g, s, k * 256 + n * P, k * 256 + n * P + P) for s in range(2)]
                                    ins = mm3(pe, out_, w, [actT[:, s, k] for s in range(2)], k == 0, k == KD - 1)
                        ins.then_inc(ring_a.used, 1)

                @block.scalar
                def _(act):
                    take[0](act)
                    for c in range(1, 11):
                        if c < 10:
                            ring_a.split_hi(act, g0 + c)
                        i = c - 1
                        ring_a.wait_used(act, g0 + i)
                        src = ps[:, i % 8, :].rearrange("p (n t) -> p n t", n=2)
                        scale = HD ** -0.5 if i < 3 or i == 9 else 1.0
                        dst = (QT[:, 2 * i:2 * i + 2] if i < 3 else KT[:, 2 * i - 6:2 * i - 4] if i < 6 else
                               Vt[:, :, (i - 6) * 256:(i - 5) * 256] if i < 9 else mqT)
                        assert act_steps.mark(act.activation(dst, src, ACT.Copy, scale=scale)) == act_at[i]

                @block.vector
                def _(dve):
                    take[1](dve)
                    for c in range(1, 10):
                        ring_a.split_lo(dve, g0 + c)

            memory_attention(mqT, arena[:, mem_at:mem_at + 2048].rearrange("p (a b) -> p a b", a=8),
                             arena[:, mem_at + 2048:mem_at + 4096].rearrange("p (a b) -> p a b", a=8),
                             sec["w_out", 1])

            pe_out.events([("scores", 0)] + [e for m in range(MT6) for e in
                                             ([("scores", m + 1)] if m + 1 < MT6 else []) + [("attT", m), ("out", m)]])
            act_out.events([("sig", 0)] + [e for m in range(MT6) for e in
                                           ([("sig", m + 1)] if m + 1 < MT6 else []) + [("attT", m), ("hi", m)]])
            dve_out.events(["last"] + [e for m in range(MT6) for e in
                                       [("keep", m), ("later", m), ("att", m)] + ([("lo", m - 1)] if m else [])]
                           + [("lo", MT6 - 1)])
            pool_out.events([("sg", m) for m in range(MT6)])
            with nc.Block() as block:
                @block.tensor
                def _(pe):
                    def scores(m):
                        if m >= 2:
                            pe.wait_ge(dve_out.sem, dve_out.at(("lo", m - 2)))
                        for p in range(2):
                            r = slice(p * HD, p * HD + HD)
                            b = ps[:, 2 * (m % 2) + p, :]
                            pe.matmul(b[:, 0:SEQ], QT[r, m, P:SEQ], KT[r, m, :], start=True, stop=True)
                            ins = pe.matmul(b[:, SEQ:W], QT[r, m, 0:P], KT[r, m, 0:P], start=True, stop=True)
                        ins.then_inc(pe_out.up(("scores", m)), 1)

                    scores(0)
                    for m in range(MT6):
                        if m + 1 < MT6:
                            scores(m + 1)
                        pe.wait_ge(dve_out.sem, dve_out.at(("att", m)))
                        if m >= 2:
                            pe.wait_ge(act_out.sem, act_out.at(("attT", m - 2)))
                        for p in range(2):
                            for i in range(3):
                                ins = pe.transpose(ps[:, 4 + 2 * (m % 2) + p, i * P:(i + 1) * P],
                                                   later[:, m % 2, p, i * P:(i + 1) * P], ident[:])
                        ins.then_inc(pe_out.up(("attT", m)), 1)
                        pe.wait_ge(act_out.sem, act_out.at(("attT", m)))
                        for p in range(2):
                            r, h = slice(p * HD, p * HD + HD), 2 * m + p
                            v = [Vt[:, t, h * HD:(h + 1) * HD] for t in range(NT)]
                            a = attT[:, m % 2, p]
                            pe.matmul(ps[r, 2 * (m % 2), W:512], v[0], a[:, SEQ:W], start=True, stop=True)
                            pe.matmul(ps[r, 2 * (m % 2) + 1, W:512], v[0], a[:, 0:P], start=True, stop=False)
                            ins = pe.matmul(ps[r, 2 * (m % 2) + 1, W:512], v[1], a[:, P:SEQ], start=False, stop=True)
                        ins.then_inc(pe_out.up(("out", m)), 1)

                @block.scalar
                def _(act):
                    def sigmoids(m):
                        b = 2 * (m % 2)
                        act.wait_ge(pe_out.sem, pe_out.at(("scores", m)))
                        if m >= 2:
                            act.wait_ge(dve_out.sem, dve_out.at(("att", m - 2)))
                        act.activation(kp[:, m % 2], ps[:, b:b + 2, 0:W], ACT.Sigmoid, scale=-1.0)
                        act.activation(sg[:, m % 2], ps[:, b:b + 2, 0:W], ACT.Sigmoid)\
                            .then_inc(act_out.up(("sig", m)), 1)

                    sigmoids(0)
                    for m in range(MT6):
                        if m + 1 < MT6:
                            sigmoids(m + 1)
                        act.wait_ge(pe_out.sem, pe_out.at(("attT", m)))
                        b = 4 + 2 * (m % 2)
                        act.activation(attT[:, m % 2], ps[:, b:b + 2, 0:W], ACT.Copy)\
                            .then_inc(act_out.up(("attT", m)), 1)
                        act.wait_ge(pe_out.sem, pe_out.at(("out", m)))
                        b = 2 * (m % 2)
                        act.activation(actT[:, 0, m].rearrange("p (t n) -> p t n", t=NT),
                                       ps[:, b:b + 2, W:512], ACT.Copy).then_inc(act_out.up(("hi", m)), 1)

                @block.gpsimd
                def _(pool):
                    for m in range(MT6):
                        pool.wait_ge(act_out.sem, act_out.at(("sig", m)))
                        diag = sg[:, m % 2, :, P:W]
                        for p in range(2):
                            d = diag[:, p].rearrange("p (a s) -> p a s", a=2)
                            ins = pool.tensor_tensor(d, d, before.unsqueeze(1).to_broadcast([P, 2, P]), ALU.mult)
                        ins.then_inc(pool_out.up(("sg", m)), 1)

                @block.vector
                def _(dve):
                    dve.memset(later[:, :, :, SEQ - 1:W:P], 1.0).then_inc(dve_out.up("last"), 1)
                    dve.wait_ge(dve_out.sem, dve_out.at("last"))

                    def lo(m):
                        dve.wait_ge(act_out.sem, act_out.at(("hi", m)))
                        b = 2 * (m % 2)
                        two = lambda ap: ap.rearrange("p (t n) -> p t n", t=NT)
                        dve.tensor_tensor(two(actT[:, 1, m]), ps[:, b:b + 2, W:512],
                                          two(actT[:, 0, m].bitcast(F32)), ALU.subtract)\
                                              .then_inc(dve_out.up(("lo", m)), 1)

                    for m in range(MT6):
                        q = m % 2
                        dve.wait_ge(act_out.sem, act_out.at(("sig", m)))
                        for p in range(2):
                            d = kp[:, q, p, P:W].rearrange("p (a s) -> p a s", a=2)
                            ins = dve.tensor_tensor(d, d, not_before.unsqueeze(1).to_broadcast([P, 2, P]), ALU.max)
                        ins.then_inc(dve_out.up(("keep", m)), 1)
                        dve.wait_ge(dve_out.sem, dve_out.at(("keep", m)))
                        if m >= 2:
                            dve.wait_ge(pe_out.sem, pe_out.at(("attT", m - 2)))
                            dve_steps.step(dve, dve.memset(later[:, q, :, SEQ - 1:W:P], 1.0))
                        for p in range(2):
                            for a, b in ((0, SEQ), (SEQ, W)):
                                ins = dve.tensor_tensor_scan(later[:, q, p, a:b - 1][:, ::-1],
                                                             kp[:, q, p, a + 1:b][:, ::-1], ones[:, 0:b - a - 1],
                                                             1.0, ALU.mult, ALU.mult)
                        ins.then_inc(dve_out.up(("later", m)), 1)
                        dve.wait_ge(dve_out.sem, dve_out.at(("later", m)))
                        dve.wait_ge(pool_out.sem, pool_out.at(("sg", m)))
                        dve.tensor_tensor(later[:, q], later[:, q], sg[:, q], ALU.mult)\
                            .then_inc(dve_out.up(("att", m)), 1)
                        if m:
                            lo(m - 1)
                    lo(MT6 - 1)

        def norm_rows(i, n):
            return A["ln_g_2"][i, n], A["ln_b_2"][i, n]

        take = ffn_stage("ffn", True, None, True, sec["ffn1", 0], sec[("ffn1", 0), "B"], take_modulated())
        take = ffn_stage(("ffn1", 0), False, norm_rows(0, 0), True, sec["rwkv_in"], sec[("ffn2", 0), "B"], take)
        rwkv_stages(take)
        take = output_stage(0)
        take = ffn_stage(("ffn2", 0), False, norm_rows(0, 2), True, sec["ffn1", 1], sec[("ffn1", 1), "B"], take)
        take = ffn_stage(("ffn1", 1), False, norm_rows(1, 0), True, sec["sb_in"], sec[("ffn2", 1), "B"], take)
        stick_stages(take)
        take = output_stage(1)
        ffn_stage(("ffn2", 1), False, norm_rows(1, 2), False, len(chunks_a), len(chunks_b), take)

        with nc.Block() as block:
            @block.sync
            def _(sp):
                sp.dma_start(out[0].rearrange("(t p) d -> p t d", p=P), x_tok[:]).then_inc(rows_loaded, 16)
                sp.wait_ge(rows_loaded, rows_count[0] + 16)


INPUTS = ["x", "c", "mod_w", "mod_b", "norm_pre_mix", "norm_post_mix", "norm_pre_ffn", "norm_post_ffn", "a_pw1_w",
          "a_pw1_b", "a_dw_w", "a_dw_b", "a_ln_g", "a_ln_b", "a_pw2_w", "a_pw2_b", "f_up_w", "f_dw_w", "f_dw_b",
          "f_down_w", "mem_2", "ffn1_w_gate_2", "ffn1_w_up_2", "ffn1_w_down_2", "ffn2_w_gate_2", "ffn2_w_up_2",
          "ffn2_w_down_2", "ln_g_2", "ln_b_2", "w_out_2", "w_mem_kv_2", "rwkv_w_in_2", "rwkv_mu_2", "rwkv_w0_2",
          "rwkv_w_up_2", "rwkv_a0_2", "rwkv_a_up_2", "rwkv_g_up_2", "rwkv_k_k_2", "rwkv_k_a_2", "rwkv_r_k_2",
          "rwkv_lnx_g_2", "rwkv_lnx_b_2", "sb_w_in_2"]


def kernel(**inputs):
    import numpy as np
    import concourse.bacc as bacc
    from concourse.bass_utils import run_bass_kernel_spmd

    nc = bacc.Bacc("TRN2", target_bir_lowering=False, num_devices=1)
    arrays, aps = {}, {}
    for name in INPUTS:
        a = np.ascontiguousarray(inputs[name])
        arrays[f"in_{name}"] = a
        aps[name] = nc.dram_tensor(f"in_{name}", a.shape, mybir.dt.from_np(a.dtype), kind="ExternalInput").ap()
    out = nc.dram_tensor("out_x", (1, SEQ, D), F32, kind="ExternalOutput").ap()
    build_program(nc, aps, out)
    return run_bass_kernel_spmd(nc, [arrays], core_ids=[0]).results[0]["out_x"]
```

```python
import math
from contextlib import ExitStack

import concourse.bass as bass
from concourse import mybir

F32 = mybir.dt.float32
F32R = mybir.dt.float32r
ALU = mybir.AluOpType
ACT = mybir.ActivationFunctionType
AX_X = mybir.AxisListType.X

P = 128
SEQ, D, DFF = 256, 1024, 2816
NT = SEQ // P
KD = D // P
NF = DFF // P
CONVW, FCONVW = 31, 3
PAD = CONVW - 1
C = 768
MT6 = C // P
HD = 64
NH, NMH = C // HD, 4
NMEM = 256
CHUNK = 64
ALPHA = 4.0 ** 0.25
DECAY = math.exp(-0.5)
RMS_EPS, LN_EPS, LNX_EPS = 1e-6, 1e-5, 64e-5
MOD_COLS = 256
MOD_SLOTS = 6
MOD_LATE = 4
RWKV_ORDER = [3, 4, 5, 9, 0, 1, 2, 6, 7, 8]
ACH, BCH = 2048, 1024


class Signal:

    def __init__(self, sem):
        self.sem, self.total, self.count, self.todo = sem, 0, {}, []

    def events(self, names):
        assert not self.todo, self.todo
        self.todo = list(names)
        self.count = {n: self.total + i + 1 for i, n in enumerate(self.todo)}
        self.total += len(self.todo)
        assert len(self.count) == len(self.todo)

    def up(self, name):
        assert self.todo and self.todo[0] == name, (self.todo[:1], name)
        self.todo.pop(0)
        return self.sem

    def at(self, name):
        return self.count[name]


class Steps:

    def __init__(self, sem):
        self.sem, self.n = sem, 0

    def mark(self, ins):
        self.n += 1
        ins.then_inc(self.sem, 1)
        return self.n

    def step(self, eng, ins):
        self.mark(ins)
        eng.wait_ge(self.sem, self.n)


class Ring:

    def __init__(self, raw, parts, sems, chunks):
        self.raw, self.parts, self.chunks = raw, parts, chunks
        self.loaded, self.hi_done, self.lo_done, self.used = sems
        self.load_no, loads = [], [0, 0]
        for g, dmas in enumerate(chunks):
            loads[g % 2] += 16 * len(dmas)
            self.load_no.append(loads[g % 2])

    def load(self, sp, g):
        if g >= len(self.chunks):
            return
        if g >= 2:
            sp.wait_ge(self.lo_done, g - 1)
        for cols, view, src in self.chunks[g]:
            dst = self.raw[:, g % 2, cols[0]:cols[1]]
            sp.dma_start(dst.rearrange(view[0], **view[1]) if view else dst, src).then_inc(self.loaded[g % 2], 16)

    def split_hi(self, act, g):
        act.wait_ge(self.loaded[g % 2], self.load_no[g])
        if g >= 2:
            act.wait_ge(self.used, g - 1)
        act.activation(self.parts[:, g % 2, 0], self.raw[:, g % 2], ACT.Copy).then_inc(self.hi_done, 1)

    def split_lo(self, dve, g):
        dve.wait_ge(self.hi_done, g + 1)
        dve.tensor_tensor(self.parts[:, g % 2, 1], self.raw[:, g % 2], self.parts[:, g % 2, 0].bitcast(F32),
                          ALU.subtract).then_inc(self.lo_done, 1)

    def wait_split(self, pe, g):
        pe.wait_ge(self.lo_done, g + 1)

    def wait_used(self, eng, g):
        eng.wait_ge(self.used, g + 1)

    def part(self, g, which, lo, hi):
        return self.parts[:, g % 2, which, lo:hi]


def mm3(pe, out, lhs, rhs, start, stop):
    pe.matmul(out, lhs[0], rhs[0], start=start, stop=False)
    pe.matmul(out, lhs[0], rhs[1], start=False, stop=False)
    return pe.matmul(out, lhs[1], rhs[0], start=False, stop=stop)


def param_columns(A):
    def rows(ap):
        return ap.rearrange("(r p) -> r p", p=P)

    parts = [("c", rows(A["c"][0])), ("norm_pre_mix", rows(A["norm_pre_mix"][0])),
             ("norm_pre_ffn", rows(A["norm_pre_ffn"][0])), ("a_pw1_b", rows(A["a_pw1_b"][0])),
             ("a_dw_b", rows(A["a_dw_b"][0])), ("a_ln_g", rows(A["a_ln_g"][0])), ("a_ln_b", rows(A["a_ln_b"][0])),
             ("mod_sh_m", rows(A["mod_b"][0, 0:D])), ("mod_sc_m", rows(A["mod_b"][0, D:2 * D])),
             ("mod_sh_f", rows(A["mod_b"][0, 3 * D:4 * D])), ("mod_sc_f", rows(A["mod_b"][0, 4 * D:5 * D]))]
    parts += [("a_dw_w", A["a_dw_w"][0].rearrange("k (r p) -> (k r) p", p=P))]
    parts += [("f_dw_w", A["f_dw_w"][0].rearrange("k (r p) -> (k r) p", p=P)), ("f_dw_b", rows(A["f_dw_b"][0])),
              ("mu", rows(A["rwkv_mu_2"][0]))]
    for n in ("w0", "a0", "k_k", "k_a"):
        parts.append((n, rows(A[f"rwkv_{n}_2"][0])))
    parts.append(("r_k", A["rwkv_r_k_2"][0].rearrange("(a b) d -> a (b d)", b=2)))
    parts += [("lnx_g", rows(A["rwkv_lnx_g_2"][0])), ("lnx_b", rows(A["rwkv_lnx_b_2"][0]))]
    at, first, loads = 0, {}, []
    for name, view in parts:
        first[name] = at
        n, done = view.shape[0], 0
        while done < n:
            m = min(n - done, P - at % P)
            loads.append((at // P, at % P, m, view[done:done + m, :]))
            done, at = done + m, at + m
    return first, loads, at


def weight_chunks(A):
    ring_a, ring_b, first = [], [], {}

    def up(name, w, cols):
        first[name] = len(ring_a)
        v = w.rearrange("(k p) n -> p k n", p=P)
        for ranges in cols:
            at, dmas = 0, []
            for a, b in ranges:
                dmas.append(((at, at + KD * (b - a)), ("p (k n) -> p k n", {"k": KD}), v[:, :, a:b]))
                at += KD * (b - a)
            ring_a.append(dmas)

    def rows2(name, w):
        first[name] = len(ring_a)
        for c in range(KD // 2):
            src = w[2 * c * P:(2 * c + 2) * P, :].rearrange("(k p) n -> p k n", p=P)
            ring_a.append([((0, ACH), ("p (k n) -> p k n", {"k": 2}), src)])

    def ffn(name, gate, up_w, down):
        first[name] = len(ring_a)
        first[name, "B"] = len(ring_b)
        g, u = (w.rearrange("(k p) n -> p k n", p=P) for w in (gate, up_w))
        for i in range(NF):
            ring_a.append([((0, BCH), ("p (k n) -> p k n", {"k": KD}), g[:, :, i * P:(i + 1) * P]),
                           ((BCH, ACH), ("p (k n) -> p k n", {"k": KD}), u[:, :, i * P:(i + 1) * P])])
            ring_b.append([((0, BCH), None, down[i * P:(i + 1) * P, :])])

    wide = lambda n: [[(256 * c, 256 * c + 256)] for c in range(n)]
    up("mem_kv", A["w_mem_kv_2"], wide(2))
    up("pw1", A["a_pw1_w"][0], [[(j * P, j * P + P), (D + j * P, D + j * P + P)] for j in range(KD)])
    rows2("pw2", A["a_pw2_w"][0])
    ffn("ffn", A["f_up_w"][0][:, 0:DFF], A["f_up_w"][0][:, DFF:2 * DFF], A["f_down_w"][0])
    for i in range(2):
        ffn(("ffn1", i), A["ffn1_w_gate_2"][i], A["ffn1_w_up_2"][i], A["ffn1_w_down_2"][i])
        if i == 0:
            w = A["rwkv_w_in_2"][0]
            up("rwkv_in", w, [[(2560, 2688)], [(2688, 2816)]] + [wide(10)[i] for i in RWKV_ORDER])
        else:
            up("sb_in", A["sb_w_in_2"][0], wide(10)[9:] + wide(10)[:9])
        rows2(("w_out", i), A["w_out_2"][i])
        ffn(("ffn2", i), A["ffn2_w_gate_2"][i], A["ffn2_w_up_2"][i], A["ffn2_w_down_2"][i])
    return ring_a, ring_b, first


def build_program(nc, A, out):
    with ExitStack() as ctx:
        def sb(name, shape, dt=F32):
            return ctx.enter_context(nc.sbuf_tensor(name, shape, dt))

        def sem(name):
            return ctx.enter_context(nc.semaphore(name))

        def signal(name):
            return Signal(sem(name))

        a_raw, a_parts = sb("a_raw", [P, 2, ACH]), sb("a_parts", [P, 2, 2, ACH], F32R)
        b_raw, b_parts = sb("b_raw", [P, 2, BCH]), sb("b_parts", [P, 2, 2, BCH], F32R)
        x_tok = sb("x_tok", [P, NT, D])
        actT = sb("actT", [P, 2, KD, SEQ], F32R)
        hid = sb("hid", [P, 2, 2, SEQ], F32R)
        gate_m, gate_f = sb("gate_m", [P, D]), sb("gate_f", [P, D])
        rows = sb("rows", [P, 2, D])
        memkT = sb("memkT", [P, 2, NMEM])
        memv = sb("memv", [P, 2, 256])
        ident = sb("ident", [P, P])
        ones_mean = sb("ones_mean", [P, P])
        head_ones = sb("head_ones", [P, P])
        mod_cols = sb("mod_cols", [P, 4, KD])
        eps = sb("eps", [P, 3])
        stats = sb("stats", [P, NT, 16])
        small = sb("small", [P, 112])
        first_col, param_loads, n_params = param_columns(A)
        par = sb("par", [P, n_params])
        arena_words = nc.sbuf_bytes_remaining // 4 - 16
        arena = sb("arena", [P, arena_words])
        ps = ctx.enter_context(nc.psum_tensor("ps", [P, 8, 512], F32))

        def carve(*shapes, limit=arena_words):
            at, got = 0, []
            for shape in shapes:
                n = math.prod(shape)
                ap = arena[:, at:at + n]
                if len(shape) == 2:
                    ap = ap.rearrange("p (a b) -> p a b", a=shape[0])
                elif len(shape) == 3:
                    ap = ap.rearrange("p (a b c) -> p a b c", a=shape[0], b=shape[1])
                got.append(ap)
                at += n
            assert at <= limit, (at, limit)
            return got

        def col(name, i=0):
            return par[:, first_col[name] + i:first_col[name] + i + 1]

        def cols(name, n):
            return par[:, first_col[name]:first_col[name] + n]

        turned = ps[:, 4:8, :].rearrange("p b (k t) -> p (b k) t", k=2)
        turned_tok = ps[:, 4:8, :].rearrange("p (t b) (k n) -> p t (b k) n", t=NT, k=4)
        acc = [ps[:, 2 * t:2 * t + 2, :].rearrange("p b n -> p (b n)") for t in range(NT)]

        chunks_a, chunks_b, sec = weight_chunks(A)
        ring_a = Ring(a_raw, a_parts, ([sem("a_loaded0"), sem("a_loaded1")], sem("a_hi_done"), sem("a_lo_done"),
                                       sem("a_used")), chunks_a)
        ring_b = Ring(b_raw, b_parts, ([sem("b_loaded0"), sem("b_loaded1")], sem("b_hi_done"), sem("b_lo_done"),
                                       sem("b_used")), chunks_b)
        dve_steps, act_steps, pool_steps = Steps(sem("dve_steps")), Steps(sem("act_steps")), Steps(sem("pool_steps"))
        params_loaded = sem("params_loaded")
        rows_loaded = sem("rows_loaded")
        rows_count = [0]
        turned_done = signal("turned_done")
        turned_read = signal("turned_read")
        stat_ready, stat_root = signal("stat_ready"), signal("stat_root")
        input_hi, input_lo = signal("input_hi"), signal("input_lo")
        acc_ready = signal("acc_ready")
        mem_pe, mem_act, mem_dve = signal("mem_pe"), signal("mem_act"), signal("mem_dve")
        norm_pe, norm_act, norm_dve = signal("norm_pe"), signal("norm_act"), signal("norm_dve")
        pe_out, pe_in = signal("pe_out"), signal("pe_in")
        act_out, dve_out = signal("act_out"), signal("dve_out")
        pool_out = signal("pool_out")

        def load_row(eng, slot, vec):
            eng.dma_start(rows[:, slot], vec.partition_broadcast(P)).then_inc(rows_loaded, 16)


        def loads(sp, name, n_a, n_b=0):
            for g in range(sec[name] + 2, sec[name] + 2 + n_a):
                ring_a.load(sp, g)

        def rms_scale(act, dve, t, scratch):
            if act is not None:
                act_steps.step(act, act.activation(scratch[:, t], x_tok[:, t], ACT.Square,
                                                   accum_out=stats[:, t, 0:1]))
                act.activation(stats[:, t, 1:2], stats[:, t, 0:1], ACT.Sqrt, bias=eps[:, 0:1],
                               scale=1.0 / D).then_inc(act_out.up(("root", t)), 1)
            if dve is not None:
                dve.wait_ge(act_out.sem, act_out.at(("root", t)))
                dve_steps.step(dve, dve.reciprocal(stats[:, t, 2:3], stats[:, t, 1:2]))
                dve.tensor_scalar(scratch[:, t], x_tok[:, t], stats[:, t, 2:3], None, ALU.mult)\
                    .then_inc(dve_out.up(("xn", t)), 1)

        def turn(pe, src, t, k0=0, k1=KD):
            for k in range(k0, k1):
                ins = pe.transpose(turned[:, k, t * P:(t + 1) * P], src[:, t, k * P:(k + 1) * P], ident[:])
            ins.then_inc(turned_done.up(t), 1)

        def affine(act, hT, shift):
            for h in range(2):
                for k in range(4 * h, 4 * h + 4):
                    ins = act.activation(hT[:, k], turned[:, k], ACT.Identity, bias=mod_cols[:, shift, k:k + 1],
                                         scale=mod_cols[:, shift + 1, k:k + 1])
                ins.then_inc(input_hi.up(h), 1)

        def split_affine(dve, hT):
            for h in range(2):
                dve.wait_ge(input_hi.sem, input_hi.at(h))
                half = slice(4 * h, 4 * h + 4)
                dve_steps.step(dve, dve.tensor_copy(actT[:, 0, half], hT[:, half]))
                dve.tensor_tensor(actT[:, 1, half], hT[:, half], actT[:, 0, half].bitcast(F32), ALU.subtract)\
                    .then_inc(input_lo.up(h), 1)

        X_PARTS = [(0, 0, KD), (1, 0, KD // 2), (1, KD // 2, KD)]

        def turn_x_pe(pe):
            for part in X_PARTS:
                t, k0, k1 = part
                pe.wait_ge(dve_out.sem, dve_out.at(("x", part)))
                for k in range(k0, k1):
                    ins = pe.transpose(turned_tok[:, t, k], x_tok[:, t, k * P:(k + 1) * P], ident[:])
                ins.then_inc(turned_done.up(part), 1)

        def first_hi(act):
            act.wait_ge(turned_done.sem, turned_done.at(X_PARTS[0]))
            act.activation(actT[:, 0, :, 0:P], turned_tok[:, 0], ACT.Copy).then_inc(act_out.up("hi"), 1)

        def first_lo(dve):
            dve.wait_ge(act_out.sem, act_out.at("hi"))
            dve_steps.step(dve, dve.tensor_tensor(actT[:, 1, :, 0:P], turned_tok[:, 0],
                                                  actT[:, 0, :, 0:P].bitcast(F32), ALU.subtract))

        def take_x():
            turned_at = [turned_done.at(part) for part in X_PARTS[1:]]

            def on_act(act):
                for h in range(2):
                    act.wait_ge(turned_done.sem, turned_at[h])
                    act.activation(actT[:, 0, 4 * h:4 * h + 4, P:SEQ], turned_tok[:, 1, 4 * h:4 * h + 4],
                                   ACT.Copy).then_inc(input_hi.up(h), 1)

            def on_dve(dve):
                for h in range(2):
                    dve.wait_ge(input_hi.sem, input_hi.at(h))
                    dve.tensor_tensor(actT[:, 1, 4 * h:4 * h + 4, P:SEQ], turned_tok[:, 1, 4 * h:4 * h + 4],
                                      actT[:, 0, 4 * h:4 * h + 4, P:SEQ].bitcast(F32),
                                      ALU.subtract).then_inc(input_lo.up(h), 1)
            return on_act, on_dve

        def wait_input(pe, k):
            if k % 4 == 0:
                pe.wait_ge(input_lo.sem, input_lo.at(k // 4))

        def expect_input():
            input_hi.events([0, 1])
            input_lo.events([0, 1])

        def mod_chunk(pe, weights, lhs, out_, n=KD):
            for k in range(n):
                ins = pe.matmul(out_, lhs(k), weights[:, k * MOD_COLS:(k + 1) * MOD_COLS], start=k == 0,
                                stop=k == KD - 1)
            return ins

        def one_row(k):
            return csilu[:, k:k + 1]

        def to_columns(pe, mod_row, h):
            for j in range(KD * h, KD * h + KD):
                ins = pe.matmul(ps[:, 0, j:j + 1], mod_row[0:1, j * P:(j + 1) * P], ones_col[0:1], start=True,
                                stop=True)
            return ins

        def mod_finish(dve, shift, names, norm):
            sh, scl = names
            dve_steps.mark(dve.tensor_tensor(mod_cols[:, shift], ps[:, 0, 0:KD], cols(sh, KD), ALU.add))
            dve_steps.step(dve, dve.tensor_tensor(mod_cols[:, shift + 1], ps[:, 0, KD:2 * KD], cols(scl, KD),
                                                  ALU.add))
            dve.scalar_tensor_tensor(mod_cols[:, shift + 1], mod_cols[:, shift + 1], 1.0,
                                     cols(norm, KD), ALU.add, ALU.mult).then_inc(dve_out.up("mod"), 1)

        slots_at = arena_words - MOD_SLOTS * ACH
        mod_slots = arena[:, slots_at:arena_words].rearrange("p (s n) -> p s n", s=MOD_SLOTS)
        late_slots, late_at = mod_slots[:, MOD_SLOTS - MOD_LATE:], arena_words - MOD_LATE * ACH
        cb, prow, tokmem, scratch = carve((KD, P), (5, P), (NT, D), (NT, D), limit=slots_at)
        csilu, csig = small[:, 0:KD], small[:, KD:2 * KD]
        ones_col = small[:, 50:51]
        mod_row = scratch.rearrange("p t d -> p (t d)")
        n_rows = (n_params + P - 1) // P
        g0 = sec["mem_kv"]
        N_MIX = 2 * D // MOD_COLS
        MOD_PE = 3
        mix_w = [mod_slots[:, c] for c in range(MOD_SLOTS)] + [rows[:].rearrange("p a b -> p (a b)"),
                                                               b_raw[:].rearrange("p a b -> p (a b)")]
        sums = [g[:, c * MOD_COLS:(c + 1) * MOD_COLS] for g in (gate_m, gate_f) for c in range(N_MIX // 2)]
        mix_loaded = [sem(f"mix_loaded{c}") for c in range(N_MIX)]
        x_loaded, mem_loaded = sem("x_loaded"), sem("mem_loaded")
        mod_v = A["mod_w"][0].rearrange("(k p) n -> p k n", p=P)

        def load_mod(eng, dst, c, done):
            eng.dma_start(dst.rearrange("p (k n) -> p k n", k=KD), mod_v[:, :, c * MOD_COLS:(c + 1) * MOD_COLS])\
               .then_inc(done, 16)

        turned_done.events(["mem", 0, 1])
        pe_out.events(["params", "shift", "scale", "columns"])
        act_out.events([("root", 0), ("root", 1), "memT0", "memT1", "csig", "memkT", "memv", "shift", "scale"])
        dve_out.events([("xn", 0), ("xn", 1), "memT", "params", "csilu"] + [("sum", c) for c in range(N_MIX)]
                       + ["mod"])

        with nc.Block() as block:
            @block.sync
            def _(sp):
                sp.dma_start(x_tok[:], A["x"][0].rearrange("(t p) d -> p t d", p=P)).then_inc(x_loaded, 16)
                sp.dma_start(tokmem, A["mem_2"][0].rearrange("(t p) d -> p t d", p=P)).then_inc(mem_loaded, 16)
                ring_a.load(sp, g0)
                ring_a.load(sp, g0 + 1)
                for t, r, m, view in param_loads:
                    sp.dma_start(prow[r:r + m, t, :], view).then_inc(params_loaded, 16)
                for c in range(N_MIX):
                    load_mod(sp, mix_w[c], c, mix_loaded[c])
                for g in range(2, 4):
                    ring_a.load(sp, g0 + g)

            @block.gpsimd
            def _(pool):
                pool_steps.step(pool, pool.memset(ident[:], 0.0))
                pool_steps.step(pool, pool.affine_select(out=ident[:], in_=ident[:], compare_op=ALU.not_equal, fill=1.0,
                                                         base=0, pattern=[[-1, P]], channel_multiplier=1))
                for i, v in enumerate((RMS_EPS, LN_EPS, LNX_EPS)):
                    pool_steps.step(pool, pool.memset(eps[:, i:i + 1], v))
                pool_steps.step(pool, pool.memset(ones_mean[:], 1.0 / D))
                pool_steps.step(pool, pool.memset(ones_col, 1.0))
                pool_steps.step(pool, pool.memset(head_ones[:], 0.0))
                for h in range(2):
                    pool_steps.step(pool, pool.memset(head_ones[h * HD:(h + 1) * HD, h * HD:(h + 1) * HD], 1.0))
            constants = pool_steps.n

            @block.scalar
            def _(act):
                act.wait_ge(pool_steps.sem, constants)
                act.wait_ge(x_loaded, 16)
                rms_scale(act, None, 0, scratch)
                rms_scale(act, None, 1, scratch)
                act.wait_ge(turned_done.sem, turned_done.at("mem"))
                for h in range(2):
                    act.activation(actT[:, 0, 4 * h:4 * h + 4, :], turned[:, 4 * h:4 * h + 4, :],
                                   ACT.Copy).then_inc(act_out.up(f"memT{h}"), 1)
                for g in range(g0, g0 + 2):
                    ring_a.split_hi(act, g)
                act.wait_ge(dve_out.sem, dve_out.at("params"))
                act.activation(csig, cols("c", KD), ACT.Sigmoid).then_inc(act_out.up("csig"), 1)
                ring_a.wait_used(act, g0)
                act.activation(memkT[:], ps[:, 1, :].rearrange("p (n m) -> p n m", n=2), ACT.Copy)\
                    .then_inc(act_out.up("memkT"), 1)
                ring_a.wait_used(act, g0 + 1)
                act.activation(memv[:], ps[:, 2, :].rearrange("p (n m) -> p n m", n=2), ACT.Copy)\
                    .then_inc(act_out.up("memv"), 1)
                ring_a.split_hi(act, sec["pw1"])
                for h, name in enumerate(("shift", "scale")):
                    act.wait_ge(pe_out.sem, pe_out.at(name))
                    act.activation(mod_row[0:1, h * D:(h + 1) * D], acc[h][0:1, :], ACT.Copy)\
                        .then_inc(act_out.up(name), 1)

            @block.tensor
            def _(pe):
                pe.wait_ge(pool_steps.sem, constants)
                pe.wait_ge(mem_loaded, 16)
                for t in range(NT):
                    for k in range(KD):
                        ins = pe.transpose(turned[:, k, t * P:(t + 1) * P], tokmem[:, t, k * P:(k + 1) * P], ident[:])
                ins.then_inc(turned_done.up("mem"), 1)
                pe.wait_ge(dve_out.sem, dve_out.at("memT"))
                ring_a.wait_split(pe, g0)
                for n in range(2):
                    for k in range(KD):
                        w = [ring_a.part(g0, s, k * 256 + n * P, k * 256 + n * P + P) for s in range(2)]
                        ins = mm3(pe, ps[:, 1, n * NMEM:(n + 1) * NMEM], w, [actT[:, s, k, :] for s in range(2)],
                                  k == 0, k == KD - 1)
                ins.then_inc(ring_a.used, 1)
                pe.wait_ge(params_loaded, 16 * len(param_loads))
                for i in range(n_rows):
                    n = min(P, n_params - i * P)
                    ins = pe.transpose(ps[:, 3 * (i // 4), (i % 4) * P:(i % 4) * P + n], prow[0:n, i, :],
                                       ident[0:n, 0:n])
                ins.then_inc(pe_out.up("params"), 1)
                ring_a.wait_split(pe, g0 + 1)
                for t in range(2):
                    for k in range(KD):
                        w = [ring_a.part(g0 + 1, s, k * 256, k * 256 + 256) for s in range(2)]
                        ins = mm3(pe, ps[:, 2, t * 256:(t + 1) * 256],
                                  [actT[:, s, k, t * P:(t + 1) * P] for s in range(2)], w, k == 0, k == KD - 1)
                ins.then_inc(ring_a.used, 1)
                for t in range(NT):
                    pe.wait_ge(dve_out.sem, dve_out.at(("xn", t)))
                    turn(pe, scratch, t)
                pe.wait_ge(dve_out.sem, dve_out.at("csilu"))
                pe.wait_ge(act_out.sem, act_out.at("memv"))
                for c in range(N_MIX):
                    out_ = acc[c // 4][0:1, (c % 4) * MOD_COLS:(c % 4 + 1) * MOD_COLS]
                    pe.wait_ge(mix_loaded[c], 16)
                    mod_chunk(pe, mix_w[c], one_row, out_, MOD_PE)
                    pe.wait_ge(dve_out.sem, dve_out.at(("sum", c)))
                    ins = pe.matmul(out_, ones_col, sums[c], start=False, stop=True)
                    if c % 4 == 3:
                        ins.then_inc(pe_out.up(("shift", "scale")[c // 4]), 1)
                    if c == 5:
                        pe.wait_ge(act_out.sem, act_out.at("shift"))
                        to_columns(pe, mod_row, 0)
                pe.wait_ge(act_out.sem, act_out.at("scale"))
                to_columns(pe, mod_row, 1).then_inc(pe_out.up("columns"), 1)

            @block.vector
            def _(dve):
                rms_scale(None, dve, 0, scratch)
                rms_scale(None, dve, 1, scratch)
                dve.wait_ge(act_out.sem, act_out.at("memT1"))
                dve.tensor_tensor(actT[:, 1], turned, actT[:, 0].bitcast(F32), ALU.subtract)\
                    .then_inc(dve_out.up("memT"), 1)
                for g in range(g0, g0 + 2):
                    ring_a.split_lo(dve, g)
                dve.wait_ge(pe_out.sem, pe_out.at("params"))
                n4 = min(n_params, 4 * P)
                dve.tensor_copy(par[:, 0:n4], ps[:, 0, 0:n4])
                dve.tensor_copy(par[:, n4:n_params], ps[:, 3, 0:n_params - n4]).then_inc(dve_out.up("params"), 1)
                dve.wait_ge(act_out.sem, act_out.at("csig"))
                dve.tensor_tensor(csilu, cols("c", KD), csig, ALU.mult).then_inc(dve_out.up("csilu"), 1)
                dve.wait_ge(dve_out.sem, dve_out.at("csilu"))
                for c in range(N_MIX):
                    dve.wait_ge(mix_loaded[c], 16)
                    for k in range(MOD_PE, KD):
                        w = mix_w[c][:, k * MOD_COLS:(k + 1) * MOD_COLS]
                        if k == MOD_PE:
                            ins = dve.tensor_scalar(sums[c], w, csilu[:, k:k + 1], None, ALU.mult)
                        else:
                            ins = dve.scalar_tensor_tensor(sums[c], w, csilu[:, k:k + 1], sums[c], ALU.mult, ALU.add)
                        if k < KD - 1:
                            dve_steps.step(dve, ins)
                    ins.then_inc(dve_out.up(("sum", c)), 1)
                ring_a.split_lo(dve, sec["pw1"])
                for k in range(KD):
                    dve_steps.step(dve, dve.tensor_copy(cb[:, k, :], csilu[:, k:k + 1].to_broadcast([P, P])))
                dve.wait_ge(pe_out.sem, pe_out.at("columns"))
                mod_finish(dve, 0, ("mod_sh_m", "mod_sc_m"), "norm_pre_mix")

        _, u_pad, conv, sig, prod, csum, mod_row = carve((KD, P), (KD, PAD + SEQ), (KD, SEQ), (2, SEQ), (4, SEQ),
                                                         (2, SEQ), (2 * D,), limit=late_at)
        hT = conv
        g0 = sec["pw1"]
        first_m, first_f, first_g = (i * D // MOD_COLS for i in (2, 3, 5))
        N_GATE = D // MOD_COLS
        late = [*range(first_f, first_f + 2 * N_GATE), *range(first_m, first_m + N_GATE),
                *range(first_g, first_g + N_GATE)]
        late_loaded, late_used = [sem(f"late_loaded{i}") for i in range(MOD_LATE)], signal("late_used")
        late_used.events(range(len(late)))

        def load_late(sp, i):
            if i >= MOD_LATE:
                sp.wait_ge(late_used.sem, late_used.at(i - MOD_LATE))
            load_mod(sp, late_slots[:, i % MOD_LATE], late[i], late_loaded[i % MOD_LATE])

        def late_chunk(pe, i, lhs, out_):
            pe.wait_ge(late_loaded[i % MOD_LATE], 16 * (i // MOD_LATE + 1))
            mod_chunk(pe, late_slots[:, i % MOD_LATE], lhs, out_).then_inc(late_used.up(i), 1)

        AHEAD = 10
        BY_POOL = [0, 2, 4]
        BY_VECTOR = [j for j in range(KD) if j not in BY_POOL]
        pool_taps = [(j, k) for j in BY_POOL for k in range(CONVW)]
        SHARE = 8
        act_plan = []
        for j in range(KD):
            act_plan.append(("sig", j))
            if j > 0:
                n = len(pool_taps) if j == KD - 1 else j * SHARE
                act_plan += [("tap", i) for i in range((j - 1) * SHARE, n)]
        expect_input()
        act_out.events(act_plan + ["shift", "scale"])
        pool_out.events([("tap", i) for i in range(len(pool_taps))])
        pe_out.events(["columns", "mean"])
        dve_out.events(["zero"] + [("u", j) for j in range(KD)] + ["mod", "gate_m"])
        rows_count[0] += 64
        gates_row = rows_count[0]
        conv_done = {}
        MEAN_ORDER = [*BY_POOL, *BY_VECTOR]
        with nc.Block() as block:
            @block.sync
            def _(sp):
                load_row(sp, 0, A["norm_post_mix"][0])
                load_row(sp, 1, A["norm_post_ffn"][0])
                sp.dma_start(gate_m[:], A["mod_b"][0, 2 * D:3 * D].partition_broadcast(P)).then_inc(rows_loaded, 16)
                sp.dma_start(gate_f[:], A["mod_b"][0, 5 * D:6 * D].partition_broadcast(P)).then_inc(rows_loaded, 16)
                for i in range(MOD_LATE):
                    ring_a.load(sp, g0 + 2 + i)
                    load_late(sp, i)
                for g in range(g0 + 2 + MOD_LATE, g0 + KD + 2):
                    ring_a.load(sp, g)
                for i in range(MOD_LATE, len(late)):
                    load_late(sp, i)

            @block.scalar
            def _(act):
                affine(act, hT, 0)
                for what, i in act_plan:
                    if what == "sig":
                        if i + 1 < KD:
                            ring_a.split_hi(act, g0 + i + 1)
                        ring_a.wait_used(act, g0 + i)
                        if i >= 2:
                            act.wait_ge(dve_out.sem, dve_out.at(("u", i - 2)))
                        act.activation(sig[:, i % 2], ps[:, 4 + i % 4, SEQ:2 * SEQ], ACT.Sigmoid,
                                       bias=col("a_pw1_b", KD + i)).then_inc(act_out.up(("sig", i)), 1)
                    else:
                        j, k = pool_taps[i]
                        if k == 0:
                            act.wait_ge(dve_out.sem, dve_out.at(("u", j)))
                        if i >= 4:
                            act.wait_ge(pool_out.sem, pool_out.at(("tap", i - 4)))
                        src, w = u_pad[:, j, k:k + SEQ], col("a_dw_w", k * KD + j)
                        if k == 0:
                            ins = act.activation(prod[:, i % 4], src, ACT.Identity, bias=col("a_dw_b", j), scale=w)
                        else:
                            ins = act.activation(prod[:, i % 4], src, ACT.Copy, scale=w)
                        ins.then_inc(act_out.up(("tap", i)), 1)
                for h, name in enumerate(("shift", "scale")):
                    act.wait_ge(late_used.sem, late_used.at(N_GATE * h + N_GATE - 1))
                    act.activation(mod_row[0:1, h * D:(h + 1) * D], acc[h][0:1, :], ACT.Copy)\
                        .then_inc(act_out.up(name), 1)

            @block.gpsimd
            def _(pool):
                for i, (j, k) in enumerate(pool_taps):
                    pool.wait_ge(act_out.sem, act_out.at(("tap", i)))
                    if k == 0:
                        ins = pool.tensor_copy(csum[:, 1], prod[:, i % 4])
                    else:
                        pool.wait_ge(pool_out.sem, pool_out.at(("tap", i - 1)))
                        dst = conv[:, j] if k == CONVW - 1 else csum[:, (k + 1) % 2]
                        ins = pool.tensor_tensor(dst, csum[:, k % 2], prod[:, i % 4], ALU.add)
                    ins.then_inc(pool_out.up(("tap", i)), 1)

            @block.vector
            def _(dve):
                dve.memset(u_pad[:, :, 0:PAD], 0.0).then_inc(dve_out.up("zero"), 1)
                dve.wait_ge(dve_out.sem, dve_out.at("zero"))
                split_affine(dve, hT)
                taps = [(j, k) for j in BY_VECTOR for k in range(CONVW)]

                def tap(made):
                    if taps[0][0] >= made:
                        return
                    j, k = taps.pop(0)
                    src, w = u_pad[:, j, k:k + SEQ], col("a_dw_w", k * KD + j)
                    if k == 0:
                        dve.wait_ge(dve_out.sem, dve_out.at(("u", j)))
                        ins = dve.tensor_scalar(conv[:, j], src, w, col("a_dw_b", j), ALU.mult, ALU.add)
                    else:
                        ins = dve.scalar_tensor_tensor(conv[:, j], src, w, conv[:, j], ALU.mult, ALU.add)
                    dve_steps.step(dve, ins)
                    conv_done[j] = dve_steps.n

                for i in range(KD):
                    if i + 1 < KD:
                        ring_a.split_lo(dve, g0 + i + 1)
                    dve.wait_ge(act_out.sem, act_out.at(("sig", i)))
                    dve.scalar_tensor_tensor(u_pad[:, i, PAD:PAD + SEQ], ps[:, 4 + i % 4, 0:SEQ],
                                             col("a_pw1_b", i), sig[:, i % 2], ALU.add, ALU.mult)\
                                                 .then_inc(dve_out.up(("u", i)), 1)
                    if i + 1 < KD:
                        for _ in range(AHEAD):
                            tap(i + 1)
                while taps:
                    tap(KD)
                dve.wait_ge(pe_out.sem, pe_out.at("columns"))
                mod_finish(dve, 2, ("mod_sh_f", "mod_sc_f"), "norm_pre_ffn")
                dve.wait_ge(late_used.sem, late_used.at(3 * N_GATE - 1))
                two = ps[:, 4:6, :].rearrange("p b n -> p (b n)")
                dve.wait_ge(rows_loaded, gates_row)
                dve_steps.step(dve, dve.tensor_tensor(gate_m[:], two, gate_m[:], ALU.add))
                dve.tensor_tensor(gate_m[:], gate_m[:], rows[:, 0], ALU.mult).then_inc(dve_out.up("gate_m"), 1)

            @block.tensor
            def _(pe):
                for j in range(KD):
                    ring_a.wait_split(pe, g0 + j)
                    if j >= 4:
                        pe.wait_ge(dve_out.sem, dve_out.at(("u", j - 4)))
                    for n in range(2):
                        for k in range(KD):
                            if j == 0 and n == 0:
                                wait_input(pe, k)
                            w = [ring_a.part(g0 + j, s, n * BCH + k * P, n * BCH + k * P + P) for s in range(2)]
                            ins = mm3(pe, ps[:, 4 + j % 4, n * SEQ:(n + 1) * SEQ], w,
                                      [actT[:, s, k] for s in range(2)], k == 0, k == KD - 1)
                    ins.then_inc(ring_a.used, 1)
                for i in range(2 * N_GATE):
                    late_chunk(pe, i, one_row, acc[i // 4][0:1, (i % 4) * MOD_COLS:(i % 4 + 1) * MOD_COLS])
                pe.wait_ge(dve_out.sem, dve_out.at(("u", KD - 1)))
                for i in range(N_GATE):
                    late_chunk(pe, 2 * N_GATE + i, lambda k: cb[:, k],
                               ps[:, 4 + i // 2, (i % 2) * MOD_COLS:(i % 2 + 1) * MOD_COLS])
                pe.wait_ge(act_out.sem, act_out.at("scale"))
                to_columns(pe, mod_row, 0)
                to_columns(pe, mod_row, 1).then_inc(pe_out.up("columns"), 1)
                for n, j in enumerate(MEAN_ORDER):
                    if j in BY_POOL:
                        pe.wait_ge(pool_out.sem, pool_out.at(("tap", CONVW * BY_POOL.index(j) + CONVW - 1)))
                    else:
                        pe.wait_ge(dve_steps.sem, conv_done[j])
                    ins = pe.matmul(ps[:, 6, 0:SEQ], ones_mean[:], conv[:, j], start=n == 0, stop=n == KD - 1)
                ins.then_inc(pe_out.up("mean"), 1)

        _, _, conv, sq, rstd, yb = carve((KD, P), (KD, PAD + SEQ), (KD, SEQ), (KD, SEQ), (SEQ,), (NT, D),
                                         limit=late_at)
        scratch = sq.rearrange("p k t -> p (k t)").rearrange("p (t d) -> p t d", t=NT)
        hT = conv
        g0 = sec["pw2"]
        pe_out.events(["var"])
        dve_out.events([("centred", k) for k in range(KD)] + [("normal", q) for q in range(4)]
                       + [("y", 0), ("y", 1), ("x", 0), ("x", 1), ("xn", 0), ("xn", 1)])
        act_out.events([("square", k) for k in range(KD)] + ["std"] + [("silu", q) for q in range(4)]
                       + [("yroot", 0), ("yroot", 1), ("root", 0), ("root", 1)])
        turned_done.events([0, 1])
        rows_count[0] += 16
        b2_row = rows_count[0]
        with nc.Block() as block:
            @block.sync
            def _(sp):
                load_row(sp, 0, A["a_pw2_b"][0])
                for g in range(g0 + 2, g0 + 4 + 2):
                    ring_a.load(sp, g)
                for g in range(2):
                    ring_b.load(sp, g)

            @block.scalar
            def _(act):
                for k in range(KD):
                    act.wait_ge(dve_out.sem, dve_out.at(("centred", k)))
                    act.activation(sq[:, k], conv[:, k], ACT.Square).then_inc(act_out.up(("square", k)), 1)
                ring_a.split_hi(act, g0)
                ring_a.split_hi(act, g0 + 1)
                act.wait_ge(pe_out.sem, pe_out.at("var"))
                act.activation(rstd, ps[:, 7, 0:SEQ], ACT.Sqrt, bias=eps[:, 1:2]).then_inc(act_out.up("std"), 1)
                for q in range(4):
                    act.wait_ge(dve_out.sem, dve_out.at(("normal", q)))
                    for k in range(2 * q, 2 * q + 2):
                        ins = act.activation(conv[:, k], conv[:, k], ACT.Silu, bias=col("a_ln_b", k),
                                             scale=col("a_ln_g", k))
                    ins.then_inc(act_out.up(("silu", q)), 1)
                for c in range(2, 5):
                    ring_a.split_hi(act, g0 + c)
                for t in range(NT):
                    act.wait_ge(dve_out.sem, dve_out.at(("y", t)))
                    act_steps.step(act, act.activation(scratch[:, t], yb[:, t], ACT.Square,
                                                       accum_out=stats[:, t, 3:4]))
                    act.activation(stats[:, t, 4:5], stats[:, t, 3:4], ACT.Sqrt, bias=eps[:, 0:1],
                                   scale=1.0 / D).then_inc(act_out.up(("yroot", t)), 1)
                for t in range(NT):
                    act.wait_ge(dve_out.sem, dve_out.at(("x", t)))
                    rms_scale(act, None, t, scratch)

            silu_split, gate_half = [], []

            @block.vector
            def _(dve):
                for k in range(KD):
                    dve.tensor_tensor(conv[:, k], conv[:, k], ps[:, 6, 0:SEQ], ALU.subtract)\
                        .then_inc(dve_out.up(("centred", k)), 1)
                ring_a.split_lo(dve, g0)
                ring_a.split_lo(dve, g0 + 1)
                dve.wait_ge(act_out.sem, act_out.at("std"))
                dve_steps.step(dve, dve.reciprocal(rstd, rstd))

                def normal(q):
                    pair = slice(2 * q, 2 * q + 2)
                    dve.tensor_tensor(conv[:, pair], conv[:, pair],
                                      rstd.unsqueeze(1).to_broadcast([P, 2, SEQ]), ALU.mult)\
                                          .then_inc(dve_out.up(("normal", q)), 1)

                def split_silu(q):
                    pair = slice(2 * q, 2 * q + 2)
                    dve.wait_ge(act_out.sem, act_out.at(("silu", q)))
                    dve_steps.step(dve, dve.tensor_copy(actT[:, 0, pair], conv[:, pair]))
                    dve_steps.step(dve, dve.tensor_tensor(actT[:, 1, pair], conv[:, pair],
                                                          actT[:, 0, pair].bitcast(F32), ALU.subtract))
                    silu_split.append(dve_steps.n)

                normal(0)
                normal(1)
                split_silu(0)
                normal(2)
                split_silu(1)
                normal(3)
                split_silu(2)
                split_silu(3)
                for c in range(2, 5):
                    ring_a.split_lo(dve, g0 + c)
                dve.wait_ge(late_used.sem, late_used.at(3 * N_GATE + 1))
                dve_steps.step(dve, dve.tensor_tensor(gate_f[:, 0:512], ps[:, 4], gate_f[:, 0:512], ALU.add))
                gate_half.append(dve_steps.n)
                ring_a.wait_used(dve, g0 + 3)
                dve.wait_ge(rows_loaded, b2_row)
                for t in range(NT):
                    dve.tensor_tensor(yb[:, t], acc[t], rows[:, 0], ALU.add).then_inc(dve_out.up(("y", t)), 1)
                for t in range(NT):
                    dve.wait_ge(act_out.sem, act_out.at(("yroot", t)))
                    dve_steps.step(dve, dve.reciprocal(stats[:, t, 5:6], stats[:, t, 4:5]))
                    dve_steps.step(dve, dve.scalar_tensor_tensor(yb[:, t], yb[:, t], stats[:, t, 5:6], gate_m[:],
                                                                 ALU.mult, ALU.mult))
                    dve.tensor_tensor(x_tok[:, t], x_tok[:, t], yb[:, t], ALU.add).then_inc(dve_out.up(("x", t)), 1)
                for t in range(NT):
                    rms_scale(None, dve, t, scratch)
                dve.wait_ge(late_used.sem, late_used.at(4 * N_GATE - 1))
                dve_steps.step(dve, dve.tensor_tensor(gate_f[:, 512:D], ps[:, 0], gate_f[:, 512:D], ALU.add))
                dve_steps.step(dve, dve.tensor_tensor(gate_f[:], gate_f[:], rows[:, 1], ALU.mult))

            @block.tensor
            def _(pe):
                def gate_chunk(i, bank):
                    late_chunk(pe, 3 * N_GATE + i, lambda k: cb[:, k],
                               ps[:, bank, (i % 2) * MOD_COLS:(i % 2 + 1) * MOD_COLS])

                gate_chunk(0, 4)
                for k in range(KD):
                    pe.wait_ge(act_out.sem, act_out.at(("square", k)))
                    ins = pe.matmul(ps[:, 7, 0:SEQ], ones_mean[:], sq[:, k], start=k == 0, stop=k == KD - 1)
                ins.then_inc(pe_out.up("var"), 1)
                gate_chunk(1, 4)
                for c in range(4):
                    ring_a.wait_split(pe, g0 + c)
                    pe.wait_ge(dve_steps.sem, silu_split[c])
                    for k in range(2 * c, 2 * c + 2):
                        for t in range(NT):
                            for n in range(2):
                                w = [ring_a.part(g0 + c, s, (k % 2) * D + n * 512, (k % 2) * D + n * 512 + 512)
                                     for s in range(2)]
                                ins = mm3(pe, acc[t][:, n * 512:(n + 1) * 512],
                                          [actT[:, s, k, t * P:(t + 1) * P] for s in range(2)], w, k == 0, k == KD - 1)
                    ins.then_inc(ring_a.used, 1)
                pe.wait_ge(dve_out.sem, dve_out.at(("y", 0)))
                gate_chunk(2, 0)
                gate_chunk(3, 0)
                pe.wait_ge(dve_steps.sem, gate_half[0])
                for t in range(NT):
                    pe.wait_ge(dve_out.sem, dve_out.at(("xn", t)))
                    turn(pe, scratch, t)

        modulated_at = turned_done.at(1)

        def take_modulated(hT=hT):
            def on_act(act):
                act.wait_ge(turned_done.sem, modulated_at)
                affine(act, hT, 2)

            return on_act, lambda dve: split_affine(dve, hT)

        h_done, f_step, conv_in, conv_done = sem("h_done"), sem("f_step"), sem("conv_in"), sem("conv_done")
        gated, scaled_x, root_ready = sem("gated"), sem("scaled_x"), sem("root_ready")
        done = {"h": 0, "f_step": 0, "conv": 0, "gated": 0}

        def ffn_stage(name, conv, norm_rows, turn_x, next_a, next_b, take):
            cg, cu, hf, yb, xs = carve((2, SEQ), (2, SEQ), (2, SEQ), (NT, D), (NT, D))
            ga, gb = sec[name], sec[name, "B"]
            sa, sb_ = ga, gb
            la, lb = [ring_a.load_no[ga + q] - 32 for q in range(2)], [ring_b.load_no[gb + q] - 16 for q in range(2)]
            h0, f0, c0, s0 = done["h"], done["f_step"], done["conv"], done["gated"]
            per = 4 if conv else 2
            done["h"] += NF
            done["f_step"] += per * NF
            done["conv"] += NF if conv else 0
            done["gated"] += NF
            BODY = NF // 2
            if not conv:
                rows_count[0] += 32
            rows_at = rows_count[0]
            dve_out.events([e for part in X_PARTS for e in ([("stat", part[0])] if part[1] == 0 else [])
                            + [("x", part)]])
            act_out.events([("root", 0)] + (["hi"] if turn_x and not conv else []) + [("root", 1)]
                           + (["hi"] if turn_x and conv else []))
            acc_ready.events([0])
            expect_input()
            if turn_x:
                turned_done.events(X_PARTS)
            if not conv:
                pool_out.events(["xs"])

            with nc.Block() as block:
                @block.sync
                def _(sp):
                    if norm_rows:
                        load_row(sp, 0, norm_rows[0])
                        load_row(sp, 1, norm_rows[1])
                    src = FFN_SOURCES[name]
                    with sp.Fori(1, BODY) as j:
                        for q in range(2):
                            sp.wait_ge(ring_a.lo_done, j * 2 + (sa + q - 1))
                            for half in range(2):
                                sp.dma_start(a_raw[:, q, half * BCH:(half + 1) * BCH].rearrange("p (k n) -> p k n", k=KD),
                                             src[half][:, :, bass.ds(j * 256 + q * P, P)])\
                                    .then_inc(ring_a.loaded[q], 16)
                            sp.wait_ge(ring_b.lo_done, j * 2 + (sb_ + q - 1))
                            sp.dma_start(b_raw[:, q], src[2][bass.ds(j * 2 + q, 1), :, :].rearrange("a p n -> (a p) n"))\
                                .then_inc(ring_b.loaded[q], 16)
                    for g in range(next_a, next_a + 2):
                        ring_a.load(sp, g)
                    for g in range(next_b, next_b + 2):
                        ring_b.load(sp, g)

                def count(ring_first, q, j, back=0):
                    return j * 2 + (ring_first + q + 1 - back)

                def split_a(act, dve, q, j):
                    if act is not None:
                        act.wait_ge(ring_a.loaded[q], j * 32 + (la[q] + 32))
                        act.wait_ge(ring_a.used, count(sa, q, j, 2))
                        act.activation(a_parts[:, q, 0], a_raw[:, q], ACT.Copy).then_inc(ring_a.hi_done, 1)
                    else:
                        dve.wait_ge(ring_a.hi_done, count(sa, q, j))
                        dve.tensor_tensor(a_parts[:, q, 1], a_raw[:, q], a_parts[:, q, 0].bitcast(F32),
                                          ALU.subtract).then_inc(ring_a.lo_done, 1)

                def split_b(act, lo, q, j):
                    if act is not None:
                        act.wait_ge(ring_b.loaded[q], j * 16 + (lb[q] + 16))
                        act.wait_ge(ring_b.used, count(sb_, q, j, 2))
                        act.activation(b_parts[:, q, 0], b_raw[:, q], ACT.Copy).then_inc(ring_b.hi_done, 1)
                    else:
                        lo.wait_ge(ring_b.hi_done, count(sb_, q, j))
                        lo.tensor_tensor(b_parts[:, q, 1], b_raw[:, q], b_parts[:, q, 0].bitcast(F32),
                                         ALU.subtract).then_inc(ring_b.lo_done, 1)

                def first_splits(act, dve):
                    if act is not None:
                        ring_a.split_hi(act, ga + 1)
                        ring_b.split_hi(act, gb)
                        ring_b.split_hi(act, gb + 1)
                    else:
                        ring_a.split_lo(dve, ga + 1)
                        if not conv:
                            ring_b.split_lo(dve, gb)
                            ring_b.split_lo(dve, gb + 1)

                def tile_act(act, q, j):
                    first = isinstance(j, int) and j == 0
                    act.wait_ge(ring_a.used, j * 2 + (sa + q + 1))
                    if not first:
                        act.wait_ge(h_done, j * 2 + (h0 + q - 1))
                    gate, up = ps[:, 4 + q, 0:SEQ], ps[:, 4 + q, SEQ:2 * SEQ]
                    if conv:
                        for buf, src, half in ((cg, gate, 0), (cu, up, NF)):
                            w = col_at("f_dw_w", 2 * 2 * NF + half + q, j)
                            b = col_at("f_dw_b", half + q, j)
                            ins = act.activation(buf[:, q], src, ACT.Identity, bias=b, scale=w)
                        ins.then_inc(conv_in, 1)
                        act.wait_ge(conv_done, j * 2 + (c0 + q + 1))
                        act.activation(cg[:, q], cg[:, q], ACT.Silu).then_inc(gated, 1)
                    else:
                        act.activation(cg[:, q], gate, ACT.Silu).then_inc(gated, 1)

                def col_at(name, i, j):
                    if isinstance(j, int):
                        return col(name, i + 2 * j)
                    return par[:, bass.ds(j * 2 + (first_col[name] + i), 1)]

                def tile_dve(dve, q, j):
                    n = f0 + per * q
                    gate, up = ps[:, 4 + q, 0:SEQ], ps[:, 4 + q, SEQ:2 * SEQ]
                    if conv:
                        dve.wait_ge(conv_in, j * 2 + (c0 + q + 1))
                        for back in (1, 2):
                            for buf, src, half in ((cg, gate, 0), (cu, up, NF)):
                                w = col_at("f_dw_w", (2 - back) * 2 * NF + half + q, j)
                                if back == 2:
                                    dve.wait_ge(f_step, j * (2 * per) + (n + (1 if half == 0 else 2)))
                                ins = dve.scalar_tensor_tensor(buf[:, q, back:SEQ], src[:, 0:SEQ - back], w,
                                                               buf[:, q, back:SEQ], ALU.mult, ALU.add)
                                if back == 1:
                                    ins.then_inc(f_step, 1)
                        ins.then_inc(conv_done, 1)
                        n += 2
                        up = cu[:, q]
                    dve.wait_ge(gated, j * 2 + (s0 + q + 1))
                    dve.tensor_tensor(hf[:, q], cg[:, q], up, ALU.mult).then_inc(f_step, 1)
                    if not (isinstance(j, int) and j == 0 and sb_ + q < 2):
                        dve.wait_ge(ring_b.used, j * 2 + (sb_ + q - 1))
                    dve.wait_ge(f_step, j * (2 * per) + (n + 1))
                    dve.tensor_copy(hid[:, q, 0], hf[:, q]).then_inc(f_step, 1)
                    dve.wait_ge(f_step, j * (2 * per) + (n + 2))
                    dve.tensor_tensor(hid[:, q, 1], hf[:, q], hid[:, q, 0].bitcast(F32),
                                      ALU.subtract).then_inc(h_done, 1)

                def up_pe(pe, q, j):
                    first = isinstance(j, int) and j == 0
                    pe.wait_ge(ring_a.lo_done, j * 2 + (sa + q + 1))
                    if not first:
                        pe.wait_ge(h_done, j * 2 + (h0 + q - 1))
                    for n in range(2):
                        for k in range(KD):
                            if first and q == 0 and n == 0:
                                wait_input(pe, k)
                            w = [a_parts[:, q, s, n * BCH + k * P:n * BCH + (k + 1) * P] for s in range(2)]
                            ins = mm3(pe, ps[:, 4 + q, n * SEQ:(n + 1) * SEQ], w, [actT[:, s, k] for s in range(2)],
                                      k == 0, k == KD - 1)
                    ins.then_inc(ring_a.used, 1)

                def down_pe(pe, q, j, start, stop):
                    pe.wait_ge(ring_b.lo_done, j * 2 + (sb_ + q + 1))
                    pe.wait_ge(h_done, j * 2 + (h0 + q + 1))
                    for t in range(NT):
                        for n in range(2):
                            ins = mm3(pe, acc[t][:, n * 512:(n + 1) * 512],
                                      [hid[:, q, s, t * P:(t + 1) * P] for s in range(2)],
                                      [b_parts[:, q, s, n * 512:(n + 1) * 512] for s in range(2)], start, stop)
                        if stop and t == 0:
                            ins.then_inc(acc_ready.up(0), 1)
                    ins.then_inc(ring_b.used, 1)

                @block.tensor
                def _(pe):
                    up_pe(pe, 0, 0)
                    up_pe(pe, 1, 0)
                    down_pe(pe, 0, 0, True, False)
                    with pe.Fori(1, BODY) as j:
                        up_pe(pe, 0, j)
                        down_pe(pe, 1, j - 1, False, False)
                        up_pe(pe, 1, j)
                        down_pe(pe, 0, j, False, False)
                    down_pe(pe, 1, BODY - 1, False, True)
                    if turn_x:
                        turn_x_pe(pe)

                @block.scalar
                def _(act):
                    take[0](act)
                    first_splits(act, None)
                    tile_act(act, 0, 0)
                    with act.Fori(1, BODY) as j:
                        split_a(act, None, 0, j)
                        tile_act(act, 1, j - 1)
                        split_b(act, None, 0, j)
                        split_a(act, None, 1, j)
                        tile_act(act, 0, j)
                        split_b(act, None, 1, j)
                    if turn_x:
                        ring_a.split_hi(act, next_a)
                    tile_act(act, 1, BODY - 1)
                    for t in range(NT):
                        if conv:
                            if t == 0:
                                act.wait_ge(acc_ready.sem, acc_ready.at(0))
                            else:
                                act.wait_ge(ring_b.used, sb_ + NF)
                            act_steps.step(act, act.activation(yb[:, t], acc[t], ACT.Square,
                                                               accum_out=stats[:, t, 6:7]))
                            act.activation(stats[:, t, 7:8], stats[:, t, 6:7], ACT.Sqrt,
                                           bias=eps[:, 0:1], scale=1.0 / D).then_inc(act_out.up(("root", t)), 1)
                        else:
                            act.wait_ge(dve_out.sem, dve_out.at(("stat", t)))
                            act.activation(stats[:, t, 7:8], stats[:, t, 13:14], ACT.Sqrt,
                                           bias=eps[:, 1:2]).then_inc(act_out.up(("root", t)), 1)
                        if turn_x and t == 0 and not conv:
                            first_hi(act)
                    if turn_x and conv:
                        first_hi(act)

                @block.gpsimd
                def _(pool):
                    if conv:
                        ring_b.split_lo(pool, gb)
                        ring_b.split_lo(pool, gb + 1)
                        with pool.Fori(1, BODY) as j:
                            split_b(None, pool, 0, j)
                            split_b(None, pool, 1, j)
                    else:
                        pool.tensor_scalar(xs, x_tok[:], ALPHA, None, ALU.mult).then_inc(pool_out.up("xs"), 1)

                @block.vector
                def _(dve):
                    take[1](dve)
                    first_splits(None, dve)
                    tile_dve(dve, 0, 0)
                    with dve.Fori(1, BODY) as j:
                        split_a(None, dve, 0, j)
                        tile_dve(dve, 1, j - 1)
                        if not conv:
                            split_b(None, dve, 0, j)
                        split_a(None, dve, 1, j)
                        tile_dve(dve, 0, j)
                        if not conv:
                            split_b(None, dve, 1, j)
                    if turn_x and not conv:
                        ring_a.split_lo(dve, next_a)
                    tile_dve(dve, 1, BODY - 1)
                    if turn_x and conv:
                        ring_a.split_lo(dve, next_a)
                    if conv:
                        for t in range(NT):
                            dve.wait_ge(act_out.sem, act_out.at(("root", t)))
                            dve.reciprocal(stats[:, t, 8:9], stats[:, t, 7:8]).then_inc(dve_out.up(("stat", t)), 1)
                            dve.wait_ge(dve_out.sem, dve_out.at(("stat", t)))
                            dve_steps.step(dve, dve.scalar_tensor_tensor(yb[:, t], acc[t], stats[:, t, 8:9],
                                                                         gate_f[:], ALU.mult, ALU.mult))
                            for part in X_PARTS:
                                if part[0] == t:
                                    w = slice(part[1] * P, part[2] * P)
                                    dve.tensor_tensor(x_tok[:, t, w], x_tok[:, t, w], yb[:, t, w], ALU.add)\
                                       .then_inc(dve_out.up(("x", part)), 1)
                    else:
                        layer_norm_dve(dve, yb, xs, 0.5, rows_at, ring_b.used, sb_ + NF)
                    if turn_x:
                        first_lo(dve)
            if turn_x:
                return take_x()

        def layer_norm_dve(dve, yb, xs, scale, rows_at, used, acc_at):
            dve.wait_ge(pool_out.sem, pool_out.at("xs"))
            dve.wait_ge(rows_loaded, rows_at)
            for t in range(NT):
                if t == 0:
                    dve.wait_ge(acc_ready.sem, acc_ready.at(0))
                else:
                    dve.wait_ge(used, acc_at)
                dve_steps.step(dve, dve.scalar_tensor_tensor(yb[:, t], acc[t], scale, xs[:, t], ALU.mult, ALU.add))
                for n in range(2):
                    ins = dve.bn_stats(stats[:, t, 6 * n:6 * n + 6], yb[:, t, n * 512:(n + 1) * 512])
                    dve_steps.mark(ins)
                dve.wait_ge(dve_steps.sem, dve_steps.n)
                dve.bn_aggr(stats[:, t, 12:14], stats[:, t, 0:12]).then_inc(dve_out.up(("stat", t)), 1)
                dve.wait_ge(dve_out.sem, dve_out.at(("stat", t)))
                dve_steps.step(dve, dve.scalar_tensor_tensor(yb[:, t], yb[:, t], stats[:, t, 12:13], rows[:, 0],
                                                             ALU.subtract, ALU.mult))
                dve.wait_ge(act_out.sem, act_out.at(("root", t)))
                dve_steps.step(dve, dve.reciprocal(stats[:, t, 14:15], stats[:, t, 7:8]))
                for part in X_PARTS:
                    if part[0] == t:
                        w = slice(part[1] * P, part[2] * P)
                        dve.scalar_tensor_tensor(x_tok[:, t, w], yb[:, t, w], stats[:, t, 14:15], rows[:, 1, w],
                                                 ALU.mult, ALU.add).then_inc(dve_out.up(("x", part)), 1)

        def ffn_views(gate, up_w, down):
            g, u = (w.rearrange("(k p) n -> p k n", p=P) for w in (gate, up_w))
            return g, u, down.rearrange("(i p) n -> i p n", p=P)

        FFN_SOURCES = {"ffn": ffn_views(A["f_up_w"][0][:, 0:DFF], A["f_up_w"][0][:, DFF:2 * DFF], A["f_down_w"][0])}
        for i in range(2):
            for f in ("ffn1", "ffn2"):
                FFN_SOURCES[f, i] = ffn_views(*(A[f"{f}_w_{n}_2"][i] for n in ("gate", "up", "down")))

        MEM_N = NMH * NT
        mem_scores = ps[:, 4:8, :].rearrange("p b (t m) -> p (b t) m", t=NT)
        mem_bank = lambda h: 2 * (h % 2) + h // 2
        neg_max, total, inv = (small[:, i * MEM_N:(i + 1) * MEM_N] for i in range(3))

        def expect_memory():
            mem_pe.events(["scores", "probsT", "out"])
            mem_act.events(["queries", "exp", "probsT", "hi"])
            mem_dve.events(["max", "probs", "probsT", "lo"])

        def mem_scores_pe(pe, mqT):
            pe.wait_ge(mem_act.sem, mem_act.at("queries"))
            for h in range(NMH):
                r = slice((h % 2) * HD, (h % 2) * HD + HD)
                for t in range(NT):
                    ins = pe.matmul(mem_scores[:, 2 * mem_bank(h) + t], mqT[r, h // 2, t * P:(t + 1) * P],
                                    memkT[r, h // 2, :], start=True, stop=True)
            ins.then_inc(mem_pe.up("scores"), 1)

        def mem_turn_pe(pe, probs):
            pe.wait_ge(mem_dve.sem, mem_dve.at("probs"))
            for h in range(NMH):
                for m in range(2):
                    for t in range(NT):
                        ins = pe.transpose(turned[:, 2 * h + m, t * P:(t + 1) * P],
                                           probs[:, 2 * mem_bank(h) + t, m * P:(m + 1) * P], ident[:])
            ins.then_inc(mem_pe.up("probsT"), 1)

        def mem_out_pe(pe, probsT):
            pe.wait_ge(mem_act.sem, mem_act.at("probsT"))
            pe.wait_ge(mem_dve.sem, mem_dve.at("probsT"))
            for h in range(NMH):
                for m in range(2):
                    ins = pe.matmul(ps[(h % 2) * HD:(h % 2) * HD + HD, 6 + h // 2, 0:SEQ],
                                    memv[:, m, h * HD:(h + 1) * HD], probsT[:, 2 * h + m, :],
                                    start=m == 0, stop=m == 1)
            ins.then_inc(mem_pe.up("out"), 1)

        def mem_exp_act(act, probs):
            act.wait_ge(mem_dve.sem, mem_dve.at("max"))
            for i in range(MEM_N):
                ins = act.activation(probs[:, i], mem_scores[:, i], ACT.Exp, bias=neg_max[:, i:i + 1],
                                     accum_out=total[:, i:i + 1])
            ins.then_inc(mem_act.up("exp"), 1)

        def mem_probsT_act(act, probsT):
            act.wait_ge(mem_pe.sem, mem_pe.at("probsT"))
            act.activation(probsT[:, 0:4], turned[:, 0:4], ACT.Copy).then_inc(mem_act.up("probsT"), 1)

        def mem_hi_act(act):
            act.wait_ge(mem_pe.sem, mem_pe.at("out"))
            act.activation(actT[:, 0, 6:8], ps[:, 6:8, 0:SEQ], ACT.Copy).then_inc(mem_act.up("hi"), 1)

        def mem_max_dve(dve):
            dve.wait_ge(mem_pe.sem, mem_pe.at("scores"))
            dve.tensor_reduce(neg_max, mem_scores, AX_X, ALU.max, negate=True).then_inc(mem_dve.up("max"), 1)

        def mem_probs_dve(dve, probs):
            dve.wait_ge(mem_act.sem, mem_act.at("exp"))
            dve_steps.step(dve, dve.reciprocal(inv, total))
            dve.tensor_tensor(probs, probs, inv.unsqueeze(2).to_broadcast([P, MEM_N, NMEM]),
                              ALU.mult).then_inc(mem_dve.up("probs"), 1)

        def mem_probsT_dve(dve, probsT):
            dve.wait_ge(mem_pe.sem, mem_pe.at("probsT"))
            dve.tensor_copy(probsT[:, 4:8], turned[:, 4:8]).then_inc(mem_dve.up("probsT"), 1)

        def mem_lo_dve(dve):
            dve.wait_ge(mem_act.sem, mem_act.at("hi"))
            dve.tensor_tensor(actT[:, 1, 6:8], ps[:, 6:8, 0:SEQ],
                              actT[:, 0, 6:8].bitcast(F32), ALU.subtract).then_inc(mem_dve.up("lo"), 1)

        def output_stage(i):
            yb, xs = carve((NT, D), (NT, D))
            g0, nxt = sec["w_out", i], sec[("ffn2", i), "B"]
            dve_out.events([e for part in X_PARTS for e in ([("stat", part[0])] if part[1] == 0 else [])
                            + [("x", part)]])
            act_out.events([("root", 0), "hi", ("root", 1)])
            acc_ready.events([0])
            turned_done.events(X_PARTS)
            pool_out.events(["xs"])
            rows_count[0] += 32
            rows_at = rows_count[0]
            with nc.Block() as block:
                @block.sync
                def _(sp):
                    load_row(sp, 0, A["ln_g_2"][i, 1])
                    load_row(sp, 1, A["ln_b_2"][i, 1])
                    for g in range(g0 + 2, g0 + 4 + 2):
                        ring_a.load(sp, g)

                @block.gpsimd
                def _(pool):
                    pool.tensor_scalar(xs, x_tok[:], ALPHA, None, ALU.mult).then_inc(pool_out.up("xs"), 1)

                @block.scalar
                def _(act):
                    for c in range(2, 5):
                        ring_a.split_hi(act, g0 + c)
                    for t in range(NT):
                        act.wait_ge(dve_out.sem, dve_out.at(("stat", t)))
                        act.activation(stats[:, t, 7:8], stats[:, t, 13:14], ACT.Sqrt,
                                       bias=eps[:, 1:2]).then_inc(act_out.up(("root", t)), 1)
                        if t == 0:
                            first_hi(act)

                @block.vector
                def _(dve):
                    for c in range(2, 5):
                        ring_a.split_lo(dve, g0 + c)
                    layer_norm_dve(dve, yb, xs, 1.0, rows_at, ring_a.used, g0 + 4)
                    first_lo(dve)

                @block.tensor
                def _(pe):
                    for c in range(4):
                        ring_a.wait_split(pe, g0 + c)
                        down_chunk(pe, g0 + c, c)
                    turn_x_pe(pe)
            return take_x()

        def down_chunk(pe, g, c):
            for t in range(NT):
                for k in range(2 * c, 2 * c + 2):
                    for n in range(2):
                        w = [ring_a.part(g, s, (k % 2) * D + n * 512, (k % 2) * D + n * 512 + 512) for s in range(2)]
                        ins = mm3(pe, acc[t][:, n * 512:(n + 1) * 512],
                                  [actT[:, s, k, t * P:(t + 1) * P] for s in range(2)], w, k == 0, k == KD - 1)
                if c == 3 and t == 0:
                    ins.then_inc(acc_ready.up(0), 1)
            ins.then_inc(ring_a.used, 1)

        def rwkv_stages(take):
            z, mqT, lora, g_up, SIG, CUM, Av, KK, BON = carve(
                (20, SEQ), (2, SEQ), (C,), (C,), (MT6, SEQ), (MT6, SEQ), (MT6, SEQ), (MT6, SEQ), (MT6, SEQ))
            R, K, V = (z[:, MT6 * i:MT6 * (i + 1)] for i in range(3))
            low, lowg = z[:, 18], z[:, 19]
            used = (20 + 2) * SEQ + 2 * C + 5 * MT6 * SEQ
            reset = gate_m[:, C:D]
            mk = rows[:].rearrange("p a (m n) -> p (a m) n", n=P)
            level_mask = [mk[:, l] for l in range(6)]
            pair_mask, below, upto = mk[:, 6], mk[:, 7], mk[:, 8]
            one_minus_mu, one_minus_ka = small[:, 24:44], small[:, 44:50]

            g0 = sec["rwkv_in"]
            expect_input()
            z_tile = [2 * i + n for i in RWKV_ORDER for n in range(2)]
            act_out.events([("z", m) for m in z_tile])
            expect_memory()
            mem_at = 22 * SEQ + 2 * C
            probs, probsT = (arena[:, mem_at + i * 2048:mem_at + (i + 1) * 2048].rearrange("p (a b) -> p a b", a=8)
                             for i in range(2))
            dve_out.events(["mu"] + [("z", m) for m in z_tile])
            norm_act.events(["square", "kk", "root", "low", "decay", "rate"])
            norm_pe.events(["sum", "decay", "rate"])
            norm_dve.events(["sum", "kk", "cum", "cumx"])
            sum_of = [ps[:, 4 + m // 2, (m % 2) * SEQ:(m % 2 + 1) * SEQ] if m < 4 else ps[:, 2 + m, SEQ:2 * SEQ]
                      for m in range(MT6)]
            load_at = 16 * 3
            lora_loaded = sem("lora_loaded")
            with nc.Block() as block:
                @block.sync
                def _(sp):
                    sp.dma_start(lora[0:HD], A["rwkv_w_up_2"][0]).then_inc(lora_loaded, 16)
                    sp.dma_start(lora[HD:P], A["rwkv_a_up_2"][0]).then_inc(lora_loaded, 16)
                    sp.dma_start(g_up, A["rwkv_g_up_2"][0]).then_inc(lora_loaded, 16)
                    for g in range(g0 + 2, g0 + 12 + 2):
                        ring_a.load(sp, g)

                @block.gpsimd
                def _(pool):
                    def select(view, base, cm, pattern):
                        pool_steps.step(pool, pool.affine_select(out=view, in_=view, compare_op=ALU.is_ge, fill=0.0,
                                                                 base=base, pattern=pattern, channel_multiplier=cm))
                    pool_steps.step(pool, pool.memset(mk[:, 0:9], 0.0))
                    for l in range(6):
                        b = 1 << l
                        view = level_mask[l].rearrange("p (B h w) -> p B h w", h=2, w=b)[:, :, 1]
                        pool_steps.step(pool, pool.memset(view, 1.0))
                        select(view, 0, 1, [[-2 * b, P // (2 * b)], [0, b]])
                        select(view, b - 1, -1, [[2 * b, P // (2 * b)], [0, b]])
                    view = pair_mask.rearrange("p (B h) -> p B h", h=2)[:, :, 0]
                    pool_steps.step(pool, pool.memset(view, 1.0))
                    select(view, -1, 1, [[-2, P // 2]])
                    select(view, 1, -1, [[2, P // 2]])
                    for m, base in ((below, -1), (upto, 0)):
                        view = m.rearrange("p (c w) -> p c w", w=CHUNK)
                        pool_steps.step(pool, pool.memset(m, 1.0))
                        select(view, base, -1, [[CHUNK, 2], [1, CHUNK]])
                        select(view, 0, 1, [[-CHUNK, 2], [0, CHUNK]])
                    pool_steps.step(pool, pool.memset(reset, 1.0))
                    pool_steps.step(pool, pool.memset(reset.rearrange("p (c w) -> p c w", w=CHUNK)[:, :, 0:1], 0.0))
                masks_made = pool_steps.n

                @block.tensor
                def _(pe):
                    for c in range(12):
                        g = g0 + c
                        ring_a.wait_split(pe, g)
                        if c >= 6:
                            pe.wait_ge(dve_out.sem, dve_out.at(("z", z_tile[2 * (c - 6) + 1])))
                        width = 256 if c >= 2 else P
                        bank = (c - 2) % 4 if c >= 2 else 4 + c
                        for n in range(width // P):
                            for k in range(KD):
                                if c == 0 and n == 0:
                                    wait_input(pe, k)
                                w = [ring_a.part(g, s, k * width + n * P, k * width + n * P + P) for s in range(2)]
                                ins = mm3(pe, ps[:, bank, n * SEQ:(n + 1) * SEQ], w, [actT[:, s, k] for s in range(2)],
                                          k == 0, k == KD - 1)
                        ins.then_inc(ring_a.used, 1)
                        if c == 2:
                            mem_scores_pe(pe, mqT)
                        elif c == 4:
                            mem_turn_pe(pe, probs)
                        elif c == 5:
                            mem_out_pe(pe, probsT)
                        elif c == 6:
                            pe.wait_ge(norm_act.sem, norm_act.at("square"))
                            for m in range(MT6):
                                ins = pe.matmul(sum_of[m], head_ones[:], BON[:, m], start=True, stop=True)
                            ins.then_inc(norm_pe.up("sum"), 1)
                        elif c in (9, 10):
                            r, name, before = ((slice(0, HD), "decay", "low"), (slice(HD, P), "rate", "decay"))[c - 9]
                            pe.wait_ge(norm_act.sem, norm_act.at(before))
                            if c == 9:
                                pe.wait_ge(norm_dve.sem, norm_dve.at("sum"))
                                pe.wait_ge(lora_loaded, 48)
                            for m in range(MT6):
                                ins = pe.matmul(sum_of[m], lora[r, m * P:(m + 1) * P], low[r], start=True, stop=True)
                            ins.then_inc(norm_pe.up(name), 1)

                @block.scalar
                def _(act):
                    take[0](act)
                    act.wait_ge(dve_out.sem, dve_out.at("mu"))
                    for c in range(1, 13):
                        if c < 12:
                            ring_a.split_hi(act, g0 + c)
                        if c == 4:
                            mem_exp_act(act, probs)
                        elif c == 6:
                            mem_probsT_act(act, probsT)
                        elif c == 8:
                            act.wait_ge(norm_dve.sem, norm_dve.at("sum"))
                            act.activation(BON, BON, ACT.Sqrt).then_inc(norm_act.up("root"), 1)
                        if c >= 2:
                            ring_a.wait_used(act, g0 + c - 1)
                        if c == 2:
                            act.activation(mqT, ps[:, 4:6, 0:SEQ], ACT.Copy, scale=HD ** -0.5)\
                               .then_inc(mem_act.up("queries"), 1)
                        for n in range(2 if c >= 3 else 0):
                            m = z_tile[2 * (c - 3) + n]
                            act.activation(z[:, m], ps[:, (c - 3) % 4, n * SEQ:(n + 1) * SEQ],
                                           ACT.Copy, scale=one_minus_mu[:, m:m + 1]).then_inc(act_out.up(("z", m)), 1)
                        if c == 5:
                            act.wait_ge(dve_out.sem, dve_out.at(("z", 2 * MT6 - 1)))
                            for m in range(MT6):
                                ins = act.activation(BON[:, m], K[:, m], ACT.Square, scale=col("k_k", m))
                            ins.then_inc(norm_act.up("square"), 1)
                        elif c == 6:
                            for m in range(MT6):
                                ins = act.activation(KK[:, m], K[:, m], ACT.Copy, scale=col("k_k", m))
                            ins.then_inc(norm_act.up("kk"), 1)
                        elif c == 8:
                            act.wait_ge(dve_out.sem, dve_out.at(("z", 18)))
                            act.activation(low[0:HD], low[0:HD], ACT.Tanh).then_inc(norm_act.up("low"), 1)
                        elif c in (10, 12):
                            dst, name, bias = ((SIG, "decay", "w0"), (Av, "rate", "a0"))[(c - 10) // 2]
                            act.wait_ge(norm_pe.sem, norm_pe.at(name))
                            for m in range(MT6):
                                ins = act.activation(dst[:, m], sum_of[m], ACT.Sigmoid, bias=col(bias, m))
                            ins.then_inc(norm_act.up(name), 1)

                @block.vector
                def _(dve):
                    take[1](dve)
                    dve_steps.mark(dve.tensor_scalar(one_minus_ka, cols("k_a", MT6), -1.0, 1.0, ALU.mult, ALU.add))
                    dve.tensor_scalar(one_minus_mu, cols("mu", 20), -1.0, 1.0, ALU.mult, ALU.add)\
                        .then_inc(dve_out.up("mu"), 1)
                    for c in range(1, 13):
                        if c == 5:
                            mem_probs_dve(dve, probs)
                        if c < 12:
                            ring_a.split_lo(dve, g0 + c)
                        if c == 4:
                            mem_max_dve(dve)
                        elif c == 6:
                            mem_probsT_dve(dve, probsT)
                        elif c == 7:
                            dve.wait_ge(norm_pe.sem, norm_pe.at("sum"))
                            dve_steps.mark(dve.tensor_scalar(BON[:, 0:4], ps[:, 4:6, :].rearrange(
                                "p b (m t) -> p (b m) t", m=2), 1e-24, None, ALU.max))
                            dve.tensor_scalar(BON[:, 4:6], ps[:, 6:8, SEQ:2 * SEQ], 1e-24, None, ALU.max)\
                               .then_inc(norm_dve.up("sum"), 1)
                        for n in range(2 if c >= 3 else 0):
                            m = z_tile[2 * (c - 3) + n]
                            dve.wait_ge(act_out.sem, act_out.at(("z", m | 1)))
                            src = ps[:, (c - 3) % 4, n * SEQ:(n + 1) * SEQ - 1]
                            dve.scalar_tensor_tensor(z[:, m, 1:SEQ], src, col("mu", m), z[:, m, 1:SEQ],
                                                     ALU.mult, ALU.add).then_inc(dve_out.up(("z", m)), 1)
                        if c == 8:
                            dve.wait_ge(norm_act.sem, norm_act.at("root"))
                        for m in {8: [0], 9: [1], 10: [2], 11: [3], 12: [4, 5]}.get(c, []):
                            dve_steps.step(dve, dve.reciprocal(BON[:, m], BON[:, m]))
                            ins = dve.tensor_tensor(KK[:, m], KK[:, m], BON[:, m], ALU.mult)
                            if m == MT6 - 1:
                                ins.then_inc(norm_dve.up("kk"), 1)
                        if c == 12:
                            dve.wait_ge(norm_act.sem, norm_act.at("decay"))
                            dve.wait_ge(pool_steps.sem, masks_made)
                            for m in range(MT6):
                                ins = dve.tensor_tensor_scan(CUM[:, m], reset, SIG[:, m], 0.0, ALU.mult, ALU.add)
                            ins.then_inc(norm_dve.up("cum"), 1)
                            dve.wait_ge(norm_dve.sem, norm_dve.at("cum"))
                            dve.tensor_tensor(SIG, CUM, SIG, ALU.subtract).then_inc(norm_dve.up("cumx"), 1)

            bonus = ps[:, 3:6, :].rearrange("p b (m t) -> p (b m) t", m=2)
            w_end = small[:, 0:24].rearrange("p (m c) -> p m c", m=MT6)
            pe_out.events(["bonus"])
            act_out.events(["Wex", "Winv", "W"])
            dve_out.events(["factor", "k", "b", "q", "rk", "bon", "kb"])
            with nc.Block() as block:
                @block.tensor
                def _(pe):
                    pe.wait_ge(dve_out.sem, dve_out.at("rk"))
                    for m in range(MT6):
                        ins = pe.matmul(bonus[:, m], head_ones[:], BON[:, m], start=True, stop=True)
                    ins.then_inc(pe_out.up("bonus"), 1)

                @block.scalar
                def _(act):
                    act.wait_ge(norm_dve.sem, norm_dve.at("cumx"))
                    act.activation(SIG, SIG, ACT.Exp, scale=-DECAY).then_inc(act_out.up("Wex"), 1)
                    mem_hi_act(act)
                    act_steps.step(act, act.activation(lowg, lowg, ACT.Sigmoid))
                    act.wait_ge(dve_out.sem, dve_out.at("q"))
                    act.activation(KK, CUM, ACT.Exp, scale=DECAY).then_inc(act_out.up("Winv"), 1)
                    act.wait_ge(act_out.sem, act_out.at("Winv"))
                    act.activation(CUM, CUM, ACT.Exp, scale=-DECAY).then_inc(act_out.up("W"), 1)

                @block.vector
                def _(dve):
                    dve.wait_ge(norm_act.sem, norm_act.at("rate"))
                    dve.wait_ge(norm_dve.sem, norm_dve.at("kk"))
                    for m in range(MT6):
                        ins = dve.tensor_scalar(BON[:, m], Av[:, m], col("k_a", m), one_minus_ka[:, m:m + 1],
                                                ALU.mult, ALU.add)
                    ins.then_inc(dve_out.up("factor"), 1)
                    dve.wait_ge(dve_out.sem, dve_out.at("factor"))
                    dve.tensor_tensor(K, K, BON, ALU.mult).then_inc(dve_out.up("k"), 1)
                    dve.scalar_tensor_tensor(Av, KK, -1.0, Av, ALU.mult, ALU.mult).then_inc(dve_out.up("b"), 1)
                    dve.wait_ge(act_out.sem, act_out.at("Wex"))
                    dve.tensor_tensor(SIG, SIG, KK, ALU.mult).then_inc(dve_out.up("q"), 1)
                    dve.wait_ge(dve_out.sem, dve_out.at("k"))
                    for m in range(MT6):
                        ins = dve.scalar_tensor_tensor(BON[:, m], R[:, m], col("r_k", m), K[:, m], ALU.mult, ALU.mult)
                    ins.then_inc(dve_out.up("rk"), 1)
                    mem_lo_dve(dve)
                    dve.wait_ge(act_out.sem, act_out.at("Winv"))
                    dve.wait_ge(dve_out.sem, dve_out.at("b"))
                    dve_steps.step(dve, dve.tensor_tensor(Av, Av, KK, ALU.mult))
                    dve.wait_ge(pe_out.sem, pe_out.at("bonus"))
                    dve.tensor_tensor(BON, bonus, V, ALU.mult).then_inc(dve_out.up("bon"), 1)
                    dve.tensor_tensor(K, K, KK, ALU.mult).then_inc(dve_out.up("kb"), 1)
                    dve.wait_ge(act_out.sem, act_out.at("W"))
                    dve_steps.step(dve, dve.tensor_tensor(R, R, CUM, ALU.mult))
                    dve_steps.step(dve, dve.tensor_copy(w_end, CUM.rearrange("p m (c w) -> p m c w", w=CHUNK)
                                                        [:, :, :, CHUNK - 1]))
            rwkv_core(R, K, V, SIG, Av, BON, CUM, KK, lowg, g_up, w_end, level_mask, pair_mask, below, upto, used)

        def rwkv_core(R, K, V, Q, BB, BON, CUM, KK, lowg, g_up, w_end, level_mask, pair_mask, below, upto, used):
            LV = range(1, 6)
            units = [(T, hf) for T in range(NT) for hf in range(2)]
            Vt, Qt = (CUM.rearrange("p m t -> p (m t)")[:, i * C:(i + 1) * C] for i in range(2))
            Kt, Bt = (KK.rearrange("p m t -> p (m t)")[:, i * C:(i + 1) * C] for i in range(2))
            tok = (Vt, Qt, Kt, Bt)

            def piece(at, *shape):
                ap = arena[:, at:at + math.prod(shape)]
                return ap.rearrange("p (a b c) -> p a b c", a=shape[0], b=shape[1]) if len(shape) == 3 else \
                    ap.rearrange("p (a b) -> p a b", a=shape[0])

            free = 20 * SEQ
            LkV, U, S = piece(free, 2, 3, HD), piece(free + 384, 2, 3, HD), piece(free + 768, MT6, HD)
            Z, LT, M0, M1 = (piece(used + i * 768, 2, 3, P) for i in range(4))
            M = (M0, M1)
            O = piece(used + 4 * 768, MT6, 2, HD)
            assert used + 5 * 768 <= arena_words
            Dm = gate_m[:, 0:C].rearrange("p (a b c) -> p a b c", a=2, b=3)
            DT = gate_f[:, 0:C].rearrange("p (a b c) -> p a b c", a=2, b=3)
            A1 = Z[:, 0]
            Oh = O.rearrange("p m a d -> p (m a) d")
            hs = [small[:, 64 + 12 * i:76 + 12 * i] for i in range(4)]

            def bank(b, cols=3 * P):
                return ps[:, b, 0:cols].rearrange("p (m t) -> p m t", m=3)

            def bmask(m):
                return m.unsqueeze(1).to_broadcast([P, 3, P])

            def first_chunk(T, c):
                return T == 0 and c == 0

            def last_chunk(T, c):
                return T == NT - 1 and c == 1

            pe_names, act_names, dve_names, pool_names = [], [], ["zero"], []
            for T in range(NT):
                pe_names += [("tr", T, i) for i in range(4)]
                act_names += [("tok", T, i) for i in range(2)]
                dve_names += [("tok", T, i) for i in range(2, 4)]
                for hf in range(2):
                    u = (T, hf)
                    pe_names += [(n, u, p) for p in range(2) for n in ("LbT", "Lb", "LkT")]
                    pe_names += [("LkV", u, p) for p in range(2)]
                    act_names += [("LT", u, p) for p in range(2)] + [("LkV", u, p) for p in range(2)]
                    dve_names += [(n, u, p) for p in range(2) for n in ("D1", ("D", 0), "LkT")]
                    pool_names += [(n, u, p) for p in range(2) for n in ("DT1", ("DT", 0))]
                    for l in LV:
                        pe_names += [(("Z", l), u, p) for p in range(2)]
                        pe_names += [(n, u, p) for p in range(2) for n in ((("dD", l), ("dDT", l)) if l < 5 else (("dDT", l),))]
                        act_names += [(("Z", l), u, p) for p in range(2)]
                        dve_names += [(n, u, p) for p in range(2) for n in ((("D", l), ("DT", l)) if l < 5 else (("DT", l),))]
                        pool_names += [(("M", l), u, p) for p in range(2)]
                    pe_names += [(n, u, p) for p in range(2) for n in ("A1", "U0")]
                    pe_names += [(n, u, p) for p in range(2) for n in ("Lrk", "Lrb")]
                    act_names += [(n, u, p) for p in range(2) for n in ("A1", "U0")]
                    dve_names += [(n, u, p) for p in range(2) for n in ("Lrk", "Lrb")]
                    for c in range(2):
                        if not first_chunk(T, c):
                            pe_names += [(("U", c), u, p) for p in range(2)] + [(("RS", c), u, p) for p in range(2)]
                            act_names += [(("RS", c), u, p) for p in range(2)]
                            dve_names += [(("U", c), u, p) for p in range(2)]
                        if not last_chunk(T, c):
                            pe_names += [(("S", c), u)]
                            dve_names += ([] if first_chunk(T, c) else [(("S1", c), u)]) + [(("S", c), u)]
                    pe_names += [("O", u)]
                    dve_names += [("O", u)]
                pe_names += [("nt", T)]
                act_names += [("sq", T), ("std", T), ("ln", T)]
                dve_names += [("sum", T), ("mean", T), ("cen", T), ("var", T), ("inv", T), ("normal", T)]
            pe_names += ["G"]
            act_names += ["hi"]
            dve_names += ["y", "yg"]
            pe_out.events(pe_names)
            act_out.events(act_names)
            dve_out.events(dve_names)
            pool_out.events(pool_names)

            with nc.Block() as block:
                @block.tensor
                def _(pe):
                    for T in range(NT):
                        tt = slice(T * P, (T + 1) * P)
                        if T:
                            pe.wait_ge(act_out.sem, act_out.at(("ln", T - 1)))
                        for i, src in enumerate((V, Q, K, BB)):
                            two = ps[:, 2 * i:2 * i + 2, :].rearrange("p b n -> p (b n)")
                            for m in range(MT6):
                                ins = pe.transpose(two[:, m * P:(m + 1) * P], src[:, m, tt], ident[:])
                            ins.then_inc(pe_out.up(("tr", T, i)), 1)
                        pe.wait_ge(act_out.sem, act_out.at(("tok", T, 1)))
                        pe.wait_ge(dve_out.sem, dve_out.at(("tok", T, 3)))
                        for hf in range(2):
                            u = (T, hf)
                            if hf:
                                pe.wait_ge(dve_out.sem, dve_out.at(("O", (T, 0))))
                            for p in range(2):
                                r = slice(p * HD, p * HD + HD)
                                for name, b, lhs, rhs in (("LbT", 0, BB, Q), ("Lb", 2, Q, BB), ("LkT", 4, K, Q)):
                                    for mm in range(3):
                                        m = 3 * hf + mm
                                        ins = pe.matmul(bank(b + p)[:, mm], lhs[r, m, tt], rhs[r, m, tt],
                                                        start=True, stop=True)
                                    ins.then_inc(pe_out.up((name, u, p)), 1)
                            for p in range(2):
                                pe.wait_ge(dve_out.sem, dve_out.at(("LkT", u, p)))
                                for mm in range(3):
                                    h = 2 * (3 * hf + mm) + p
                                    ins = pe.matmul(bank(6 + p, 3 * HD)[:, mm], Z[:, p, mm], Vt[:, h * HD:(h + 1) * HD],
                                                    start=True, stop=True)
                                ins.then_inc(pe_out.up(("LkV", u, p)), 1)
                            for l in LV:
                                for p in range(2):
                                    pe.wait_ge(pool_out.sem, pool_out.at((("M", l), u, p)))
                                    pe.wait_ge(dve_out.sem, dve_out.at((("D", l - 1), u, p)))
                                    for mm in range(3):
                                        ins = pe.matmul(bank(p)[:, mm], M[l % 2][:, p, mm], Dm[:, p, mm],
                                                        start=True, stop=True)
                                    ins.then_inc(pe_out.up((("Z", l), u, p)), 1)
                                for p in range(2):
                                    pe.wait_ge(act_out.sem, act_out.at((("Z", l), u, p)))
                                    made = dve_out if l > 1 else pool_out
                                    pe.wait_ge(made.sem, made.at((("DT", l - 1), u, p)))
                                    if l < 5:
                                        for mm in range(3):
                                            ins = pe.matmul(bank(2 + p)[:, mm], DT[:, p, mm], Z[:, p, mm],
                                                            start=True, stop=True)
                                        ins.then_inc(pe_out.up((("dD", l), u, p)), 1)
                                    for mm in range(3):
                                        ins = pe.matmul(bank(4 + p)[:, mm], Z[:, p, mm], DT[:, p, mm],
                                                        start=True, stop=True)
                                    ins.then_inc(pe_out.up((("dDT", l), u, p)), 1)
                            for p in range(2):
                                r = slice(p * HD, p * HD + HD)
                                pe.wait_ge(dve_out.sem, dve_out.at((("DT", 5), u, p)))
                                pe.wait_ge(act_out.sem, act_out.at(("LkV", u, p)))
                                for mm in range(3):
                                    h = 2 * (3 * hf + mm) + p
                                    ins = pe.matmul(bank(p)[r, mm], Qt[:, h * HD:(h + 1) * HD], DT[:, p, mm],
                                                    start=True, stop=True)
                                ins.then_inc(pe_out.up(("A1", u, p)), 1)
                                for mm in range(3):
                                    ins = pe.matmul(ps[:, 6 + p, 192 + mm * HD:192 + (mm + 1) * HD], DT[:, p, mm],
                                                    LkV[:, p, mm], start=True, stop=True)
                                ins.then_inc(pe_out.up(("U0", u, p)), 1)
                            for p in range(2):
                                r = slice(p * HD, p * HD + HD)
                                for name, b, lhs in (("Lrk", 2, K), ("Lrb", 4, BB)):
                                    for mm in range(3):
                                        m = 3 * hf + mm
                                        ins = pe.matmul(bank(b + p)[:, mm], lhs[r, m, tt], R[r, m, tt],
                                                        start=True, stop=True)
                                    ins.then_inc(pe_out.up((name, u, p)), 1)
                            for c in range(2):
                                rc = slice(c * CHUNK, (c + 1) * CHUNK)
                                if not first_chunk(T, c):
                                    for p in range(2):
                                        r = slice(p * HD, p * HD + HD)
                                        pe.wait_ge(act_out.sem, act_out.at(("U0", u, p)))
                                        pe.wait_ge(dve_out.sem, dve_out.at((("S", 0), u) if c else (("S", 1), (T - 1, hf))))
                                        for mm in range(3):
                                            ins = pe.matmul(bank(6 + p, 3 * HD)[rc, mm], A1[r, mm, rc],
                                                            S[r, 3 * hf + mm, :], start=True, stop=True)
                                        ins.then_inc(pe_out.up((("U", c), u, p)), 1)
                                    for p in range(2):
                                        r = slice(p * HD, p * HD + HD)
                                        if c:
                                            if not first_chunk(T, 0):
                                                pe.wait_ge(act_out.sem, act_out.at((("RS", 0), u, p)))
                                        for mm in range(3):
                                            m = 3 * hf + mm
                                            ins = pe.matmul(bank(p, 3 * HD)[rc, mm],
                                                            R[r, m, T * P + c * CHUNK:T * P + (c + 1) * CHUNK],
                                                            S[r, m, :], start=True, stop=True)
                                        ins.then_inc(pe_out.up((("RS", c), u, p)), 1)
                                if not last_chunk(T, c):
                                    for p in range(2):
                                        r = slice(p * HD, p * HD + HD)
                                        if first_chunk(T, c):
                                            pe.wait_ge(act_out.sem, act_out.at(("U0", u, p)))
                                        else:
                                            pe.wait_ge(dve_out.sem, dve_out.at((("U", c), u, p)))
                                        pe.wait_ge(dve_out.sem, dve_out.at(("Lrk", u, 0)))
                                        for mm in range(3):
                                            h = 2 * (3 * hf + mm) + p
                                            hc = slice(h * HD, (h + 1) * HD)
                                            pe.matmul(bank(2, 3 * HD)[r, mm], Kt[rc, hc], Vt[rc, hc],
                                                      start=True, stop=False)
                                            ins = pe.matmul(bank(2, 3 * HD)[r, mm], Bt[rc, hc], U[rc, p, mm],
                                                            start=False, stop=True)
                                    ins.then_inc(pe_out.up((("S", c), u)), 1)
                            for p in range(2):
                                pe.wait_ge(dve_out.sem, dve_out.at(("Lrb", u, p)))
                                pe.wait_ge(dve_out.sem, dve_out.at((("U", 1), u, p)))
                                for mm in range(3):
                                    h = 2 * (3 * hf + mm) + p
                                    o = ps[:, 3, (2 * mm + p) * HD:(2 * mm + p + 1) * HD]
                                    pe.matmul(o, M0[:, p, mm], Vt[:, h * HD:(h + 1) * HD], start=True, stop=False)
                                    ins = pe.matmul(o, M1[:, p, mm], U[:, p, mm], start=False, stop=True)
                            ins.then_inc(pe_out.up(("O", u)), 1)
                        pe.wait_ge(dve_out.sem, dve_out.at(("normal", T)))
                        two = ps[:, 0:2, :].rearrange("p b n -> p (b n)")
                        for m in range(MT6):
                            ins = pe.transpose(two[:, m * P:(m + 1) * P], O[:, m], ident[:])
                        ins.then_inc(pe_out.up(("nt", T)), 1)
                    for m in range(MT6):
                        ins = pe.matmul(ps[:, 4 + m // 2, (m % 2) * SEQ:(m % 2 + 1) * SEQ], g_up[:, m * P:(m + 1) * P],
                                        lowg, start=True, stop=True)
                    ins.then_inc(pe_out.up("G"), 1)

                @block.scalar
                def _(act):
                    for c in range(2):
                        ring_a.split_hi(act, sec["w_out", 0] + c)
                    for T in range(NT):
                        for i in range(2):
                            act.wait_ge(pe_out.sem, pe_out.at(("tr", T, i)))
                            two = ps[:, 2 * i:2 * i + 2, :].rearrange("p b n -> p (b n)")
                            act.activation(tok[i], two[:, 0:C], ACT.Copy).then_inc(act_out.up(("tok", T, i)), 1)
                        for hf in range(2):
                            u = (T, hf)
                            for p in range(2):
                                act.wait_ge(pe_out.sem, pe_out.at(("LbT", u, p)))
                                if units.index(u):
                                    prev = units[units.index(u) - 1]
                                    act.wait_ge(pool_out.sem, pool_out.at((("M", 5), prev, p)))
                                act.activation(LT[:, p], bank(p), ACT.Copy).then_inc(act_out.up(("LT", u, p)), 1)
                            for p in range(2):
                                act.wait_ge(pe_out.sem, pe_out.at(("LkV", u, p)))
                                act.activation(LkV[:, p], bank(6 + p, 3 * HD), ACT.Copy)\
                                    .then_inc(act_out.up(("LkV", u, p)), 1)
                            for l in LV:
                                for p in range(2):
                                    act.wait_ge(pe_out.sem, pe_out.at((("Z", l), u, p)))
                                    act.activation(Z[:, p], bank(p), ACT.Copy).then_inc(act_out.up((("Z", l), u, p)), 1)
                            for p in range(2):
                                r = slice(p * HD, p * HD + HD)
                                act.wait_ge(pe_out.sem, pe_out.at(("A1", u, 1) if p == 0 else ("A1", u, p)))
                                act.activation(A1[r], bank(p)[r], ACT.Copy).then_inc(act_out.up(("A1", u, p)), 1)
                                act.wait_ge(pe_out.sem, pe_out.at(("U0", u, p)))
                                act.activation(U[:, p], ps[:, 6 + p, 192:384].rearrange(
                     "p (m t) -> p m t", m=3), ACT.Copy).then_inc(act_out.up(("U0", u, p)), 1)
                            for c in range(2):
                                rc = slice(c * CHUNK, (c + 1) * CHUNK)
                                if not first_chunk(T, c):
                                    for p in range(2):
                                        act.wait_ge(pe_out.sem, pe_out.at((("RS", c), u, p)))
                                        if hf == 0:
                                            if T:
                                                act.wait_ge(act_out.sem, act_out.at(("ln", T - 1)))
                                            else:
                                                act.wait_ge(dve_out.sem, dve_out.at("zero"))
                                        act.activation(O[rc, 3 * hf:3 * hf + 3, p],
                                                       bank(p, 3 * HD)[rc], ACT.Copy)\
                                                           .then_inc(act_out.up((("RS", c), u, p)), 1)
                        act.wait_ge(dve_out.sem, dve_out.at(("cen", T)))
                        act.activation(M0.rearrange("p a b c -> p (a b c)"),
                                       O.rearrange("p m a d -> p (m a d)"), ACT.Square)\
                                           .then_inc(act_out.up(("sq", T)), 1)
                        act.wait_ge(dve_out.sem, dve_out.at(("var", T)))
                        act.activation(hs[2], hs[1], ACT.Sqrt, bias=eps[:, 2:3], scale=1.0 / HD)\
                            .then_inc(act_out.up(("std", T)), 1)
                        act.wait_ge(pe_out.sem, pe_out.at(("nt", T)))
                        two = ps[:, 0:2, :].rearrange("p b n -> p (b n)")
                        for m in range(MT6):
                            ins = act.activation(V[:, m, T * P:(T + 1) * P], two[:, m * P:(m + 1) * P], ACT.Identity,
                                                 bias=col("lnx_b", m), scale=col("lnx_g", m))
                        ins.then_inc(act_out.up(("ln", T)), 1)
                    act.wait_ge(dve_out.sem, dve_out.at("yg"))
                    act.activation(actT[:, 0, 0:MT6], V, ACT.Copy).then_inc(act_out.up("hi"), 1)

                @block.gpsimd
                def _(pool):
                    for T, hf in units:
                        u = (T, hf)
                        for p in range(2):
                            pool.wait_ge(act_out.sem, act_out.at(("LT", u, p)))
                            if units.index(u):
                                pool.wait_ge(pe_out.sem, pe_out.at(("U0", units[units.index(u) - 1], p)))
                            pool.tensor_tensor(DT[:, p], LT[:, p], bmask(level_mask[0]), ALU.mult)\
                                .then_inc(pool_out.up(("DT1", u, p)), 1)
                            pool.wait_ge(pool_out.sem, pool_out.at(("DT1", u, p)))
                            pool.tensor_tensor(DT[:, p], DT[:, p], bmask(ident[:]), ALU.add)\
                                .then_inc(pool_out.up((("DT", 0), u, p)), 1)
                        for l in LV:
                            for p in range(2):
                                if l > 2:
                                    pool.wait_ge(pe_out.sem, pe_out.at((("Z", l - 2), u, p)))
                                elif units.index(u):
                                    pool.wait_ge(pe_out.sem, pe_out.at(("O", units[units.index(u) - 1])))
                                    if hf == 0:
                                        pool.wait_ge(dve_out.sem, dve_out.at(("var", T - 1)))
                                pool.tensor_tensor(M[l % 2][:, p], LT[:, p], bmask(level_mask[l]),
                                                   ALU.mult).then_inc(pool_out.up((("M", l), u, p)), 1)

                @block.vector
                def _(dve):
                    dve.memset(O[0:CHUNK], 0.0).then_inc(dve_out.up("zero"), 1)
                    for T in range(NT):
                        if T == 1:
                            for c in range(2):
                                ring_a.split_lo(dve, sec["w_out", 0] + c)
                        for i in range(2, 4):
                            dve.wait_ge(pe_out.sem, pe_out.at(("tr", T, i)))
                            two = ps[:, 2 * i:2 * i + 2, :].rearrange("p b n -> p (b n)")
                            dve.tensor_copy(tok[i], two[:, 0:C]).then_inc(dve_out.up(("tok", T, i)), 1)
                        for hf in range(2):
                            u = (T, hf)
                            for p in range(2):
                                dve.wait_ge(pe_out.sem, pe_out.at(("Lb", u, p)))
                                dve.tensor_tensor(Dm[:, p], bank(2 + p), bmask(pair_mask), ALU.mult)\
                                    .then_inc(dve_out.up(("D1", u, p)), 1)
                                dve.wait_ge(dve_out.sem, dve_out.at(("D1", u, p)))
                                dve.tensor_tensor(Dm[:, p], Dm[:, p], bmask(ident[:]), ALU.add)\
                                    .then_inc(dve_out.up((("D", 0), u, p)), 1)
                                dve.wait_ge(pe_out.sem, pe_out.at(("LkT", u, p)))
                                if units.index(u) and p == 0:
                                    prev = units[units.index(u) - 1]
                                    dve.wait_ge(pe_out.sem, pe_out.at(("O", prev)))
                                dve.tensor_tensor(Z[:, p], bank(4 + p), bmask(below), ALU.mult)\
                                    .then_inc(dve_out.up(("LkT", u, p)), 1)
                            for l in LV:
                                for p in range(2):
                                    if l < 5:
                                        dve.wait_ge(pe_out.sem, pe_out.at((("dD", l), u, p)))
                                        dve.tensor_tensor(Dm[:, p], Dm[:, p], bank(2 + p), ALU.add)\
                                            .then_inc(dve_out.up((("D", l), u, p)), 1)
                                    dve.wait_ge(pe_out.sem, pe_out.at((("dDT", l), u, p)))
                                    dve.tensor_tensor(DT[:, p], DT[:, p], bank(4 + p), ALU.add)\
                                        .then_inc(dve_out.up((("DT", l), u, p)), 1)
                            for p in range(2):
                                for name, b, dst in (("Lrk", 2, M0), ("Lrb", 4, M1)):
                                    dve.wait_ge(pe_out.sem, pe_out.at((name, u, p)))
                                    dve.tensor_tensor(dst[:, p], bank(b + p), bmask(upto), ALU.mult)\
                                        .then_inc(dve_out.up((name, u, p)), 1)
                            Sh = S[:, 3 * hf:3 * hf + 3]
                            for c in range(2):
                                rc = slice(c * CHUNK, (c + 1) * CHUNK)
                                if not first_chunk(T, c):
                                    for p in range(2):
                                        dve.wait_ge(pe_out.sem, pe_out.at((("U", c), u, p)))
                                        dve.wait_ge(act_out.sem, act_out.at(("U0", u, p)))
                                        dve.tensor_tensor(U[rc, p], U[rc, p], bank(6 + p, 3 * HD)[rc],
                                                          ALU.add).then_inc(dve_out.up((("U", c), u, p)), 1)
                                if not last_chunk(T, c):
                                    dve.wait_ge(pe_out.sem, pe_out.at((("S", c), u)))
                                    w = w_end[:, 3 * hf:3 * hf + 3, 2 * T + c:2 * T + c + 1].to_broadcast([P, 3, HD])
                                    if first_chunk(T, c):
                                        ins = dve.tensor_tensor(Sh, bank(2, 3 * HD), w, ALU.mult)
                                    else:
                                        dve.tensor_tensor(Sh, Sh, bank(2, 3 * HD), ALU.add)\
                                            .then_inc(dve_out.up((("S1", c), u)), 1)
                                        dve.wait_ge(dve_out.sem, dve_out.at((("S1", c), u)))
                                        ins = dve.tensor_tensor(Sh, Sh, w, ALU.mult)
                                    ins.then_inc(dve_out.up((("S", c), u)), 1)
                            dve.wait_ge(pe_out.sem, pe_out.at(("O", u)))
                            dve.wait_ge(act_out.sem, act_out.at((("RS", 1), u, 1)))
                            Ou = Oh[:, 6 * hf:6 * hf + 6]
                            dve.tensor_tensor(Ou, Ou, ps[:, 3, 0:6 * HD].rearrange("p (h d) -> p h d", h=6),
                                              ALU.add).then_inc(dve_out.up(("O", u)), 1)
                        wide = lambda s: s.unsqueeze(2).to_broadcast([P, NH, HD])
                        dve.wait_ge(dve_out.sem, dve_out.at(("O", (T, 1))))
                        dve.tensor_reduce(hs[0], Oh, AX_X, ALU.add).then_inc(dve_out.up(("sum", T)), 1)
                        dve.wait_ge(dve_out.sem, dve_out.at(("sum", T)))
                        dve.tensor_scalar(hs[0], hs[0], 1.0 / HD, None, ALU.mult).then_inc(dve_out.up(("mean", T)), 1)
                        dve.wait_ge(dve_out.sem, dve_out.at(("mean", T)))
                        dve.tensor_tensor(Oh, Oh, wide(hs[0]), ALU.subtract).then_inc(dve_out.up(("cen", T)), 1)
                        dve.wait_ge(act_out.sem, act_out.at(("sq", T)))
                        dve.tensor_reduce(hs[1], M0.rearrange("p a b c -> p (a b c)").rearrange(
             "p (h d) -> p h d", h=NH), AX_X, ALU.add).then_inc(dve_out.up(("var", T)), 1)
                        dve.wait_ge(act_out.sem, act_out.at(("std", T)))
                        dve.reciprocal(hs[3], hs[2]).then_inc(dve_out.up(("inv", T)), 1)
                        dve.wait_ge(dve_out.sem, dve_out.at(("inv", T)))
                        dve.tensor_tensor(Oh, Oh, wide(hs[3]), ALU.mult).then_inc(dve_out.up(("normal", T)), 1)
                    dve.wait_ge(act_out.sem, act_out.at(("ln", NT - 1)))
                    dve.tensor_tensor(V, V, BON, ALU.add).then_inc(dve_out.up("y"), 1)
                    dve.wait_ge(pe_out.sem, pe_out.at("G"))
                    dve.wait_ge(dve_out.sem, dve_out.at("y"))
                    dve.tensor_tensor(V, V, ps[:, 4:7, :].rearrange("p b (m t) -> p (b m) t", m=2),
                                      ALU.mult).then_inc(dve_out.up("yg"), 1)
                    dve.wait_ge(act_out.sem, act_out.at("hi"))
                    dve_steps.step(dve, dve.tensor_tensor(actT[:, 1, 0:MT6], V, actT[:, 0, 0:MT6].bitcast(F32),
                                                          ALU.subtract))

        def stick_stages(take):
            W = SEQ + P
            QT, KT, Vt, mqT, sg, kp, later, attT = carve((MT6, SEQ), (MT6, SEQ), (NT, C), (2, SEQ),
                                                         (2, 2, W), (2, 2, W), (2, 2, W), (2, 2, W))
            mem_at = (2 * MT6 + 2) * SEQ + NT * C
            before, not_before = gate_m[:, 0:P], gate_m[:, P:2 * P]
            ones = gate_m[:, 2 * P:2 * P + SEQ]
            g0 = sec["sb_in"]
            act_at = [act_steps.n + c for c in range(10)]
            expect_input()
            expect_memory()
            probs, probsT = (arena[:, mem_at + i * 2048:mem_at + (i + 1) * 2048].rearrange("p (a b) -> p a b", a=8)
                             for i in range(2))
            with nc.Block() as block:
                @block.sync
                def _(sp):
                    for g in range(g0 + 2, g0 + 10 + 2):
                        ring_a.load(sp, g)

                @block.gpsimd
                def _(pool):
                    pool_steps.mark(pool.memset(ones, 1.0))
                    pool_steps.mark(pool.memset(before, 1.0))
                    pool_steps.step(pool, pool.memset(not_before, 1.0))
                    pool_steps.step(pool, pool.affine_select(out=before, in_=before, compare_op=ALU.is_gt, fill=0.0,
                                                             base=0, pattern=[[-1, P]], channel_multiplier=1))
                    pool_steps.step(pool, pool.affine_select(out=not_before, in_=not_before, compare_op=ALU.is_ge,
                                                             fill=0.0, base=0, pattern=[[1, P]], channel_multiplier=-1))

                @block.tensor
                def _(pe):
                    for c in range(10):
                        g = g0 + c
                        ring_a.wait_split(pe, g)
                        i = c - 1
                        if i >= 4:
                            pe.wait_ge(act_steps.sem, act_at[c - 4])
                        for n in range(2):
                            for k in range(KD):
                                if c == 0 and n == 0:
                                    wait_input(pe, k)
                                out_ = ps[:, i % 4 if c else 4, n * SEQ:(n + 1) * SEQ]
                                if i >= 6:
                                    w = [ring_a.part(g, s, k * 256, k * 256 + 256) for s in range(2)]
                                    ins = mm3(pe, out_, [actT[:, s, k, n * P:(n + 1) * P] for s in range(2)], w,
                                              k == 0, k == KD - 1)
                                else:
                                    w = [ring_a.part(g, s, k * 256 + n * P, k * 256 + n * P + P) for s in range(2)]
                                    ins = mm3(pe, out_, w, [actT[:, s, k] for s in range(2)], k == 0, k == KD - 1)
                        ins.then_inc(ring_a.used, 1)
                        if c == 1:
                            mem_scores_pe(pe, mqT)
                        elif c == 3:
                            mem_turn_pe(pe, probs)
                        elif c == 4:
                            mem_out_pe(pe, probsT)

                @block.scalar
                def _(act):
                    take[0](act)
                    for c in range(1, 11):
                        if c < 10:
                            ring_a.split_hi(act, g0 + c)
                        if c == 3:
                            mem_exp_act(act, probs)
                        elif c == 5:
                            mem_probsT_act(act, probsT)
                        i = c - 2
                        ring_a.wait_used(act, g0 + i + 1)
                        src = ps[:, i % 4 if c > 1 else 4, :].rearrange("p (n t) -> p n t", n=2)
                        scale = HD ** -0.5 if i < 3 else 1.0
                        dst = (mqT if i < 0 else QT[:, 2 * i:2 * i + 2] if i < 3 else KT[:, 2 * i - 6:2 * i - 4] if i < 6
                               else Vt[:, :, (i - 6) * 256:(i - 5) * 256])
                        ins = act.activation(dst, src, ACT.Copy, scale=scale)
                        if i < 0:
                            ins.then_inc(mem_act.up("queries"), 1)
                        else:
                            assert act_steps.mark(ins) == act_at[i + 1]

                @block.vector
                def _(dve):
                    take[1](dve)
                    for c in range(1, 10):
                        if c == 4:
                            mem_probs_dve(dve, probs)
                        ring_a.split_lo(dve, g0 + c)
                        if c == 3:
                            mem_max_dve(dve)
                        elif c == 5:
                            mem_probsT_dve(dve, probsT)

            ahead = lambda name, m: [(name, m + 2)] if m + 2 < MT6 else []
            pe_out.events([("scores", 0), ("scores", 1)]
                          + [e for m in range(MT6) for e in [("attT", m), *ahead("scores", m), ("out", m)]])
            act_out.events([("sig", 0), ("sig", 1)]
                           + [e for m in range(MT6) for e in [("attT", m), *ahead("sig", m), ("hi", m)]])
            dve_out.events(["last"] + [e for m in range(MT6) for e in
                                       [("keep", m), ("later", m), ("att", m)] + ([("lo", m - 2)] if m >= 2 else [])]
                           + [("lo", MT6 - 2), ("lo", MT6 - 1)])
            pool_out.events([("sg", m) for m in range(MT6)])
            with nc.Block() as block:
                @block.tensor
                def _(pe):
                    def scores(m):
                        if m >= 2:
                            pe.wait_ge(act_out.sem, act_out.at(("sig", m - 2)))
                        for p in range(2):
                            r = slice(p * HD, p * HD + HD)
                            b = ps[:, 2 * (m % 2) + p, :]
                            pe.matmul(b[:, 0:SEQ], QT[r, m, P:SEQ], KT[r, m, :], start=True, stop=True)
                            ins = pe.matmul(b[:, SEQ:W], QT[r, m, 0:P], KT[r, m, 0:P], start=True, stop=True)
                        ins.then_inc(pe_out.up(("scores", m)), 1)

                    scores(0)
                    scores(1)
                    for m in range(MT6):
                        pe.wait_ge(dve_out.sem, dve_out.at(("att", m)))
                        if m >= 2:
                            pe.wait_ge(dve_out.sem, dve_out.at(("lo", m - 2)))
                        elif m == 1:
                            pe.wait_ge(mem_dve.sem, mem_dve.at("lo"))
                        for p in range(2):
                            for i in range(3):
                                ins = pe.transpose(ps[:, 4 + 2 * (m % 2) + p, i * P:(i + 1) * P],
                                                   later[:, m % 2, p, i * P:(i + 1) * P], ident[:])
                        ins.then_inc(pe_out.up(("attT", m)), 1)
                        if m + 2 < MT6:
                            scores(m + 2)
                        pe.wait_ge(act_out.sem, act_out.at(("attT", m)))
                        for p in range(2):
                            r, h = slice(p * HD, p * HD + HD), 2 * m + p
                            v = [Vt[:, t, h * HD:(h + 1) * HD] for t in range(NT)]
                            a, b = attT[:, m % 2, p], 4 + 2 * (m % 2)
                            pe.matmul(ps[r, b, W:512], v[0], a[:, SEQ:W], start=True, stop=True)
                            pe.matmul(ps[r, b + 1, W:512], v[0], a[:, 0:P], start=True, stop=False)
                            ins = pe.matmul(ps[r, b + 1, W:512], v[1], a[:, P:SEQ], start=False, stop=True)
                        ins.then_inc(pe_out.up(("out", m)), 1)

                @block.scalar
                def _(act):
                    def sigmoids(m):
                        b = 2 * (m % 2)
                        act.wait_ge(pe_out.sem, pe_out.at(("scores", m)))
                        if m >= 2:
                            act.wait_ge(dve_out.sem, dve_out.at(("att", m - 2)))
                        act.activation(kp[:, m % 2], ps[:, b:b + 2, 0:W], ACT.Sigmoid, scale=-1.0)
                        act.activation(sg[:, m % 2], ps[:, b:b + 2, 0:W], ACT.Sigmoid)\
                            .then_inc(act_out.up(("sig", m)), 1)

                    mem_hi_act(act)
                    sigmoids(0)
                    sigmoids(1)
                    for m in range(MT6):
                        act.wait_ge(pe_out.sem, pe_out.at(("attT", m)))
                        b = 4 + 2 * (m % 2)
                        act.activation(attT[:, m % 2], ps[:, b:b + 2, 0:W], ACT.Copy)\
                            .then_inc(act_out.up(("attT", m)), 1)
                        if m + 2 < MT6:
                            sigmoids(m + 2)
                        act.wait_ge(pe_out.sem, pe_out.at(("out", m)))
                        act.activation(actT[:, 0, m].rearrange("p (t n) -> p t n", t=NT),
                                       ps[:, b:b + 2, W:512], ACT.Copy).then_inc(act_out.up(("hi", m)), 1)
                        if m in (2, 3):
                            ring_a.split_hi(act, sec["w_out", 1] + m - 2)

                @block.gpsimd
                def _(pool):
                    for m in range(MT6):
                        pool.wait_ge(act_out.sem, act_out.at(("sig", m)))
                        diag = sg[:, m % 2, :, P:W]
                        for p in range(2):
                            d = diag[:, p].rearrange("p (a s) -> p a s", a=2)
                            ins = pool.tensor_tensor(d, d, before.unsqueeze(1).to_broadcast([P, 2, P]), ALU.mult)
                        ins.then_inc(pool_out.up(("sg", m)), 1)

                @block.vector
                def _(dve):
                    dve.memset(later[:, :, :, SEQ - 1:W:P], 1.0).then_inc(dve_out.up("last"), 1)
                    dve.wait_ge(dve_out.sem, dve_out.at("last"))

                    def lo(m):
                        dve.wait_ge(act_out.sem, act_out.at(("hi", m)))
                        b = 4 + 2 * (m % 2)
                        two = lambda ap: ap.rearrange("p (t n) -> p t n", t=NT)
                        dve.tensor_tensor(two(actT[:, 1, m]), ps[:, b:b + 2, W:512],
                                          two(actT[:, 0, m].bitcast(F32)), ALU.subtract)\
                                              .then_inc(dve_out.up(("lo", m)), 1)

                    mem_lo_dve(dve)
                    for m in range(MT6):
                        q = m % 2
                        if m in (4, 5):
                            ring_a.split_lo(dve, sec["w_out", 1] + m - 4)
                        dve.wait_ge(act_out.sem, act_out.at(("sig", m)))
                        for p in range(2):
                            d = kp[:, q, p, P:W].rearrange("p (a s) -> p a s", a=2)
                            ins = dve.tensor_tensor(d, d, not_before.unsqueeze(1).to_broadcast([P, 2, P]), ALU.max)
                        ins.then_inc(dve_out.up(("keep", m)), 1)
                        dve.wait_ge(dve_out.sem, dve_out.at(("keep", m)))
                        if m >= 2:
                            dve.wait_ge(pe_out.sem, pe_out.at(("attT", m - 2)))
                            dve_steps.step(dve, dve.memset(later[:, q, :, SEQ - 1:W:P], 1.0))
                        for p in range(2):
                            for a, b in ((0, SEQ), (SEQ, W)):
                                ins = dve.tensor_tensor_scan(later[:, q, p, a:b - 1][:, ::-1],
                                                             kp[:, q, p, a + 1:b][:, ::-1], ones[:, 0:b - a - 1],
                                                             1.0, ALU.mult, ALU.mult)
                        ins.then_inc(dve_out.up(("later", m)), 1)
                        dve.wait_ge(dve_out.sem, dve_out.at(("later", m)))
                        dve.wait_ge(pool_out.sem, pool_out.at(("sg", m)))
                        dve.tensor_tensor(later[:, q], later[:, q], sg[:, q], ALU.mult)\
                            .then_inc(dve_out.up(("att", m)), 1)
                        if m >= 2:
                            lo(m - 2)
                    lo(MT6 - 2)
                    lo(MT6 - 1)

        def norm_rows(i, n):
            return A["ln_g_2"][i, n], A["ln_b_2"][i, n]

        take = ffn_stage("ffn", True, None, True, sec["ffn1", 0], sec[("ffn1", 0), "B"], take_modulated())
        take = ffn_stage(("ffn1", 0), False, norm_rows(0, 0), True, sec["rwkv_in"], sec[("ffn2", 0), "B"], take)
        rwkv_stages(take)
        take = output_stage(0)
        take = ffn_stage(("ffn2", 0), False, norm_rows(0, 2), True, sec["ffn1", 1], sec[("ffn1", 1), "B"], take)
        take = ffn_stage(("ffn1", 1), False, norm_rows(1, 0), True, sec["sb_in"], sec[("ffn2", 1), "B"], take)
        stick_stages(take)
        take = output_stage(1)
        ffn_stage(("ffn2", 1), False, norm_rows(1, 2), False, len(chunks_a), len(chunks_b), take)

        with nc.Block() as block:
            @block.sync
            def _(sp):
                sp.dma_start(out[0].rearrange("(t p) d -> p t d", p=P), x_tok[:]).then_inc(rows_loaded, 16)
                sp.wait_ge(rows_loaded, rows_count[0] + 16)


INPUTS = ["x", "c", "mod_w", "mod_b", "norm_pre_mix", "norm_post_mix", "norm_pre_ffn", "norm_post_ffn", "a_pw1_w",
          "a_pw1_b", "a_dw_w", "a_dw_b", "a_ln_g", "a_ln_b", "a_pw2_w", "a_pw2_b", "f_up_w", "f_dw_w", "f_dw_b",
          "f_down_w", "mem_2", "ffn1_w_gate_2", "ffn1_w_up_2", "ffn1_w_down_2", "ffn2_w_gate_2", "ffn2_w_up_2",
          "ffn2_w_down_2", "ln_g_2", "ln_b_2", "w_out_2", "w_mem_kv_2", "rwkv_w_in_2", "rwkv_mu_2", "rwkv_w0_2",
          "rwkv_w_up_2", "rwkv_a0_2", "rwkv_a_up_2", "rwkv_g_up_2", "rwkv_k_k_2", "rwkv_k_a_2", "rwkv_r_k_2",
          "rwkv_lnx_g_2", "rwkv_lnx_b_2", "sb_w_in_2"]


def kernel(**inputs):
    import numpy as np
    import concourse.bacc as bacc
    from concourse.bass_utils import run_bass_kernel_spmd

    nc = bacc.Bacc("TRN2", target_bir_lowering=False, num_devices=1)
    arrays, aps = {}, {}
    for name in INPUTS:
        a = np.ascontiguousarray(inputs[name])
        arrays[f"in_{name}"] = a
        aps[name] = nc.dram_tensor(f"in_{name}", a.shape, mybir.dt.from_np(a.dtype), kind="ExternalInput").ap()
    out = nc.dram_tensor("out_x", (1, SEQ, D), F32, kind="ExternalOutput").ap()
    build_program(nc, aps, out)
    return run_bass_kernel_spmd(nc, [arrays], core_ids=[0]).results[0]["out_x"]
```
